# Optimizing a Trainium2 kernel written in Bass

```python
import math
import jax
import jax.numpy as jnp
from jax import lax
import numpy as np

D_MODEL = 1024
BATCH = 1
SEQ = 512
DEPTH = 2
DEC_BATCH = 8
DEC_SEQ = 4
PAST_LEN = 2048
PAGE_SIZE = 128

N_EVEN = (DEPTH + 1) // 2
N_ODD = DEPTH // 2
HEAD_DIM = 64
A_HEADS = 8
A_KV_HEADS = 2
A_GROUP = A_HEADS // A_KV_HEADS
A_Q_W = A_HEADS * HEAD_DIM
A_KV_W = A_KV_HEADS * HEAD_DIM
WINDOW = 128
N_BUCKETS = 32
MAX_DISTANCE = 128
SG_GROUPS = 4
SG_GROUP_DIM = 128
SG_WIDTH = SG_GROUPS * SG_GROUP_DIM
CHUNK = 128
IN_EVEN = A_Q_W + 2 * A_KV_W + 2 * SG_WIDTH
MIX_EVEN = A_Q_W + SG_WIDTH
C_WIDTH = 512
CONV_WIDTH = 3
MLA_HEADS = 8
NOPE_DIM = 64
ROPE_DIM = 32
V_DIM = 64
Q_LORA = 768
KV_LORA = 256
ROPE_THETA = 10000.0
MLA_BLOCK = 128
IN_ODD = 3 * C_WIDTH + Q_LORA + KV_LORA + ROPE_DIM
MIX_ODD = C_WIDTH + MLA_HEADS * V_DIM
D_FF = 2816
EPS = 1e-6
NEG = -1e30

kernel_name = 'hybrid_swa_sgu_conv_mla_decoder_step'

def rms_norm(x, g):
    xf = x.astype(jnp.float32)
    y = xf * lax.rsqrt(jnp.mean(xf * xf, axis=-1, keepdims=True) + EPS)
    return (y * g.astype(jnp.float32)).astype(x.dtype)

def layer_norm(x, g, b):
    xf = x.astype(jnp.float32)
    xc = xf - jnp.mean(xf, axis=-1, keepdims=True)
    y = xc * lax.rsqrt(jnp.mean(xc * xc, axis=-1, keepdims=True) + EPS)
    return (y * g.astype(jnp.float32) + b.astype(jnp.float32)).astype(x.dtype)

def swiglu(x, w_gate, w_up, w_down):
    return (jax.nn.silu(x @ w_gate) * (x @ w_up)) @ w_down

def t5_bucket(dist):
    n = jnp.maximum(dist, 0)
    max_exact = N_BUCKETS // 2
    nf = jnp.maximum(n, 1).astype(jnp.float32)
    large = max_exact + (jnp.log(nf / max_exact) / math.log(MAX_DISTANCE / max_exact)
                         * (N_BUCKETS - max_exact)).astype(jnp.int32)
    return jnp.where(n < max_exact, n, jnp.minimum(large, N_BUCKETS - 1))

def t5_bias(dist, rel_bias):
    b = rel_bias[t5_bucket(dist)].astype(jnp.float32)
    b = jnp.moveaxis(b, -1, 0)
    return b.reshape((A_KV_HEADS, A_GROUP) + dist.shape)

def sink_softmax(s, sinks):
    sk = sinks.astype(jnp.float32).reshape(A_KV_HEADS, A_GROUP, 1, 1)
    m = jnp.maximum(jnp.max(s, axis=-1, keepdims=True), sk)
    p = jnp.exp(s - m)
    return p / (jnp.sum(p, axis=-1, keepdims=True) + jnp.exp(sk - m))

def swa_prompt(q, k, v, sinks, rel_bias):
    b, s = q.shape[:2]
    nb = s // WINDOW
    qb = q.reshape(b, nb, WINDOW, A_KV_HEADS, A_GROUP, HEAD_DIM)
    kb = k.reshape(b, nb, WINDOW, A_KV_HEADS, HEAD_DIM)
    vb = v.reshape(b, nb, WINDOW, A_KV_HEADS, HEAD_DIM)
    pad = ((0, 0), (1, 0), (0, 0), (0, 0), (0, 0))
    kk = jnp.concatenate([jnp.pad(kb, pad)[:, :-1], kb], axis=2)
    vv = jnp.concatenate([jnp.pad(vb, pad)[:, :-1], vb], axis=2)
    qpos = WINDOW + jnp.arange(WINDOW)
    kpos = jnp.arange(2 * WINDOW)
    dist = qpos[:, None] - kpos[None, :]
    band = (dist >= 0) & (dist <= WINDOW)
    has_prev = (jnp.arange(nb)[:, None, None] > 0) | (kpos[None, None, :] >= WINDOW)
    mask = band[None] & has_prev
    sc = jnp.einsum('bnqhgd,bnjhd->bnhgqj', qb, kk,
                    preferred_element_type=jnp.float32) * (HEAD_DIM ** -0.5)
    sc = sc + t5_bias(dist, rel_bias)
    sc = jnp.where(mask[None, :, None, None], sc, NEG)
    p = sink_softmax(sc, sinks)
    o = jnp.einsum('bnhgqj,bnjhd->bnqhgd', p.astype(v.dtype), vv)
    wb = min(WINDOW, s)
    return o.reshape(b, s, A_Q_W), k[:, s - wb:], v[:, s - wb:]

def swa_sample(q, k, v, buf_k, buf_v, sinks, rel_bias):
    bd, t = q.shape[:2]
    wb = buf_k.shape[1]
    kk = jnp.concatenate([buf_k, k], axis=1)
    vv = jnp.concatenate([buf_v, v], axis=1)
    qpos = jnp.arange(t)
    kpos = jnp.arange(wb + t) - wb
    dist = qpos[:, None] - kpos[None, :]
    mask = (dist >= 0) & (dist <= WINDOW)
    qg = q.reshape(bd, t, A_KV_HEADS, A_GROUP, HEAD_DIM)
    sc = jnp.einsum('bqhgd,bjhd->bhgqj', qg, kk,
                    preferred_element_type=jnp.float32) * (HEAD_DIM ** -0.5)
    sc = jnp.where(mask, sc + t5_bias(dist, rel_bias), NEG)
    p = sink_softmax(sc, sinks)
    o = jnp.einsum('bhgqj,bjhd->bqhgd', p.astype(v.dtype), vv)
    return o.reshape(bd, t, A_Q_W), kk[:, t:], vv[:, t:]

def spatial_gate(u, v, ln_g, ln_b, w_s, b_s):
    b, s, _ = u.shape
    u = jax.nn.gelu(u, approximate=False)
    v = layer_norm(jax.nn.gelu(v, approximate=False), ln_g, ln_b)
    L = min(s, CHUNK)
    nc = s // L
    w = jnp.tril(w_s[:, :L, :L])
    vc = v.reshape(b, nc, L, SG_GROUPS, SG_GROUP_DIM)
    y = jnp.einsum('gij,bcjgd->bcigd', w, vc) + b_s[:, :L].T[None, None, :, :, None]
    return u * y.reshape(b, s, SG_WIDTH), v

def even_mixer(h, buf_k, buf_v, w_in, w_out, sinks, rel_bias, ln_g, ln_b, w_s, b_s):
    b, s, _ = h.shape
    p = h @ w_in
    q, k, v, u, g = jnp.split(p, [A_Q_W, A_Q_W + A_KV_W, A_Q_W + 2 * A_KV_W,
                                  A_Q_W + 2 * A_KV_W + SG_WIDTH], axis=-1)
    q = q.reshape(b, s, A_HEADS, HEAD_DIM)
    k = k.reshape(b, s, A_KV_HEADS, HEAD_DIM)
    v = v.reshape(b, s, A_KV_HEADS, HEAD_DIM)
    if buf_k is None:
        a, nk, nv = swa_prompt(q, k, v, sinks, rel_bias)
    else:
        a, nk, nv = swa_sample(q, k, v, buf_k, buf_v, sinks, rel_bias)
    sg, v_rows = spatial_gate(u, g, ln_g, ln_b, w_s, b_s)
    return jnp.concatenate([a, sg], axis=-1) @ w_out, nk, nv, v_rows

def short_conv(x_in, gate_b, gate_c, conv_w, prev):
    s = x_in.shape[1]
    z = jnp.concatenate([prev, gate_c * x_in], axis=1)
    y = conv_w[0] * z[:, 0:s]
    for j in range(1, CONV_WIDTH):
        y = y + conv_w[j] * z[:, j:j + s]
    return gate_b * y, z[:, s:]

def rope(x, pos):
    half = ROPE_DIM // 2
    inv = jnp.exp(-math.log(ROPE_THETA) * jnp.arange(half, dtype=jnp.float32) / half)
    ang = pos.astype(jnp.float32)[:, None] * inv[None, :]
    cos = jnp.cos(ang)[None, :, None, :]
    sin = jnp.sin(ang)[None, :, None, :]
    xf = x.astype(jnp.float32)
    x1, x2 = xf[..., :half], xf[..., half:]
    return jnp.concatenate([x1 * cos - x2 * sin, x2 * cos + x1 * sin], axis=-1).astype(x.dtype)

def mla_project(c_q, c_kv, k_pe, pos, q_norm, w_uq, kv_norm, w_uk):
    b, s, _ = c_q.shape
    q = (rms_norm(c_q, q_norm) @ w_uq).reshape(b, s, MLA_HEADS, NOPE_DIM + ROPE_DIM)
    q_nope = q[..., :NOPE_DIM]
    q_pe = rope(q[..., NOPE_DIM:], pos)
    k_pe = rope(k_pe[:, :, None, :], pos)[:, :, 0]
    ckv = rms_norm(c_kv, kv_norm)
    q_abs = jnp.einsum('bshn,chn->bshc', q_nope, w_uk)
    return q_abs, q_pe, ckv, k_pe

def mla_scores(q_abs, q_pe, kc, kp):
    scale = (NOPE_DIM + ROPE_DIM) ** -0.5
    return (jnp.einsum('bqhc,bjc->bhqj', q_abs, kc, preferred_element_type=jnp.float32)
            + jnp.einsum('bqhr,bjr->bhqj', q_pe, kp, preferred_element_type=jnp.float32)) * scale

def mla_prompt_attend(q_abs, q_pe, ckv, k_pe):
    b, s, h, c = q_abs.shape
    blk = min(MLA_BLOCK, s)
    nb = s // blk
    qa = jnp.moveaxis(q_abs.reshape(b, nb, blk, h, c), 1, 0)
    qp = jnp.moveaxis(q_pe.reshape(b, nb, blk, h, ROPE_DIM), 1, 0)
    kpos = jnp.arange(s)

    def one_block(args):
        i, qa_i, qp_i = args
        sc = mla_scores(qa_i, qp_i, ckv, k_pe)
        qpos = i * blk + jnp.arange(blk)
        sc = jnp.where(kpos[None, :] <= qpos[:, None], sc, NEG)
        p = jax.nn.softmax(sc, axis=-1)
        return jnp.einsum('bhqj,bjc->bqhc', p.astype(ckv.dtype), ckv)

    o = lax.map(one_block, (jnp.arange(nb), qa, qp))
    return jnp.moveaxis(o, 0, 1).reshape(b, s, h, c)

def mla_sample_attend(q_abs, q_pe, ckv, k_pe, pool_ckv, pool_kpe, page_table):
    bd, t, h, c = q_abs.shape
    past = page_table.shape[1] * PAGE_SIZE
    past_ckv = pool_ckv[page_table].reshape(bd, past, c)
    past_kpe = pool_kpe[page_table].reshape(bd, past, ROPE_DIM)
    kc = jnp.concatenate([past_ckv, ckv], axis=1)
    kp = jnp.concatenate([past_kpe, k_pe], axis=1)
    sc = mla_scores(q_abs, q_pe, kc, kp)
    kpos = jnp.arange(past + t)
    qpos = past + jnp.arange(t)
    sc = jnp.where(kpos[None, :] <= qpos[:, None], sc, NEG)
    p = jax.nn.softmax(sc, axis=-1)
    return jnp.einsum('bhqj,bjc->bqhc', p.astype(kc.dtype), kc)

def odd_mixer(h, pos, conv_prev, pool_ckv, pool_kpe, page_table,
              w_in, w_out, conv_w, q_norm, w_uq, kv_norm, w_uk, w_uv):
    b, s, _ = h.shape
    p = h @ w_in
    gate_b, gate_c, x_in, c_q, c_kv, k_pe = jnp.split(
        p, [C_WIDTH, 2 * C_WIDTH, 3 * C_WIDTH, 3 * C_WIDTH + Q_LORA,
            3 * C_WIDTH + Q_LORA + KV_LORA], axis=-1)
    c_out, conv_state = short_conv(x_in, gate_b, gate_c, conv_w, conv_prev)
    q_abs, q_pe, ckv, kpe = mla_project(c_q, c_kv, k_pe, pos, q_norm, w_uq, kv_norm, w_uk)
    if pool_ckv is None:
        o_lat = mla_prompt_attend(q_abs, q_pe, ckv, kpe)
    else:
        o_lat = mla_sample_attend(q_abs, q_pe, ckv, kpe, pool_ckv, pool_kpe, page_table)
    o = jnp.einsum('bshc,chv->bshv', o_lat, w_uv).reshape(b, s, MLA_HEADS * V_DIM)
    return jnp.concatenate([c_out, o], axis=-1) @ w_out, conv_state, ckv, kpe

def setup_inputs(seed: int = 0) -> dict:
    key = jax.random.key(seed)
    keys = jax.random.split(key, 40)
    counter = [0]

    def nxt():
        k = keys[counter[0]]
        counter[0] += 1
        return k

    def nrm(shape, scale):
        return jax.random.normal(nxt(), shape, jnp.float32) * scale

    def gain(shape):
        return 1.0 + nrm(shape, 0.01)

    n_pages = PAST_LEN // PAGE_SIZE
    n_used = DEC_BATCH * n_pages
    n_pool = n_used + n_used // 4
    wb = min(WINDOW, PAST_LEN)
    d = D_MODEL
    inp = {}
    inp['x_prompt'] = nrm((BATCH, SEQ, d), 1.0)
    inp['x_sample'] = nrm((DEC_BATCH, DEC_SEQ, d), 1.0)
    inp['cache_swa_k'] = nrm((N_EVEN, DEC_BATCH, wb, A_KV_HEADS, HEAD_DIM), 1.0)
    inp['cache_swa_v'] = nrm((N_EVEN, DEC_BATCH, wb, A_KV_HEADS, HEAD_DIM), 1.0)
    inp['state_conv'] = nrm((N_ODD, DEC_BATCH, CONV_WIDTH - 1, C_WIDTH), 1.0)
    inp['cache_mla_ckv'] = nrm((N_ODD, n_pool, PAGE_SIZE, KV_LORA), 1.0)
    inp['cache_mla_kpe'] = nrm((N_ODD, n_pool, PAGE_SIZE, ROPE_DIM), 1.0)
    inp['page_table'] = jax.random.permutation(nxt(), n_pool)[:n_used].reshape(
        DEC_BATCH, n_pages).astype(jnp.int32)
    inp['rel_bias'] = nrm((N_BUCKETS, A_HEADS), 0.2)
    inp['ffn1_norm'] = gain((DEPTH, d))
    inp['ffn1_w_gate'] = nrm((DEPTH, d, D_FF), d ** -0.5)
    inp['ffn1_w_up'] = nrm((DEPTH, d, D_FF), d ** -0.5)
    inp['ffn1_w_down'] = nrm((DEPTH, D_FF, d), D_FF ** -0.5)
    inp['mix_norm'] = gain((DEPTH, d))
    inp['ffn2_norm'] = gain((DEPTH, d))
    inp['ffn2_w_gate'] = nrm((DEPTH, d, D_FF), d ** -0.5)
    inp['ffn2_w_up'] = nrm((DEPTH, d, D_FF), d ** -0.5)
    inp['ffn2_w_down'] = nrm((DEPTH, D_FF, d), D_FF ** -0.5)
    inp['even_w_in'] = nrm((N_EVEN, d, IN_EVEN), d ** -0.5)
    inp['even_w_out'] = nrm((N_EVEN, MIX_EVEN, d), MIX_EVEN ** -0.5)
    inp['attn_sinks'] = nrm((N_EVEN, A_HEADS), 1.0)
    inp['sgu_ln_g'] = gain((N_EVEN, SG_WIDTH))
    inp['sgu_ln_b'] = nrm((N_EVEN, SG_WIDTH), 0.01)
    inp['sgu_w'] = nrm((N_EVEN, SG_GROUPS, CHUNK, CHUNK), CHUNK ** -0.5)
    inp['sgu_b'] = nrm((N_EVEN, SG_GROUPS, CHUNK), 0.01)
    inp['odd_w_in'] = nrm((N_ODD, d, IN_ODD), d ** -0.5)
    inp['odd_w_out'] = nrm((N_ODD, MIX_ODD, d), MIX_ODD ** -0.5)
    inp['conv_w'] = nrm((N_ODD, CONV_WIDTH, C_WIDTH), CONV_WIDTH ** -0.5)
    inp['mla_q_norm'] = gain((N_ODD, Q_LORA))
    inp['mla_w_uq'] = nrm((N_ODD, Q_LORA, MLA_HEADS * (NOPE_DIM + ROPE_DIM)), Q_LORA ** -0.5)
    inp['mla_kv_norm'] = gain((N_ODD, KV_LORA))
    inp['mla_w_uk'] = nrm((N_ODD, KV_LORA, MLA_HEADS, NOPE_DIM), KV_LORA ** -0.5)
    inp['mla_w_uv'] = nrm((N_ODD, KV_LORA, MLA_HEADS, V_DIM), KV_LORA ** -0.5)
    inp['final_norm'] = gain((d,))
    return inp

def reference(x_prompt, x_sample, cache_swa_k, cache_swa_v, state_conv, cache_mla_ckv,
              cache_mla_kpe, page_table, rel_bias, ffn1_norm, ffn1_w_gate, ffn1_w_up,
              ffn1_w_down, mix_norm, ffn2_norm, ffn2_w_gate, ffn2_w_up, ffn2_w_down,
              even_w_in, even_w_out, attn_sinks, sgu_ln_g, sgu_ln_b, sgu_w, sgu_b,
              odd_w_in, odd_w_out, conv_w, mla_q_norm, mla_w_uq, mla_kv_norm, mla_w_uk,
              mla_w_uv, final_norm):
    bp, sp, _ = x_prompt.shape
    ts = x_sample.shape[1]
    past = page_table.shape[1] * PAGE_SIZE
    pos_p = jnp.arange(sp)
    pos_s = past + jnp.arange(ts)
    xp, xs = x_prompt, x_sample
    swa_kp, swa_vp, swa_ks, swa_vs, sgu_vs = [], [], [], [], []
    conv_p, conv_s, ckv_p, kpe_p, ckv_s, kpe_s = [], [], [], [], [], []
    for l in range(DEPTH):
        f1 = (ffn1_w_gate[l], ffn1_w_up[l], ffn1_w_down[l])
        xp = xp + 0.5 * swiglu(rms_norm(xp, ffn1_norm[l]), *f1)
        xs = xs + 0.5 * swiglu(rms_norm(xs, ffn1_norm[l]), *f1)
        hp = rms_norm(xp, mix_norm[l])
        hs = rms_norm(xs, mix_norm[l])
        if l % 2 == 0:
            e = l // 2
            ew = (even_w_in[e], even_w_out[e], attn_sinks[e], rel_bias,
                  sgu_ln_g[e], sgu_ln_b[e], sgu_w[e], sgu_b[e])
            mp, kp_new, vp_new, _ = even_mixer(hp, None, None, *ew)
            ms, ks_new, vs_new, v_rows = even_mixer(hs, cache_swa_k[e], cache_swa_v[e], *ew)
            swa_kp.append(kp_new)
            swa_vp.append(vp_new)
            swa_ks.append(ks_new)
            swa_vs.append(vs_new)
            sgu_vs.append(v_rows)
        else:
            j = l // 2
            ow = (odd_w_in[j], odd_w_out[j], conv_w[j], mla_q_norm[j], mla_w_uq[j],
                  mla_kv_norm[j], mla_w_uk[j], mla_w_uv[j])
            zero_prev = jnp.zeros((bp, CONV_WIDTH - 1, C_WIDTH), hp.dtype)
            mp, cp_new, ckvp_new, kpep_new = odd_mixer(hp, pos_p, zero_prev, None, None, None, *ow)
            ms, cs_new, ckvs_new, kpes_new = odd_mixer(hs, pos_s, state_conv[j], cache_mla_ckv[j],
                                                       cache_mla_kpe[j], page_table, *ow)
            conv_p.append(cp_new)
            conv_s.append(cs_new)
            ckv_p.append(ckvp_new)
            kpe_p.append(kpep_new)
            ckv_s.append(ckvs_new)
            kpe_s.append(kpes_new)
        xp = xp + mp
        xs = xs + ms
        f2 = (ffn2_w_gate[l], ffn2_w_up[l], ffn2_w_down[l])
        xp = xp + 0.5 * swiglu(rms_norm(xp, ffn2_norm[l]), *f2)
        xs = xs + 0.5 * swiglu(rms_norm(xs, ffn2_norm[l]), *f2)
    y_prompt = rms_norm(xp, final_norm)
    y_sample = rms_norm(xs, final_norm)
    swa_k_prompt = jnp.stack(swa_kp)
    swa_v_prompt = jnp.stack(swa_vp)
    swa_k_sample = jnp.stack(swa_ks)
    swa_v_sample = jnp.stack(swa_vs)
    sgu_v_sample = jnp.stack(sgu_vs)
    conv_prompt = jnp.stack(conv_p)
    conv_sample = jnp.stack(conv_s)
    mla_ckv_prompt = jnp.stack(ckv_p)
    mla_kpe_prompt = jnp.stack(kpe_p)
    mla_ckv_sample = jnp.stack(ckv_s)
    mla_kpe_sample = jnp.stack(kpe_s)
    return (y_prompt, y_sample, swa_k_prompt, swa_v_prompt, swa_k_sample, swa_v_sample,
            sgu_v_sample, conv_prompt, conv_sample, mla_ckv_prompt, mla_kpe_prompt,
            mla_ckv_sample, mla_kpe_sample)


_drawn_inputs = setup_inputs


def setup_inputs(seed=0):
    import zlib

    import numpy as np

    out = dict(_drawn_inputs(seed))
    spreads = {}
    factors = {'cache_mla_ckv': 2.792,
     'cache_mla_kpe': 5.048,
     'ffn1_norm': 6.732,
     'mix_norm': 3.337,
     'ffn2_norm': 8.0,
     'attn_sinks': 26.239,
     'sgu_ln_g': 34.795,
     'sgu_ln_b': 32.036,
     'sgu_b': 25.702,
     'mla_q_norm': 64.0,
     'mla_kv_norm': 29.209,
     'final_norm': 32.162,
     'rel_bias': 4.161}
    for name, (base, spread) in spreads.items():
        noise = np.random.default_rng([zlib.crc32(name.encode()), seed]).standard_normal(out[name].shape)
        drawn = base * np.exp(spread * noise) if base else spread * noise
        out[name] = jnp.asarray(drawn.astype(out[name].dtype))
    for name, factor in factors.items():
        out[name] = (out[name] * factor).astype(out[name].dtype)
    return out
```

```python
from contextlib import ExitStack

import numpy as np

import concourse.bass as bass
from concourse import mybir

F32 = mybir.dt.float32
F32R = mybir.dt.float32r
I32 = mybir.dt.int32
ACT = mybir.ActivationFunctionType
ALU = mybir.AluOpType
AX = mybir.AxisListType.X

P = 128
D = 1024
SEQ = 512
DB, DS = 8, 4
NS = DB * DS
T = SEQ + NS
TH = T // 2
DT = D // P
D_FF = 2816
CHUNKS = 2
FT = D_FF // P // CHUNKS
EPS = 1e-6
NEG = -1e30

HD = 64
HEADS = 8
GROUP = 4
WIN = 128
BUCKETS = 32
BLOCKS = SEQ // WIN
SGW = 512
SGT = SGW // P

CT = 4
Q_LORA = 768
QT = Q_LORA // P
KV_LORA = 256
KT = KV_LORA // P
NOPE, ROPE, VD = 64, 32, 64
QK = NOPE + ROPE
PAGES = 16
PAGE = 128
N_POOL = 160
PAIR = 2
KEY_SLOTS = 4
VAL_SLOTS = 8
MLA_SCALE = float(QK) ** -0.5
SWA_SCALE = float(HD) ** -0.5

EVEN_IN = 14
ODD_IN = 3 * CT + QT + KT + 1

FFN_K = ([DT] * (2 * FT) + [FT] * DT) * CHUNKS
EVEN_K = [DT] * EVEN_IN + [DT] * DT
ODD_K = [DT] * ODD_IN + [QT] * HEADS + [DT] * DT
PANEL_K = FFN_K + EVEN_K + FFN_K + FFN_K + ODD_K + FFN_K
N_PANELS = len(PANEL_K)
START = dict(zip(("f0", "even", "f1", "f2", "odd", "f3"),
                 np.cumsum([0] + [len(k) for k in (FFN_K, EVEN_K, FFN_K, FFN_K, ODD_K)]).tolist()))
CONSTS = 4 * 16
N_NORMS = 7


def stat(norm):
    return norm + 1 if norm < 5 else norm + 3


def sumsq_steps(norm):
    return DT * (norm + 1) if norm < 5 else DT * (norm + 1) + QT + KT


def decoder_step(nc, d):
    ctx = ExitStack()
    with ctx:
        base = (nc.sbuf_base + 255) // 256 * 256
        top = [base]

        def at(name, shape, dt, offset):
            return nc.alloc_sbuf_tensor_at(name, shape, dt, offset=offset)

        def size(shape):
            return 4 * int(np.prod(shape[1:]))

        def place(name, shape, dt=F32):
            t = at(name, shape, dt, top[0])
            top[0] += (size(shape) + 31) // 32 * 32
            return t

        def v_ln_at(t):
            return t.manual_sbuf_range[0]

        x = place("x", [P, DT, T])
        region_h = top[0]
        hx_hi = place("hx_hi", [P, DT, T], F32R)
        hx_lo = place("hx_lo", [P, DT, T], F32R)
        end_h = top[0]
        region_hid = top[0]
        hid_hi = place("hid_hi", [P, FT, T], F32R)
        hid_lo = place("hid_lo", [P, FT, T], F32R)
        end_hid = top[0]
        raw = [place(f"raw{s}", [P, FT * P]) for s in range(2)]
        w_hi = [place(f"w_hi{s}", [P, FT * P], F32R) for s in range(2)]
        w_lo = [place(f"w_lo{s}", [P, FT * P], F32R) for s in range(2)]
        gate = place("gate", [P, T])
        silu = place("silu", [P, T])
        up = place("up", [P, T])
        prod = place("prod", [P, T])
        rinv = place("rinv", [P, T])
        rms = place("rms", [P, T])
        square = place("square", [P, T])
        sumsq = place("sumsq", [P, T])
        ident = place("ident", [P, P])
        ones = place("ones", [P, P])
        gains = place("gains", [P, N_NORMS, DT])
        eps = place("eps", [P, 1])
        region_e = top[0]
        end_e = nc.sbuf_usable_end

        def region(start, end):
            cur = [start]

            def put(name, shape, dt=F32):
                t = at(name, shape, dt, cur[0])
                cur[0] += (size(shape) + 31) // 32 * 32
                assert cur[0] <= end, (name, cur[0], end)
                return t
            return put

        put = region(region_hid, end_hid)
        mix_hi = put("mix_hi", [P, DT, T], F32R)
        mix_lo = put("mix_lo", [P, DT, T], F32R)
        spare = region_hid + 2 * size([P, DT, T])

        put = region(spare, end_hid)
        k_cache = put("k_cache", [P, DB, WIN])
        v_cache = put("v_cache", [P, DB, P])
        put = region(region_e, end_e)
        pre = put("pre", [P, EVEN_IN, T])
        bias = put("bias", [P, HEADS, 2 * WIN])
        bias_s = put("bias_s", [P, WIN + DS])
        sgu_w = put("sgu_w", [P, SGT, P])
        sgu_ws = put("sgu_ws", [NS, SGT, NS])
        sgu_b = put("sgu_b", [1, SGT, P])
        sgu_bs = put("sgu_bs", [1, SGT, NS])
        ln_g = put("ln_g", [P, SGW])
        ln_b = put("ln_b", [P, SGW])
        sink = put("sink", [P, HEADS])
        sink_s = put("sink_s", [P, 1])
        smax = put("smax", [P, HEADS])
        nmax = put("nmax", [P, HEADS])
        dsink = put("dsink", [P, HEADS])
        esink = put("esink", [P, HEADS])
        rsum = put("rsum", [P, HEADS])
        rden = put("rden", [P, HEADS])
        ln_st = put("ln_st", [P, 6])
        ln_mv = put("ln_mv", [P, 5, 2])
        ln_sd = put("ln_sd", [P, 5])
        ln_r = put("ln_r", [P, 5])
        v_ln = put("v_ln", [P, 5, SGW])
        put = region(v_ln_at(v_ln), end_e)
        rel = put("rel", [BUCKETS + 1, HEADS])
        onehot = put("onehot", [BUCKETS + 1, 3 * WIN])
        by_dist = put("by_dist", [HEADS, 3 * WIN])
        put = region(region_h, end_h)
        prob = [put(f"prob{s}", [P, HEADS, 2 * WIN]) for s in range(2)]
        prob_t = put("prob_t", [P, 2, HEADS, WIN])
        v_tok = put("v_tok", [P, BLOCKS, P])
        v_new = put("v_new", [DS, DB, P])
        prob_s = put("prob_s", [P, 2, WIN + DS])
        prob_st = put("prob_st", [P, 2, P])
        prob_st2 = put("prob_st2", [DS, 2, P])
        put = region(region_hid, end_hid)
        q_bd = at("q_bd", [P, DB, NS], F32, spare + 2 * size([P, DB, WIN]))

        put = region(spare, end_hid)
        w_uk_t = put("w_uk_t", [NOPE, HEADS, KV_LORA])
        cos = put("cos", [P, T])
        sin = put("sin", [P, T])
        put = region(region_e, end_e)
        cq_hi = put("cq_hi", [P, QT, T], F32R)
        cq_lo = put("cq_lo", [P, QT, T], F32R)
        end_cq = region_e + 2 * size([P, QT, T])
        ckv = put("ckv", [P, KT, T])
        kpe = put("kpe", [P, T])
        conv_z = put("conv_z", [P, CT, SEQ + 2])
        conv_zs = put("conv_zs", [P, CT, DB, DS + 2])
        w_uk = put("w_uk", [P, KT, HEADS * NOPE])
        w_uv = put("w_uv", [P, KT, HEADS * VD])
        perm = put("perm", [P, ROPE])
        conv_w = put("conv_w", [P, 3, CT])
        q_gain = put("q_gain", [P, QT])
        kv_gain = put("kv_gain", [P, KT])
        causal = put("causal", [P, P])
        causal_s = put("causal_s", [P, DS])
        qa = put("qa", [P, 3, DB, NS])
        qa_new = put("qa_new", [P, KT, DB, NS])
        o_lat = put("o_lat", [P, KT, HEADS, NS])
        s_new = put("s_new", [P, DS])
        mx = put("mx", [P, 4])
        nmx = put("nmx", [P, 4])
        sm = put("sm", [P, 4])
        rs = put("rs", [P, 4])
        table = put("table", [1, DB * PAGES], I32)
        put = region(region_h, end_h)
        qf = put("qf", [P, HEADS, T])
        kf = put("kf", [P, HEADS, SEQ])
        put = region(region_e, end_cq)
        v_mla = put("v_mla", [P, BLOCKS, HEADS * VD])
        p_mla = put("p_mla", [P, 10, P])
        p_mla_t = put("p_mla_t", [P, 10, P])
        put = region(region_e, end_cq)
        p_s = put("p_s", [P, PAGES * PAGE + DS])
        p_st = put("p_st", [P, PAGES, P])
        p_st2 = put("p_st2", [DS, P])
        ckv_new = put("ckv_new", [DS, DB, KV_LORA])
        put = region(region_h, end_h)
        key_page = [put(f"key_page{s}", [QK, PAIR, 3, PAGE]) for s in range(KEY_SLOTS)]
        val_page = [put(f"val_page{s}", [P, PAIR, KV_LORA]) for s in range(VAL_SLOTS)]
        y = at("y", [P, DT, T], F32, region_e)

        ps = ctx.enter_context(nc.psum_tensor("ps", [P, 8, 512], F32))
        ps_flat = ps[:].rearrange("p b c -> p (b c)")
        acc = [ps[:, 2 * s:2 * s + 2, :] for s in range(2)]

        def sem(name):
            return ctx.enter_context(nc.semaphore(name))

        raw_landed = [sem(f"raw_landed{s}") for s in range(2)]
        w_hi_done = sem("w_hi_done")
        w_lo_done = sem("w_lo_done")
        panel_done = sem("panel_done")
        acc_read = sem("acc_read")
        consts_landed = sem("consts_landed")
        x_landed = sem("x_landed")
        rel_landed = sem("rel_landed")
        dist_stored = sem("dist_stored")
        even_landed = sem("even_landed")
        cache_landed = sem("cache_landed")
        odd_landed = sem("odd_landed")
        spare_landed = sem("spare_landed")
        table_landed = sem("table_landed")
        key_landed = [sem(f"key_landed{s}") for s in range(KEY_SLOTS)]
        val_landed = [sem(f"val_landed{s}") for s in range(VAL_SLOTS)]
        copied = sem("copied")
        stored = sem("stored")
        stored_even = sem("stored_even")
        stored_odd = sem("stored_odd")
        hx_hi_done = sem("hx_hi_done")
        hx_done = sem("hx_done")
        square_done = sem("square_done")
        sumsq_step = sem("sumsq_step")
        stat_ready = sem("stat_ready")
        rms_done = sem("rms_done")
        rinv_ready = sem("rinv_ready")
        silu_done = sem("silu_done")
        prod_ready = sem("prod_ready")
        hid_hi_done = sem("hid_hi_done")
        hid_done = sem("hid_done")
        mix_ready = sem("mix_ready")
        mix_hi_done = sem("mix_hi_done")
        mix_done = sem("mix_done")
        step = sem("step")
        dist_ready = sem("dist_ready")
        dist_copied = sem("dist_copied")
        sgu_masked = sem("sgu_masked")
        gelu_done = sem("gelu_done")
        g_turned = sem("g_turned")
        v_ln_read = sem("v_ln_read")
        ln_var = sem("ln_var")
        ln_sd_done = sem("ln_sd_done")
        v_ln_done = sem("v_ln_done")
        gate_sum = sem("gate_sum")
        v_turned = sem("v_turned")
        v_tok_done = sem("v_tok_done")
        swa_scored = sem("swa_scored")
        swa_biased = sem("swa_biased")
        swa_max = sem("swa_max")
        swa_exp = sem("swa_exp")
        swa_prob = sem("swa_prob")
        swa_turned = sem("swa_turned")
        swa_copied = sem("swa_copied")
        swa_out = sem("swa_out")
        q_bd_ready = sem("q_bd_ready")
        cq_hi_done = sem("cq_hi_done")
        cq_done = sem("cq_done")
        ckv_done = sem("ckv_done")
        rotated = sem("rotated")
        q_done = sem("q_done")
        kpe_done = sem("kpe_done")
        kf_ready = sem("kf_ready")
        kf_done = sem("kf_done")
        vm_ready = sem("vm_ready")
        vm_done = sem("vm_done")
        mla_scored = sem("mla_scored")
        mla_max = sem("mla_max")
        mla_exp = sem("mla_exp")
        mla_prob = sem("mla_prob")
        mla_turned = sem("mla_turned")
        mla_copied = sem("mla_copied")
        mla_out = sem("mla_out")
        qa_ready = sem("qa_ready")
        qa_done = sem("qa_done")
        new_turned = sem("new_turned")
        new_copied = sem("new_copied")
        keys_read = sem("keys_read")
        s_new_ready = sem("s_new_ready")
        s_new_read = sem("s_new_read")
        s_max = sem("s_max")
        s_exp = sem("s_exp")
        s_prob = sem("s_prob")
        s_turned = sem("s_turned")
        s_copied = sem("s_copied")
        vals_read = sem("vals_read")
        s_out = sem("s_out")
        o_lat_done = sem("o_lat_done")
        y_done = sem("y_done")

        def halves(t2d):
            return t2d.rearrange("p (a b) -> p a b", a=2)

        def acc_of(slot, rows=P):
            return acc[slot][0:rows, :, 0:TH]

        def tile_of(t3d, i):
            return t3d[:, bass.ds(i, 1), :].rearrange("p a t -> p (a t)")

        def swa_halves(n):
            return (1,) if n == 0 else (0, 1)

        def swa_units(n):
            return sum(2 * len(swa_halves(b)) for b in range(n))

        FFNS = ((START["f0"], 0, 0), (START["f1"], 1, 2), (START["f2"], 2, 3), (START["f3"], 3, 5))
        S_EVEN, S_ODD = START["even"], START["odd"]
        EVEN_OUT, ODD_UQ = S_EVEN + EVEN_IN, S_ODD + ODD_IN
        ODD_OUT = ODD_UQ + HEADS
        LAST_G, LAST_U = S_EVEN + SGT, S_EVEN + 2 * SGT
        CQ0, CKV0, KPE = S_ODD + 3 * CT, S_ODD + 3 * CT + QT, S_ODD + 3 * CT + QT + KT
        EVEN_PIECES = BLOCKS + SGT + 1
        ODD_PIECES = CT + HEADS + 1
        SGU_PIECE, SWA_PIECE, SWA_S_PIECE = 0, SGT, SGT + BLOCKS
        CONV_PIECE, MLA_PIECE, MLA_S_PIECE = EVEN_PIECES, EVEN_PIECES + CT, EVEN_PIECES + CT + HEADS

        TURN_ORDER = [(j, i) for j in range(BLOCKS) for i in range(j, BLOCKS)]
        EVEN_LOADS = 16 * (1 + 4 + 7 + 4)
        ODD_LOADS = 16 * (8 + CT)

        def panel_cols(n):
            return PANEL_K[n] * (QK if ODD_UQ <= n < ODD_OUT else P)

        block = ctx.enter_context(nc.Block())

        @block.sync
        def _(sp):
            def load_panel(n, slot, cols, src, first=False):
                if not first:
                    sp.wait_ge(w_lo_done, n - 1)
                sp.dma_start(raw[slot][:, 0:cols], src).then_inc(raw_landed[slot], 16)

            def load_ffn(start, gu, down, layer, first=False):
                for c in range(CHUNKS):
                    n0 = start + c * (2 * FT + DT)
                    i0 = 0
                    if first and c == 0:
                        for s in range(2):
                            load_panel(n0 + s, s, DT * P, gu[layer, 0, s], first=True)
                        i0 = 1
                    with sp.Fori(i0, FT) as i:
                        for s in range(2):
                            load_panel(n0 + 2 * i + s, (n0 + s) % 2, DT * P, gu[layer, c * FT + i, s])
                    with sp.Fori(0, DT // 2) as i:
                        for s in range(2):
                            load_panel(n0 + 2 * FT + 2 * i + s, (n0 + s) % 2, FT * P, down[layer, c, 2 * i + s])

            def load_matrix(start, w, first=0, end=None):
                for t in range(first, w.shape[0] if end is None else end):
                    load_panel(start + t, (start + t) % 2, panel_cols(start + t), w[t])

            sp.dma_start(x[:], d["xT"]).then_inc(x_landed, 16)
            load_ffn(START["f0"], d["gu1"], d["down1"], 0, first=True)
            load_matrix(S_EVEN, d["even_in"])
            sp.dma_start(d["o_kc"], d["k_nat"][:, DS:WIN]).then_inc(copied, 16)
            sp.dma_start(d["o_vc"], d["v_nat"][:, DS:WIN]).then_inc(copied, 16)
            load_matrix(EVEN_OUT, d["even_out"])
            load_ffn(START["f1"], d["gu2"], d["down2"], 0)
            load_ffn(START["f2"], d["gu1"], d["down1"], 1)
            load_matrix(S_ODD, d["odd_in"])
            load_matrix(ODD_UQ, d["w_uq"])
            load_matrix(ODD_OUT, d["odd_out"], 0, 2)

            def page(b, g):
                return sp.value_load(table[0:1, b * PAGES + g:b * PAGES + g + 1], min_val=0, max_val=N_POOL - 1)

            def load_keys(u):
                if u == 0:
                    sp.wait_ge(table_landed, 16)
                    sp.wait_ge(qa_ready, 1)
                    sp.wait_ge(qa_done, 1)
                if u >= KEY_SLOTS:
                    sp.wait_ge(keys_read, u - KEY_SLOTS + 1)
                for j in range(PAIR):
                    g = PAIR * u + j
                    sp.dma_start(key_page[u % KEY_SLOTS][:, j], d["key_pool"][bass.ds(page(g // PAGES, g % PAGES), 1)].rearrange("a p j k -> (a p) j k"))\
                      .then_inc(key_landed[u % KEY_SLOTS], 16)

            def load_vals(u):
                if u >= VAL_SLOTS:
                    sp.wait_ge(vals_read, u - VAL_SLOTS + 1)
                for j in range(PAIR):
                    g = PAIR * u + j
                    sp.dma_start(val_page[u % VAL_SLOTS][:, j], d["val_pool"][bass.ds(page(g // PAGES, g % PAGES), 1)].rearrange("a p c -> (a p) c"))\
                      .then_inc(val_landed[u % VAL_SLOTS], 16)

            units = DB * PAGES // PAIR
            for u in range(units // 2 + KEY_SLOTS):
                load_keys(u)
            for u in range(VAL_SLOTS):
                load_vals(u)
            for u in range(units // 2 + KEY_SLOTS, units):
                load_keys(u)
            for u in range(VAL_SLOTS, units):
                load_vals(u)
            load_matrix(ODD_OUT, d["odd_out"], 2)
            load_ffn(START["f3"], d["gu2"], d["down2"], 1)
            for t in range(DT):
                sp.wait_ge(y_done, t + 1)
                sp.dma_start(d["o_y"][:, t, :], y[:, t, :]).then_inc(stored, 16)
            sp.wait_ge(stored, 16 * DT)
            sp.wait_ge(copied, 32)
            sp.wait_ge(stored_even, 16 * 5)
            sp.wait_ge(stored_odd, 16 * 4)

        @block.tensor
        def _(pe):
            def panel(n, slot, rhs_hi, rhs_lo, k, wait_input=None, m=P):
                pe.wait_ge(w_lo_done, n + 1)
                if not (isinstance(n, int) and n < 2):
                    pe.wait_ge(acc_read, n - 1)
                for t in range(k):
                    if wait_input is not None:
                        wait_input(t)
                    hi, lo = w_hi[slot][:, t * m:(t + 1) * m], w_lo[slot][:, t * m:(t + 1) * m]
                    for w, r, one in ((hi, rhs_hi, 0), (hi, rhs_lo, 1), (lo, rhs_hi, 2)):
                        for a in range(2):
                            last = pe.matmul(acc[slot][0:m, a, 0:TH], w, r[:, t, a * TH:(a + 1) * TH],
                                             start=(t == 0 and one == 0), stop=(t == k - 1 and one == 2))
                last.then_inc(panel_done, 1)

            def stats(steps):
                pe.wait_ge(sumsq_step, steps)
                for a in range(2):
                    last = pe.matmul(ps[:, 4 + a, 0:TH], ones[:], sumsq[:, a * TH:(a + 1) * TH], start=True, stop=True)
                last.then_inc(stat_ready, 1)

            def ffn(start, f, norm):
                for c in range(CHUNKS):
                    n0 = start + c * (2 * FT + DT)
                    done = (f * CHUNKS + c) * FT
                    i0 = 0
                    if c == 0:
                        def split_input(t):
                            pe.wait_ge(hx_done, DT * norm + t + 1)
                        panel(n0, n0 % 2, hx_hi, hx_lo, DT, split_input)
                        stats(sumsq_steps(norm))
                        panel(n0 + 1, (n0 + 1) % 2, hx_hi, hx_lo, DT)
                        i0 = 1
                    with pe.Fori(i0, FT) as i:
                        for s in range(2):
                            panel(n0 + 2 * i + s, (n0 + s) % 2, hx_hi, hx_lo, DT)
                    n1 = n0 + 2 * FT

                    def hidden(t):
                        pe.wait_ge(hid_done, done + t + 1)
                    panel(n1, n1 % 2, hid_hi, hid_lo, FT, hidden)
                    panel(n1 + 1, (n1 + 1) % 2, hid_hi, hid_lo, FT)
                    with pe.Fori(1, DT // 2) as i:
                        for s in range(2):
                            panel(n1 + 2 * i + s, (n1 + s) % 2, hid_hi, hid_lo, FT)

            def mixer_out(start, pieces):
                pe.wait_ge(mix_done, pieces)
                for t in range(DT):
                    panel(start + t, (start + t) % 2, mix_hi, mix_lo, DT)

            def by_distance():
                pe.wait_ge(rel_landed, 32)
                pe.matmul(ps[0:HEADS, 7, 0:3 * WIN], rel[:], onehot[:], start=True, stop=True).then_inc(dist_ready, 1)

            def turn_g(tt):
                rows = P if tt < BLOCKS else NS
                if tt == 0:
                    pe.wait_ge(gelu_done, SGT)
                    pe.wait_ge(rms_done, stat(1))
                if tt >= 4:
                    pe.wait_ge(v_ln_read, tt - 3)
                for g in range(SGT):
                    last = pe.transpose(ps[0:rows, 4 + tt % 4, g * P:(g + 1) * P], pre[:, g, tt * P:tt * P + rows], ident[:])
                last.then_inc(g_turned, 1)

            def gate_matmul(g):
                b0 = 4 + 2 * (g % 2)
                if g == 0:
                    pe.wait_ge(v_ln_done, 5)
                    pe.wait_ge(sgu_masked, 2)
                if g >= 2:
                    pe.wait_ge(mix_ready, SGU_PIECE + g - 1)
                for c in range(BLOCKS):
                    out = ps[:, b0, c * P:(c + 1) * P]
                    pe.matmul(out, ones[0:1, :], sgu_b[:, g, :], start=True, stop=False)
                    pe.matmul(out, v_ln[:, c, g * P:(g + 1) * P], sgu_w[:, g, :], start=False, stop=True)
                out = ps[:, b0 + 1, 0:NS]
                pe.matmul(out, ones[0:1, :], sgu_bs[:, g, :], start=True, stop=False)
                pe.matmul(out, v_ln[0:NS, 4, g * P:(g + 1) * P], sgu_ws[:, g, :], start=False, stop=True)\
                  .then_inc(gate_sum, 1)

            def turn_v():
                pe.wait_ge(acc_read, EVEN_OUT)
                pe.wait_ge(mix_ready, SGU_PIECE + SGT)
                for n in range(BLOCKS):
                    pe.transpose(ps[:, 4, n * P:(n + 1) * P], pre[:, 13, n * P:(n + 1) * P], ident[:])
                for b in range(DB):
                    last = pe.transpose(ps[0:DS, 5 + b // 4, (b % 4) * P:(b % 4 + 1) * P],
                                        pre[:, 13, SEQ + b * DS:SEQ + (b + 1) * DS], ident[:])
                last.then_inc(v_turned, 1)

            def swa_score(n):
                if n == 0:
                    pe.wait_ge(acc_read, EVEN_OUT)
                if n:
                    pe.wait_ge(swa_biased, n)
                k0 = swa_halves(n)[0]
                for h in range(HEADS):
                    r = HD * (h // GROUP)
                    last = pe.matmul(ps_flat[:, h * 2 * WIN + k0 * WIN:(h + 1) * 2 * WIN],
                                     pre[r:r + HD, 8 + h % GROUP, n * WIN:(n + 1) * WIN],
                                     pre[r:r + HD, 12, (n - 1 + k0) * WIN:(n + 1) * WIN], start=True, stop=True)
                last.then_inc(swa_scored, 1)

            def swa_values(n):
                pe.wait_ge(swa_prob, n + 1)
                if n == 0:
                    pe.wait_ge(v_tok_done, 2)
                u = swa_units(n)
                for kv in range(2):
                    for j in swa_halves(n):
                        if u >= 3:
                            pe.wait_ge(swa_copied, u - 2)
                        for hh in range(GROUP):
                            last = pe.transpose(ps[:, 4 + u % 3, hh * WIN:(hh + 1) * WIN],
                                                prob[n % 2][:, kv * GROUP + hh, j * WIN:(j + 1) * WIN], ident[:])
                        last.then_inc(swa_turned, 1)
                        u += 1
                if n:
                    pe.wait_ge(mix_done, SWA_PIECE + n)
                u = swa_units(n)
                for kv in range(2):
                    for j in swa_halves(n):
                        u += 1
                        pe.wait_ge(swa_copied, u)
                        last = pe.matmul(ps[kv * HD:(kv + 1) * HD, 7, :], v_tok[:, n - 1 + j, kv * HD:(kv + 1) * HD],
                                         prob_t[:, j, kv * GROUP:(kv + 1) * GROUP, :], start=(j == swa_halves(n)[0]), stop=(j == 1))
                last.then_inc(swa_out, 1)

            def swa_sample_score():
                pe.wait_ge(swa_biased, BLOCKS)
                pe.wait_ge(q_bd_ready, 1)
                pe.wait_ge(cache_landed, 32)
                for b in range(DB):
                    r = NS * (b % 4)
                    pe.matmul(ps[r:r + NS, b // 4, 0:WIN], q_bd[:, b, :], k_cache[:, b, :], start=True, stop=True)
                    last = pe.matmul(ps[r:r + NS, b // 4, WIN:WIN + DS], q_bd[:, b, :],
                                     pre[:, 12, SEQ + b * DS:SEQ + (b + 1) * DS], start=True, stop=True)
                last.then_inc(swa_scored, 1)

            def swa_sample_values():
                pe.wait_ge(swa_prob, BLOCKS + 1)
                pe.wait_ge(swa_copied, swa_units(BLOCKS))
                for g in range(2):
                    pe.transpose(ps[:, 4, g * P:(g + 1) * P], prob_s[:, g, 0:WIN], ident[:])
                    last = pe.transpose(ps[0:DS, 5, g * P:(g + 1) * P], prob_s[:, g, WIN:WIN + DS], ident[:])
                last.then_inc(swa_turned, 1)
                pe.wait_ge(swa_copied, swa_units(BLOCKS) + 2)
                pe.wait_ge(mix_done, SWA_PIECE + BLOCKS)
                for b in range(DB):
                    r = NS * (b % 4)
                    pe.matmul(ps[:, 7, b * NS:(b + 1) * NS], v_cache[:, b, :], prob_st[:, b // 4, r:r + NS],
                              start=True, stop=False)
                    last = pe.matmul(ps[:, 7, b * NS:(b + 1) * NS], v_new[:, b, :], prob_st2[:, b // 4, r:r + NS],
                                     start=False, stop=True)
                last.then_inc(swa_out, 1)

            def even():
                def split_input(t):
                    pe.wait_ge(hx_done, DT + t + 1)
                for t in range(EVEN_IN):
                    n = S_EVEN + t
                    panel(n, n % 2, hx_hi, hx_lo, DT, split_input if t == 0 else None)
                    if t == 0:
                        stats(sumsq_steps(1))
                        pe.wait_ge(even_landed, EVEN_LOADS)
                    if SGT + 1 <= t <= SGT + 5:
                        turn_g(t - SGT - 1)
                swa_score(0)
                for g in range(SGT):
                    gate_matmul(g)
                turn_v()
                for n in range(BLOCKS):
                    if n + 1 < BLOCKS:
                        swa_score(n + 1)
                    else:
                        swa_sample_score()
                    swa_values(n)
                swa_sample_values()
                mixer_out(EVEN_OUT, EVEN_PIECES)

            def rotate(src, h):
                for a in range(2):
                    last = pe.matmul(ps[NOPE:QK, 6 + a, 0:TH], perm[NOPE:QK, :], src[NOPE:QK, a * TH:(a + 1) * TH],
                                     start=True, stop=True)
                last.then_inc(rotated, 1)

            def nope_keys(h):
                if h >= 2:
                    pe.wait_ge(kf_done, h)
                for c in range(KT):
                    last = pe.matmul(ps[0:NOPE, 4 + h % 2, :], w_uk[:, c, h * NOPE:(h + 1) * NOPE], ckv[:, c, 0:SEQ],
                                     start=(c == 0), stop=(c == KT - 1))
                last.then_inc(kf_ready, 1)

            def mla_values_of(j):
                if j == 0:
                    pe.wait_ge(q_done, HEADS)
                if j >= 2:
                    pe.wait_ge(vm_done, j - 1)
                for c in range(KT):
                    last = pe.matmul(ps[:, 6 + j % 2, :], ckv[:, c, j * P:(j + 1) * P], w_uv[:, c, :],
                                     start=(c == 0), stop=(c == KT - 1))
                last.then_inc(vm_ready, 1)

            def mla_score(h):
                if h == 0:
                    pe.wait_ge(kf_done, HEADS + 1)
                    pe.wait_ge(q_done, HEADS)
                else:
                    pe.wait_ge(mla_exp, h)
                for i in range(BLOCKS):
                    last = pe.matmul(ps[:, i, 0:(i + 1) * P], qf[0:QK, h, i * P:(i + 1) * P], kf[0:QK, h, 0:(i + 1) * P],
                                     start=True, stop=True)
                last.then_inc(mla_scored, 1)

            def mla_values(h):
                pe.wait_ge(mla_prob, h + 1)
                if h:
                    pe.wait_ge(mla_copied, h)
                else:
                    pe.wait_ge(vm_done, BLOCKS)
                for s, (j, i) in enumerate(TURN_ORDER):
                    last = pe.transpose(ps[:, 4 + s // 4, (s % 4) * P:(s % 4 + 1) * P], p_mla[:, i * (i + 1) // 2 + j, :], ident[:])
                last.then_inc(mla_turned, 1)
                pe.wait_ge(mla_copied, h + 1)
                if h >= 2:
                    pe.wait_ge(mix_done, MLA_PIECE + h - 1)
                r = VD * (h % 2)
                for j in range(BLOCKS):
                    s = TURN_ORDER.index((j, j))
                    last = pe.matmul(ps[r:r + VD, 7, j * P:SEQ], v_mla[:, j, h * VD:(h + 1) * VD], p_mla_t[:, s:s + BLOCKS - j, :],
                                     start=(j == 0), stop=(j == BLOCKS - 1))
                last.then_inc(mla_out, 1)

            def absorb():
                pe.wait_ge(mla_copied, HEADS)
                for h in range(HEADS):
                    q_h = qf[0:NOPE, h, SEQ:T]
                    for j in range(2):
                        pe.matmul(ps[0:QK, 4, (j * HEADS + h) * NS:(j * HEADS + h + 1) * NS], w_uk_t[:, h, j * QK:(j + 1) * QK], q_h,
                                  start=True, stop=True)
                    pe.matmul(ps[0:NOPE, 5, h * NS:(h + 1) * NS], w_uk_t[:, h, 2 * QK:KV_LORA], q_h, start=True, stop=True)
                    for c in range(KT):
                        last = pe.matmul(ps[:, 6, (c * HEADS + h) * NS:(c * HEADS + h + 1) * NS], w_uk_t[:, h, c * P:(c + 1) * P], q_h,
                                         start=True, stop=True)
                last.then_inc(qa_ready, 1)

            def turn_new():
                pe.wait_ge(qa_done, 1)
                pe.wait_ge(mix_done, MLA_PIECE + HEADS)
                for b in range(DB):
                    for c in range(KT):
                        s = b * KT + c
                        last = pe.transpose(ps[0:DS, 4 + s // 4, (s % 4) * P:(s % 4 + 1) * P],
                                            ckv[:, c, SEQ + b * DS:SEQ + (b + 1) * DS], ident[:])
                last.then_inc(new_turned, 1)

            def sample_score(g):
                if g == 0:
                    pe.wait_ge(new_copied, 1)
                    pe.wait_ge(mla_exp, HEADS)
                else:
                    pe.wait_ge(s_exp, g)
                for b4 in range(4):
                    b, r = 4 * g + b4, NS * b4
                    for c in range(KT):
                        pe.matmul(ps[r:r + NS, 4, 0:DS], qa_new[:, c, b, :], ckv[:, c, SEQ + b * DS:SEQ + (b + 1) * DS],
                                  start=(c == 0), stop=False)
                    last = pe.matmul(ps[r:r + NS, 4, 0:DS], qa[NOPE:QK, 2, b, :], kpe[NOPE:QK, SEQ + b * DS:SEQ + (b + 1) * DS],
                                     start=False, stop=True)
                last.then_inc(s_new_ready, 1)
                for b4 in range(4):
                    b, r = 4 * g + b4, NS * b4
                    for c in range(PAGES // PAIR):
                        u = b * (PAGES // PAIR) + c
                        pe.wait_ge(key_landed[u % KEY_SLOTS], 32 * (u // KEY_SLOTS + 1))
                        col = c * PAIR * PAGE
                        for j in range(3):
                            last = pe.matmul(ps_flat[r:r + NS, col:col + PAIR * PAGE], qa[0:QK, j, b, :],
                                             key_page[u % KEY_SLOTS][:, :, j, :], start=(j == 0), stop=(j == 2))
                        last.then_inc(keys_read, 1)

            def sample_values(g):
                pe.wait_ge(s_prob, g + 1)
                if g == 0:
                    pe.wait_ge(s_new_read, 2)
                for q in range(5):
                    u = 5 * g + q
                    if u >= 2:
                        pe.wait_ge(s_copied, u - 1)
                    if q < 4:
                        for j in range(4):
                            last = pe.transpose(ps[:, 4 + u % 2, j * P:(j + 1) * P], p_s[:, (4 * q + j) * PAGE:(4 * q + j + 1) * PAGE], ident[:])
                    else:
                        last = pe.transpose(ps[0:DS, 4 + u % 2, 0:P], p_s[:, PAGES * PAGE:PAGES * PAGE + DS], ident[:])
                    last.then_inc(s_turned, 1)
                pe.wait_ge(s_copied, 5 * g + 5)
                if g:
                    pe.wait_ge(o_lat_done, g)
                for b4 in range(4):
                    b, r = 4 * g + b4, NS * b4
                    for c in range(PAGES // PAIR):
                        u = b * (PAGES // PAIR) + c
                        pe.wait_ge(val_landed[u % VAL_SLOTS], 32 * (u // VAL_SLOTS + 1))
                        for j in range(PAIR):
                            for cc in range(KT):
                                last = pe.matmul(ps[:, 6 + cc, r:r + NS], val_page[u % VAL_SLOTS][:, j, cc * P:(cc + 1) * P],
                                                 p_st[:, c * PAIR + j, r:r + NS], start=(c == 0 and j == 0), stop=False)
                        last.then_inc(vals_read, 1)
                    for cc in range(KT):
                        last = pe.matmul(ps[:, 6 + cc, r:r + NS], ckv_new[:, b, cc * P:(cc + 1) * P], p_st2[:, r:r + NS],
                                         start=False, stop=True)
                last.then_inc(s_out, 1)

            def sample_out():
                pe.wait_ge(o_lat_done, 2)
                pe.wait_ge(s_copied, 10)
                for h in range(HEADS):
                    r = VD * (h % 2)
                    for c in range(KT):
                        last = pe.matmul(ps[r:r + VD, 4, (h // 2) * NS:(h // 2 + 1) * NS], w_uv[:, c, h * VD:(h + 1) * VD], o_lat[:, c, h, :],
                                         start=(c == 0), stop=(c == KT - 1))
                last.then_inc(s_out, 1)

            def odd():
                def split_input(t):
                    pe.wait_ge(hx_done, 4 * DT + t + 1)
                for t in range(ODD_IN):
                    n = S_ODD + t
                    panel(n, n % 2, hx_hi, hx_lo, DT, split_input if t == 0 else None)
                    if t == 0:
                        stats(sumsq_steps(4))
                    if n == CKV0 + 1:
                        pe.wait_ge(rms_done, stat(4))
                        stats(DT * 5 + QT)
                for h in range(HEADS):
                    n = ODD_UQ + h

                    def split_cq(t):
                        pe.wait_ge(cq_done, t + 1)
                    panel(n, n % 2, cq_hi, cq_lo, QT, split_cq if h == 0 else None, m=QK)
                    if h == 0:
                        pe.wait_ge(rms_done, stat(4) + 1)
                        stats(DT * 5 + QT + KT)
                        pe.wait_ge(spare_landed, 48)
                        pe.wait_ge(acc_read, KPE + 1)
                        rotate(kpe, 0)
                    else:
                        pe.wait_ge(acc_read, n)
                        if h == 1:
                            pe.wait_ge(kpe_done, 1)
                        else:
                            pe.wait_ge(q_done, h - 1)
                        rotate(qf[:, h - 1, :], h)
                pe.wait_ge(acc_read, ODD_OUT)
                pe.wait_ge(q_done, HEADS - 1)
                rotate(qf[:, HEADS - 1, :], HEADS)
                pe.wait_ge(ckv_done, KT)
                for h in range(HEADS):
                    nope_keys(h)
                for j in range(BLOCKS):
                    mla_values_of(j)
                mla_score(0)
                for h in range(HEADS):
                    if h + 1 < HEADS:
                        mla_score(h + 1)
                    mla_values(h)
                absorb()
                turn_new()
                sample_score(0)
                sample_score(1)
                sample_values(0)
                sample_values(1)
                sample_out()
                mixer_out(ODD_OUT, EVEN_PIECES + ODD_PIECES)

            by_distance()
            pe.wait_ge(consts_landed, CONSTS)
            ffn(*FFNS[0])
            even()
            ffn(*FFNS[1])
            ffn(*FFNS[2])
            odd()
            ffn(*FFNS[3])
            stats(sumsq_steps(6))

        @block.scalar
        def _(act):
            def split_hi(n, slot, cols):
                act.wait_ge(raw_landed[slot], 8 * (n - slot) + 16)
                if not (isinstance(n, int) and n < 2):
                    act.wait_ge(panel_done, n - 1)
                act.activation(w_hi[slot][:, 0:cols], raw[slot][:, 0:cols], ACT.Copy).then_inc(w_hi_done, 1)

            def split_next(n):
                if n + 2 < N_PANELS:
                    split_hi(n + 2, n % 2, panel_cols(n + 2))

            def root(k, terms):
                act.wait_ge(stat_ready, k)
                if k > 1:
                    act.wait_ge(rinv_ready, k - 1)
                act.activation(halves(rms[:]), ps[:, 4:6, 0:TH], ACT.Sqrt, scale=1.0 / terms, bias=eps[:, 0:1])\
                   .then_inc(rms_done, 1)

            def input_hi(norm, m):
                act.activation(tile_of(hx_hi, m), tile_of(x, m), ACT.Copy, scale=gains[:, norm, bass.ds(m, 1)])\
                   .then_inc(hx_hi_done, 1)

            def ffn(start, f, norm):
                for c in range(CHUNKS):
                    n0 = start + c * (2 * FT + DT)
                    h0 = (f * CHUNKS + c) * FT

                    def tile(i, cols):
                        split_hi(n0 + 2 * i + 2, n0 % 2, cols)
                        act.wait_ge(acc_read, n0 + 2 * i + 1)
                        act.activation(silu[:], gate[:], ACT.Silu).then_inc(silu_done, 1)
                        split_hi(n0 + 2 * i + 3, (n0 + 1) % 2, cols)
                        act.wait_ge(prod_ready, h0 + i + 1)
                        act.activation(tile_of(hid_hi, i), prod[:], ACT.Copy).then_inc(hid_hi_done, 1)
                    if c == 0:
                        root(stat(norm), D)
                    with act.Fori(0, FT - 1) as i:
                        tile(i, DT * P)
                    tile(FT - 1, FT * P)
                    n1 = n0 + 2 * FT

                    def final_input(m):
                        if c == CHUNKS - 1 and norm + 1 < N_NORMS - 1:
                            act.wait_ge(acc_read, n1 + m + 1)
                            input_hi(norm + 1, m)
                    with act.Fori(0, DT // 2 - 1) as i:
                        for s in range(2):
                            split_hi(n1 + 2 * i + s + 2, (n1 + s) % 2, FT * P)
                            final_input(2 * i + s)
                    for m in (DT - 2, DT - 1):
                        split_next(n1 + m)
                        final_input(m)

            def mixer_out(start, norm):
                for m in range(DT):
                    split_next(start + m)
                    act.wait_ge(acc_read, start + m + 1)
                    input_hi(norm + 1, m)

            def mix_upper(out, src, ready, count):
                act.wait_ge(ready, count)
                act.activation(out, src, ACT.Copy).then_inc(mix_hi_done, 1)

            def swa_exps(n):
                act.wait_ge(swa_max, n + 1)
                lo = swa_halves(n)[0] * WIN
                for h in range(HEADS):
                    act.activation(prob[n % 2][:, h, lo:2 * WIN], prob[n % 2][:, h, lo:2 * WIN], ACT.Exp,
                                   bias=nmax[:, h:h + 1], accum_out=rsum[:, h:h + 1])
                act.activation(esink[:], dsink[:], ACT.Exp).then_inc(swa_exp, 1)

            def swa_copies(n):
                u = swa_units(n)
                if n:
                    act.wait_ge(swa_out, n)
                for kv in range(2):
                    for j in swa_halves(n):
                        act.wait_ge(swa_turned, u + 1)
                        act.activation(prob_t[:, j, kv * GROUP:(kv + 1) * GROUP, :].rearrange("p h q -> p (h q)"), ps[:, 4 + u % 3, :], ACT.Copy)\
                           .then_inc(swa_copied, 1)
                        u += 1

            def swa_upper(n):
                mix_upper(mix_hi[:, 0:GROUP, n * WIN:(n + 1) * WIN],
                          ps[:, 7, :].rearrange("p (h q) -> p h q", h=GROUP), swa_out, n + 1)

            def even():
                for t in range(EVEN_IN):
                    n = S_EVEN + t
                    if t == 0:
                        root(stat(1), D)
                    split_next(n)
                    if t < 2 * SGT:
                        act.wait_ge(acc_read, n + 1)
                        act.activation(pre[:, t, :], pre[:, t, :], ACT.Gelu).then_inc(gelu_done, 1)
                    if t == SGT + 6:
                        act.wait_ge(ln_var, 1)
                        act.activation(ln_sd[:, 0:4], ln_mv[:, 0:4, 1], ACT.Sqrt, bias=eps[:, 0:1])
                        act.activation(ln_sd[0:NS, 4:5], ln_mv[0:NS, 4, 1:2], ACT.Sqrt, bias=eps[0:NS, 0:1]).then_inc(ln_sd_done, 1)
                swa_exps(0)
                for g in range(SGT):
                    mix_upper(mix_hi[:, GROUP + g, :], (up if g % 2 else prod)[:], mix_ready, g + 1)
                act.wait_ge(v_turned, 1)
                act.activation(v_tok[:].rearrange("p n c -> p (n c)"), ps[:, 4, :], ACT.Copy).then_inc(v_tok_done, 1)
                act.activation(v_new[:].rearrange("p (a b) c -> p a (b c)", a=2), ps[0:DS, 5:7, :], ACT.Copy).then_inc(v_tok_done, 1)
                for n in range(BLOCKS):
                    swa_copies(n)
                    if n + 1 < BLOCKS:
                        swa_exps(n + 1)
                    else:
                        act.wait_ge(swa_max, BLOCKS + 1)
                        for g in range(2):
                            act.activation(prob_s[:, g, :], prob_s[:, g, :], ACT.Exp, bias=nmax[:, g:g + 1], accum_out=rsum[:, g:g + 1])
                        act.activation(esink[:, 0:2], dsink[:, 0:2], ACT.Exp).then_inc(swa_exp, 1)
                    swa_upper(n)
                act.wait_ge(swa_turned, swa_units(BLOCKS) + 1)
                act.activation(prob_st[:].rearrange("p g r -> p (g r)"), ps[:, 4, 0:2 * P], ACT.Copy).then_inc(swa_copied, 1)
                act.activation(prob_st2[:].rearrange("p g r -> p (g r)"), ps[0:DS, 5, 0:2 * P], ACT.Copy).then_inc(swa_copied, 1)
                act.wait_ge(swa_out, BLOCKS + 1)
                for kv in range(2):
                    r = kv * HD
                    last = act.activation(mix_hi[r:r + HD, 0:GROUP, SEQ:T].rearrange("p h (b t) -> p b h t", b=DB),
                                          ps[r:r + HD, 7, 0:DB * NS].rearrange("p (b g h t) -> p b g h t", b=DB, g=2, h=GROUP)[:, :, kv],
                                          ACT.Copy)
                last.then_inc(mix_hi_done, 1)
                mixer_out(EVEN_OUT, 1)

            def odd():
                for t in range(ODD_IN):
                    n = S_ODD + t
                    if t == 0:
                        root(stat(4), D)
                    split_next(n)
                    if t < 3 * CT and t % 3 == 2:
                        mix_upper(mix_hi[:, t // 3, :], prod[:], mix_ready, SGT + t // 3 + 1)
                    if CQ0 <= n < CKV0:
                        c = n - CQ0
                        act.wait_ge(acc_read, n + 1)
                        act.activation(cq_hi[:, c, :], (prod if c % 2 else silu)[:], ACT.Copy, scale=q_gain[:, c:c + 1]).then_inc(cq_hi_done, 1)
                    if n == KPE:
                        root(stat(4) + 1, Q_LORA)
                for h in range(HEADS):
                    split_next(ODD_UQ + h)
                    if h == 0:
                        root(stat(4) + 2, KV_LORA)
                    if h == 1:
                        act.wait_ge(kpe_done, 1)
                        for hh in range(HEADS):
                            last = act.activation(kf[NOPE:QK, hh, :], kpe[NOPE:QK, 0:SEQ], ACT.Copy)
                        last.then_inc(kf_done, 1)
                for h in range(HEADS):
                    act.wait_ge(kf_ready, h + 1)
                    act.activation(kf[0:NOPE, h, :], ps[0:NOPE, 4 + h % 2, :], ACT.Copy).then_inc(kf_done, 1)
                for j in range(BLOCKS):
                    act.wait_ge(vm_ready, j + 1)
                    act.activation(v_mla[:, j, :], ps[:, 6 + j % 2, :], ACT.Copy).then_inc(vm_done, 1)

                def exps(h):
                    act.wait_ge(mla_max, h + 1)
                    if h:
                        act.wait_ge(mla_turned, h)
                    for i in range(BLOCKS):
                        s = i * (i + 1) // 2
                        last = act.activation(p_mla[:, s:s + i + 1, :].rearrange("p j k -> p (j k)"), ps[:, i, 0:(i + 1) * P], ACT.Exp,
                                              bias=nmx[:, i:i + 1], scale=MLA_SCALE, accum_out=sm[:, i:i + 1])
                    last.then_inc(mla_exp, 1)
                exps(0)
                for h in range(HEADS):
                    act.wait_ge(mla_turned, h + 1)
                    if h:
                        act.wait_ge(mla_out, h)
                    flat = p_mla_t[:].rearrange("p s q -> p (s q)")
                    last = act.activation(flat, ps_flat[:, 4 * 512:4 * 512 + 10 * P], ACT.Copy)
                    last.then_inc(mla_copied, 1)
                    if h + 1 < HEADS:
                        exps(h + 1)
                    r = VD * (h % 2)
                    mix_upper(mix_hi[r:r + VD, CT + h // 2, 0:SEQ], ps[r:r + VD, 7, :], mla_out, h + 1)
                act.wait_ge(new_turned, 1)
                act.activation(ckv_new[:].rearrange("p b c -> p (b c)"), ps_flat[0:DS, 4 * 512:8 * 512], ACT.Copy).then_inc(new_copied, 1)

                def sample_exps(g):
                    act.wait_ge(s_max, g + 1)
                    if g:
                        act.wait_ge(s_turned, 5 * g)
                    act.activation(p_s[:, 0:PAGES * PAGE], ps_flat[:, 0:PAGES * PAGE], ACT.Exp, bias=nmx[:, 3:4], scale=MLA_SCALE,
                                   accum_out=sm[:, 0:1])
                    act.activation(p_s[:, PAGES * PAGE:PAGES * PAGE + DS], s_new[:], ACT.Exp, bias=nmx[:, 3:4], scale=MLA_SCALE,
                                   accum_out=sm[:, 1:2]).then_inc(s_exp, 1)

                def sample_copies(g):
                    for q in range(5):
                        u = 5 * g + q
                        act.wait_ge(s_turned, u + 1)
                        if g and q == 0:
                            act.wait_ge(s_out, g)
                        if q < 4:
                            act.activation(p_st[:, 4 * q:4 * q + 4, :].rearrange("p j r -> p (j r)"), ps[:, 4 + u % 2, :], ACT.Copy)\
                               .then_inc(s_copied, 1)
                        else:
                            act.activation(p_st2[:], ps[0:DS, 4 + u % 2, 0:P], ACT.Copy).then_inc(s_copied, 1)
                sample_exps(0)
                sample_copies(0)
                sample_exps(1)
                sample_copies(1)
                mix_upper(mix_hi[:, CT:2 * CT, SEQ:T], ps[:, 4, 0:CT * NS].rearrange("p (h t) -> p h t", h=CT), s_out, 3)
                mixer_out(ODD_OUT, 4)

            act.wait_ge(consts_landed, CONSTS)
            act.wait_ge(x_landed, 16)
            for t in range(DT):
                input_hi(0, t)
            split_hi(0, 0, DT * P)
            split_hi(1, 1, DT * P)
            ffn(*FFNS[0])
            even()
            ffn(*FFNS[1])
            ffn(*FFNS[2])
            odd()
            ffn(*FFNS[3])
            root(stat(6), D)

        @block.vector
        def _(dve):
            steps = [0]

            def link(ins):
                steps[0] += 1
                ins.then_inc(step, 1)
                dve.wait_ge(step, steps[0])

            def split_lo(n, slot, cols):
                dve.wait_ge(w_hi_done, n + 1)
                dve.tensor_tensor(w_lo[slot][:, 0:cols], raw[slot][:, 0:cols], w_hi[slot][:, 0:cols].bitcast(F32),
                                  ALU.subtract).then_inc(w_lo_done, 1)

            def split_next(n):
                if n + 2 < N_PANELS:
                    split_lo(n + 2, n % 2, panel_cols(n + 2))

            def invert(k, out=None):
                dve.wait_ge(rms_done, k)
                dve.reciprocal((rinv if out is None else out)[:], rms[:]).then_inc(rinv_ready, 1)
                dve.wait_ge(rinv_ready, k)

            def scaled(n, out, by, rows=P):
                dve.wait_ge(panel_done, n + 1)
                dve.tensor_tensor(halves(out), acc_of(n % 2, rows), halves(by), ALU.mult).then_inc(acc_read, 1)

            def input_lo(norm, m):
                dve.wait_ge(hx_hi_done, DT * norm + m + 1)
                dve.scalar_tensor_tensor(out=tile_of(hx_lo, m), in0=tile_of(x, m), scalar=gains[:, norm, bass.ds(m, 1)],
                                         in1=tile_of(hx_hi, m).bitcast(F32), op0=ALU.mult, op1=ALU.subtract).then_inc(hx_done, 1)

            def add_to_x(n, slot, m, factor):
                dve.wait_ge(panel_done, n + 1)
                xm = halves(tile_of(x, m))
                dve.scalar_tensor_tensor(out=xm, in0=acc_of(slot), scalar=factor, in1=xm, op0=ALU.mult, op1=ALU.add)\
                   .then_inc(acc_read, 1)

            def mix_lower(piece, out, src, hi):
                dve.wait_ge(mix_hi_done, piece + 1)
                dve.tensor_tensor(out, src, hi.bitcast(F32), ALU.subtract).then_inc(mix_done, 1)

            def ffn(start, f, norm):
                for c in range(CHUNKS):
                    n0 = start + c * (2 * FT + DT)
                    h0 = (f * CHUNKS + c) * FT

                    def tile(i, cols):
                        dve.wait_ge(panel_done, n0 + 2 * i + 1)
                        dve.tensor_tensor(halves(gate[:]), acc_of(n0 % 2), halves(rinv[:]), ALU.mult).then_inc(acc_read, 1)
                        split_lo(n0 + 2 * i + 2, n0 % 2, cols)
                        dve.wait_ge(panel_done, n0 + 2 * i + 2)
                        dve.tensor_tensor(halves(up[:]), acc_of((n0 + 1) % 2), halves(rinv[:]), ALU.mult).then_inc(acc_read, 1)
                        dve.wait_ge(silu_done, h0 + i + 1)
                        dve.wait_ge(acc_read, n0 + 2 * i + 2)
                        dve.tensor_tensor(prod[:], up[:], silu[:], ALU.mult).then_inc(prod_ready, 1)
                        split_lo(n0 + 2 * i + 3, (n0 + 1) % 2, cols)
                        dve.wait_ge(hid_hi_done, h0 + i + 1)
                        dve.tensor_tensor(tile_of(hid_lo, i), prod[:], tile_of(hid_hi, i).bitcast(F32), ALU.subtract).then_inc(hid_done, 1)
                    if c == 0:
                        invert(stat(norm))
                    with dve.Fori(0, FT - 1) as i:
                        tile(i, DT * P)
                    tile(FT - 1, FT * P)
                    n1 = n0 + 2 * FT

                    def final_input(m):
                        if c == CHUNKS - 1 and norm + 1 < N_NORMS - 1:
                            input_lo(norm + 1, m)
                    with dve.Fori(0, DT // 2 - 1) as i:
                        for s in range(2):
                            add_to_x(n1 + 2 * i + s, (n1 + s) % 2, 2 * i + s, 0.5)
                            split_lo(n1 + 2 * i + s + 2, (n1 + s) % 2, FT * P)
                            final_input(2 * i + s)
                    for m in (DT - 2, DT - 1):
                        add_to_x(n1 + m, (n1 + m) % 2, m, 0.5)
                        split_next(n1 + m)
                        final_input(m)

            def mixer_out(start, norm):
                for m in range(DT):
                    add_to_x(start + m, (start + m) % 2, m, 1.0)
                    split_next(start + m)
                    input_lo(norm + 1, m)

            def turned_g(tt):
                rows = P if tt < BLOCKS else NS
                dve.wait_ge(g_turned, tt + 1)
                dve.tensor_copy(v_ln[0:rows, tt, :], ps[0:rows, 4 + tt % 4, :]).then_inc(v_ln_read, 1)
                dve.wait_ge(v_ln_read, tt + 1)
                link(dve.bn_stats(ln_st[0:rows, :], v_ln[0:rows, tt, :]))
                stats_of = dve.bn_aggr(ln_mv[0:rows, tt, :], ln_st[0:rows, :])
                if tt == BLOCKS:
                    stats_of.then_inc(ln_var, 1)
                else:
                    link(stats_of)

            def normed_g(tt):
                rows = P if tt < BLOCKS else NS
                v = v_ln[0:rows, tt, :]
                link(dve.tensor_scalar(v, v, ln_mv[0:rows, tt, 0:1], ln_r[0:rows, tt:tt + 1], ALU.subtract, ALU.mult))
                link(dve.tensor_tensor(v, v, ln_g[0:rows, :], ALU.mult))
                dve.tensor_tensor(v, v, ln_b[0:rows, :], ALU.add).then_inc(v_ln_done, 1)

            def gated(g):
                out = (up if g % 2 else prod)
                dve.wait_ge(gate_sum, g + 1)
                if g >= 2:
                    dve.wait_ge(mix_done, SGU_PIECE + g - 1)
                b0 = 4 + 2 * (g % 2)
                dve.tensor_tensor(out[:, 0:SEQ], ps[:, b0, :], pre[:, SGT + g, 0:SEQ], ALU.mult)
                dve.tensor_tensor(out[:, SEQ:T], ps[:, b0 + 1, 0:NS], pre[:, SGT + g, SEQ:T], ALU.mult).then_inc(mix_ready, 1)

            def gated_lower(g):
                mix_lower(SGU_PIECE + g, mix_lo[:, GROUP + g, :], (up if g % 2 else prod)[:], mix_hi[:, GROUP + g, :])

            def maxima(p3, cols, sinks):
                link(dve.tensor_reduce(smax[:, 0:cols], p3, AX, ALU.max))
                link(dve.tensor_tensor(smax[:, 0:cols], smax[:, 0:cols], sinks, ALU.max))
                link(dve.tensor_scalar(nmax[:, 0:cols], smax[:, 0:cols], -1.0, None, ALU.mult))
                dve.tensor_tensor(dsink[:, 0:cols], sinks, smax[:, 0:cols], ALU.subtract).then_inc(swa_max, 1)

            def swa_softmax_in(n):
                dve.wait_ge(swa_scored, n + 1)
                if n >= 2:
                    dve.wait_ge(swa_turned, swa_units(n - 1))
                lo = swa_halves(n)[0] * WIN
                p3 = prob[n % 2][:, :, lo:2 * WIN]
                dve.scalar_tensor_tensor(out=p3, in0=ps_flat[:, 0:HEADS * 2 * WIN].rearrange("p (h k) -> p h k", h=HEADS)[:, :, lo:2 * WIN],
                                         scalar=SWA_SCALE, in1=bias[:, :, lo:2 * WIN], op0=ALU.mult, op1=ALU.add).then_inc(swa_biased, 1)
                dve.wait_ge(swa_biased, n + 1)
                maxima(p3, HEADS, sink[:])

            def swa_softmax_out(n):
                dve.wait_ge(swa_exp, n + 1)
                link(dve.tensor_tensor(rsum[:], rsum[:], esink[:], ALU.add))
                link(dve.reciprocal(rden[:], rsum[:]))
                lo = swa_halves(n)[0] * WIN
                for h in range(HEADS):
                    p = prob[n % 2][:, h, lo:2 * WIN]
                    last = dve.tensor_scalar(p, p, rden[:, h:h + 1], None, ALU.mult)
                last.then_inc(swa_prob, 1)

            def swa_lower(n):
                mix_lower(SWA_PIECE + n, mix_lo[:, 0:GROUP, n * WIN:(n + 1) * WIN],
                          ps[:, 7, :].rearrange("p (h q) -> p h q", h=GROUP), mix_hi[:, 0:GROUP, n * WIN:(n + 1) * WIN])

            def sample_softmax_in():
                dve.wait_ge(swa_scored, BLOCKS + 1)
                for g in range(2):
                    last = dve.scalar_tensor_tensor(out=prob_s[:, g, :], in0=ps[:, g, 0:WIN + DS], scalar=SWA_SCALE, in1=bias_s[:],
                                                    op0=ALU.mult, op1=ALU.add)
                link(last)
                link(dve.tensor_reduce(smax[:, 0:2], prob_s[:], AX, ALU.max))
                link(dve.tensor_scalar(smax[:, 0:2], smax[:, 0:2], sink_s[:, 0:1], None, ALU.max))
                link(dve.tensor_scalar(nmax[:, 0:2], smax[:, 0:2], -1.0, None, ALU.mult))
                dve.tensor_scalar(dsink[:, 0:2], nmax[:, 0:2], sink_s[:, 0:1], None, ALU.add).then_inc(swa_max, 1)

            def sample_softmax_out():
                dve.wait_ge(swa_exp, BLOCKS + 1)
                link(dve.tensor_tensor(rsum[:, 0:2], rsum[:, 0:2], esink[:, 0:2], ALU.add))
                link(dve.reciprocal(rden[:, 0:2], rsum[:, 0:2]))
                for g in range(2):
                    last = dve.tensor_scalar(prob_s[:, g, :], prob_s[:, g, :], rden[:, g:g + 1], None, ALU.mult)
                last.then_inc(swa_prob, 1)

            def even():
                for t in range(EVEN_IN):
                    n = S_EVEN + t
                    if t == 0:
                        invert(stat(1))
                        dve.wait_ge(even_landed, EVEN_LOADS)
                    scaled(n, pre[:, t, :], rinv[:])
                    split_next(n)
                    if t == 1:
                        link(dve.memset(q_bd[:], 0.0))
                    if SGT + 2 <= t <= SGT + 6:
                        turned_g(t - SGT - 2)
                    if t == SGT + 7:
                        dve.wait_ge(ln_sd_done, 1)
                        link(dve.reciprocal(ln_r[:, 0:4], ln_sd[:, 0:4]))
                        link(dve.reciprocal(ln_r[0:NS, 4:5], ln_sd[0:NS, 4:5]))
                        normed_g(0)
                        normed_g(1)
                    if t == SGT + 8:
                        dve.wait_ge(acc_read, n + 1)
                        for kv in range(2):
                            r = kv * HD
                            last = dve.tensor_copy(
                                q_bd[r:r + HD, :, kv * GROUP * DS:(kv + 1) * GROUP * DS].rearrange("p b (h t) -> p b h t", h=GROUP),
                                pre[r:r + HD, 8:12, SEQ:T].rearrange("p h (b t) -> p b h t", b=DB))
                        last.then_inc(q_bd_ready, 1)
                        normed_g(2)
                        normed_g(3)
                    if t == SGT + 9:
                        normed_g(4)
                swa_softmax_in(0)
                for g in range(SGT):
                    gated(g)
                    if g:
                        gated_lower(g - 1)
                gated_lower(SGT - 1)
                swa_softmax_out(0)
                for n in range(BLOCKS):
                    if n + 1 < BLOCKS:
                        swa_softmax_in(n + 1)
                        swa_softmax_out(n + 1)
                    else:
                        sample_softmax_in()
                        sample_softmax_out()
                    swa_lower(n)
                for kv in range(2):
                    r = kv * HD
                    if kv == 0:
                        dve.wait_ge(mix_hi_done, SWA_S_PIECE + 1)
                    last = dve.tensor_tensor(mix_lo[r:r + HD, 0:GROUP, SEQ:T].rearrange("p h (b t) -> p b h t", b=DB),
                                             ps[r:r + HD, 7, 0:DB * NS].rearrange("p (b g h t) -> p b g h t", b=DB, g=2, h=GROUP)[:, :, kv],
                                             mix_hi[r:r + HD, 0:GROUP, SEQ:T].bitcast(F32).rearrange("p h (b t) -> p b h t", b=DB), ALU.subtract)
                last.then_inc(mix_done, 1)
                mixer_out(EVEN_OUT, 1)

            def convolve(t):
                zs = conv_zs[:, t]
                out = prod[:, 0:SEQ]
                out_s = prod[:, SEQ:T].rearrange("p (b s) -> p b s", b=DB)
                link(dve.tensor_scalar(out, conv_z[:, t, 0:SEQ], conv_w[:, 0, t:t + 1], None, ALU.mult))
                link(dve.tensor_scalar(out_s, zs[:, :, 0:DS], conv_w[:, 0, t:t + 1], None, ALU.mult))
                for j in range(1, 3):
                    link(dve.scalar_tensor_tensor(out=out, in0=conv_z[:, t, j:j + SEQ], scalar=conv_w[:, j, t:t + 1], in1=out,
                                                  op0=ALU.mult, op1=ALU.add))
                    link(dve.scalar_tensor_tensor(out=out_s, in0=zs[:, :, j:j + DS], scalar=conv_w[:, j, t:t + 1], in1=out_s,
                                                  op0=ALU.mult, op1=ALU.add))
                dve.tensor_tensor(prod[:], prod[:], silu[:], ALU.mult).then_inc(mix_ready, 1)

            def rope(t2d, count):
                r = slice(NOPE, QK)
                dve.wait_ge(rotated, count)
                dve.tensor_tensor(halves(silu[r, :]), ps[r, 6:8, 0:TH], halves(sin[r, :]), ALU.mult)
                link(dve.tensor_tensor(prod[r, :], t2d, cos[r, :], ALU.mult))
                return dve.tensor_tensor(t2d, prod[r, :], silu[r, :], ALU.add)

            def mla_maxima(h):
                dve.wait_ge(mla_scored, h + 1)
                diag = ps_flat[:, 0:BLOCKS * 640].rearrange("p (i c) -> p i c", i=BLOCKS)[:, :, 0:P]
                link(dve.tensor_tensor(diag, diag, causal[:].unsqueeze(1).to_broadcast([P, BLOCKS, P]), ALU.add))
                for i in range(BLOCKS):
                    last = dve.tensor_reduce(mx[:, i:i + 1], ps[:, i, 0:(i + 1) * P], AX, ALU.max)
                link(last)
                dve.tensor_scalar(nmx[:], mx[:], -MLA_SCALE, None, ALU.mult).then_inc(mla_max, 1)

            def mla_normalise(h):
                dve.wait_ge(mla_exp, h + 1)
                link(dve.reciprocal(rs[:], sm[:]))
                for i in range(BLOCKS):
                    p = p_mla[:, i * (i + 1) // 2:(i + 1) * (i + 2) // 2, :].rearrange("p j k -> p (j k)")
                    last = dve.tensor_scalar(p, p, rs[:, i:i + 1], None, ALU.mult)
                last.then_inc(mla_prob, 1)

            def mla_lower(h):
                r = VD * (h % 2)
                mix_lower(MLA_PIECE + h, mix_lo[r:r + VD, CT + h // 2, 0:SEQ], ps[r:r + VD, 7, :], mix_hi[r:r + VD, CT + h // 2, 0:SEQ])

            def sample_new(g):
                dve.wait_ge(s_new_ready, g + 1)
                if g:
                    dve.wait_ge(s_exp, g)
                dve.tensor_tensor(s_new[:], ps[:, 4, 0:DS], causal_s[:], ALU.add).then_inc(s_new_read, 1)

            def sample_maxima(g):
                dve.wait_ge(keys_read, (4 * g + 4) * (PAGES // PAIR))
                dve.tensor_reduce(mx[:, 0:1], ps_flat[:, 0:PAGES * PAGE], AX, ALU.max)
                dve.wait_ge(s_new_read, g + 1)
                link(dve.tensor_reduce(mx[:, 1:2], s_new[:], AX, ALU.max))
                link(dve.tensor_tensor(mx[:, 2:3], mx[:, 0:1], mx[:, 1:2], ALU.max))
                dve.tensor_scalar(nmx[:, 3:4], mx[:, 2:3], -MLA_SCALE, None, ALU.mult).then_inc(s_max, 1)

            def sample_normalise(g):
                dve.wait_ge(s_exp, g + 1)
                link(dve.tensor_tensor(rs[:, 0:1], sm[:, 0:1], sm[:, 1:2], ALU.add))
                link(dve.reciprocal(rs[:, 1:2], rs[:, 0:1]))
                dve.tensor_scalar(p_s[:], p_s[:], rs[:, 1:2], None, ALU.mult).then_inc(s_prob, 1)

            def sample_latent(g):
                dve.wait_ge(s_out, g + 1)
                for c in range(KT):
                    last = dve.tensor_copy(o_lat[:, c].rearrange("p h (b t) -> p b h t", b=DB)[:, 4 * g:4 * g + 4],
                                           ps[:, 6 + c, 0:4 * NS].rearrange("p (b h t) -> p b h t", b=4, h=HEADS))
                last.then_inc(o_lat_done, 1)

            def odd():
                for t in range(ODD_IN):
                    n = S_ODD + t
                    if t == 0:
                        invert(stat(4))
                        dve.wait_ge(odd_landed, ODD_LOADS)
                        link(dve.memset(conv_z[:, :, 0:2], 0.0))
                    if t < 3 * CT:
                        scaled(n, (gate, up, silu)[t % 3][:], rinv[:])
                        split_next(n)
                        dve.wait_ge(acc_read, n + 1)
                        if t % 3 == 1:
                            link(dve.tensor_tensor(conv_z[:, t // 3, 2:SEQ + 2], gate[:, 0:SEQ], up[:, 0:SEQ], ALU.mult))
                            link(dve.tensor_tensor(conv_zs[:, t // 3, :, 2:DS + 2], gate[:, SEQ:T].rearrange("p (b s) -> p b s", b=DB),
                                                   up[:, SEQ:T].rearrange("p (b s) -> p b s", b=DB), ALU.mult))
                        if t % 3 == 2:
                            convolve(t // 3)
                            mix_lower(CONV_PIECE + t // 3, mix_lo[:, t // 3, :], prod[:], mix_hi[:, t // 3, :])
                    elif n < CKV0:
                        c = n - CQ0
                        if c >= 2:
                            dve.wait_ge(square_done, 5 * DT + c - 1)
                        buf = prod if c % 2 else silu
                        scaled(n, buf[:], rinv[:])
                        split_next(n)
                        dve.wait_ge(cq_hi_done, c + 1)
                        dve.wait_ge(acc_read, n + 1)
                        dve.scalar_tensor_tensor(out=cq_lo[:, c, :], in0=buf[:], scalar=q_gain[:, c:c + 1], in1=cq_hi[:, c, :].bitcast(F32),
                                                 op0=ALU.mult, op1=ALU.subtract).then_inc(cq_done, 1)
                    else:
                        scaled(n, kpe[:] if n == KPE else ckv[:, n - CKV0, :], rinv[:])
                        split_next(n)
                invert(stat(4) + 1, gate)
                for h in range(HEADS):
                    n = ODD_UQ + h
                    dve.wait_ge(panel_done, n + 1)
                    dve.tensor_tensor(halves(qf[0:QK, h, :]), acc_of(n % 2, QK), halves(gate[0:QK, :]), ALU.mult).then_inc(acc_read, 1)
                    split_next(n)
                    if h == 0:
                        invert(stat(4) + 2, up)
                        for c in range(KT):
                            dve.wait_ge(square_done, 5 * DT + QT + KT)
                            dve.scalar_tensor_tensor(out=ckv[:, c, :], in0=ckv[:, c, :], scalar=kv_gain[:, c:c + 1], in1=up[:],
                                                     op0=ALU.mult, op1=ALU.mult).then_inc(ckv_done, 1)
                        dve.wait_ge(spare_landed, 48)
                        rope(kpe[NOPE:QK, :], 1).then_inc(kpe_done, 1)
                    else:
                        rope(qf[NOPE:QK, h - 1, :], h + 1).then_inc(q_done, 1)
                rope(qf[NOPE:QK, HEADS - 1, :], HEADS + 1).then_inc(q_done, 1)
                mla_maxima(0)
                mla_normalise(0)
                for h in range(HEADS):
                    if h + 1 < HEADS:
                        mla_maxima(h + 1)
                        mla_normalise(h + 1)
                    mla_lower(h)
                dve.wait_ge(qa_ready, 1)
                for j in range(3):
                    rows = QK if j < 2 else NOPE
                    src = ps[0:rows, 4, j * HEADS * NS:(j + 1) * HEADS * NS] if j < 2 else ps[0:rows, 5, 0:HEADS * NS]
                    dve.tensor_copy(qa[0:rows, j].rearrange("p b (h t) -> p b h t", h=HEADS), src.rearrange("p (h b t) -> p b h t", h=HEADS, b=DB))
                for c in range(KT):
                    dve.tensor_copy(qa_new[:, c].rearrange("p b (h t) -> p b h t", h=HEADS),
                                    ps[:, 6, c * HEADS * NS:(c + 1) * HEADS * NS].rearrange("p (h b t) -> p b h t", h=HEADS, b=DB))
                dve.tensor_copy(qa[NOPE:QK, 2].rearrange("p b (h t) -> p b h t", h=HEADS),
                                qf[NOPE:QK, :, SEQ:T].rearrange("p h (b t) -> p b h t", b=DB)).then_inc(qa_done, 1)
                sample_new(0)
                sample_maxima(0)
                sample_normalise(0)
                sample_new(1)
                sample_maxima(1)
                dve.wait_ge(s_turned, 5)
                sample_normalise(1)
                sample_latent(0)
                sample_latent(1)
                mix_lower(MLA_S_PIECE, mix_lo[:, CT:2 * CT, SEQ:T], ps[:, 4, 0:CT * NS].rearrange("p (h t) -> p h t", h=CT), mix_hi[:, CT:2 * CT, SEQ:T])
                mixer_out(ODD_OUT, 4)

            dve.wait_ge(dist_ready, 1)
            dve.tensor_copy(by_dist[:], ps[0:HEADS, 7, 0:3 * WIN]).then_inc(dist_copied, 1)
            dve.wait_ge(consts_landed, CONSTS)
            for t in range(DT):
                input_lo(0, t)
            split_lo(0, 0, DT * P)
            split_lo(1, 1, DT * P)
            ffn(*FFNS[0])
            even()
            ffn(*FFNS[1])
            ffn(*FFNS[2])
            odd()
            ffn(*FFNS[3])
            invert(stat(6))
            for t in range(DT):
                dve.scalar_tensor_tensor(out=y[:, t, :], in0=x[:, t, :], scalar=gains[:, N_NORMS - 1, t:t + 1], in1=rinv[:],
                                         op0=ALU.mult, op1=ALU.mult).then_inc(y_done, 1)

        @block.gpsimd
        def _(pool):
            def add_square(k, src, first):
                pool.tensor_tensor(sumsq[:] if first else square[:], src, src, ALU.mult).then_inc(square_done, 1)
                pool.wait_ge(square_done, k + 1)
                if first:
                    pool.nop().then_inc(sumsq_step, 1)
                else:
                    pool.tensor_tensor(sumsq[:], sumsq[:], square[:], ALU.add).then_inc(sumsq_step, 1)

            def x_squares(k0, n1):
                pool.wait_ge(acc_read, n1 + 1)
                add_square(k0, x[:, 0, :], True)
                with pool.Fori(1, DT) as m:
                    pool.wait_ge(acc_read, n1 + m + 1)
                    pool.wait_ge(sumsq_step, k0 + m)
                    add_square(k0 + m, tile_of(x, m), False)

            def ffn_end(start):
                return start + CHUNKS * (2 * FT + DT) - DT

            for t, name in ((rel, "rel"), (onehot, "onehot")):
                pool.dma_start(t[:], d[name]).then_inc(rel_landed, 16)
            for t, name in ((ident, "ident"), (ones, "ones"), (gains, "gains"), (eps, "eps")):
                pool.dma_start(t[:], d[name]).then_inc(consts_landed, 16)
            pool.wait_ge(x_landed, 16)
            add_square(0, x[:, 0, :], True)
            with pool.Fori(1, DT) as m:
                pool.wait_ge(sumsq_step, m)
                add_square(m, tile_of(x, m), False)
            pool.wait_ge(dist_copied, 1)
            pool.dma_start(d["dist"], by_dist[:].unsqueeze(1).to_broadcast([HEADS, P, 3 * WIN])).then_inc(dist_stored, 16)
            pool.wait_ge(dist_stored, 16)
            dist = d["dist"]
            row = P * 3 * WIN
            pool.dma_start(bias[:], bass.AP(dist.tensor, P - 1, [[3 * WIN - 1, P], [row, HEADS], [1, 2 * WIN]])).then_inc(even_landed, 16)
            for b4 in range(4):
                pool.dma_start(bias_s[b4 * NS:(b4 + 1) * NS, :], bass.AP(dist.tensor, P - 1, [[row, HEADS], [3 * WIN - 1, DS], [1, WIN + DS]]))\
                    .then_inc(even_landed, 16)
            for t, name in ((sgu_w, "sgu_w"), (sgu_ws, "sgu_ws"), (sgu_b, "sgu_b"), (sgu_bs, "sgu_bs"), (ln_g, "ln_g"), (ln_b, "ln_b"),
                            (sink, "sink")):
                src = d[name] if name not in ("ln_g", "ln_b", "sink") else d[name].partition_broadcast(P)
                pool.dma_start(t[:], src).then_inc(even_landed, 16)
            for b4 in range(4):
                pool.dma_start(sink_s[b4 * NS:(b4 + 1) * NS, :], d["sink_s"]).then_inc(even_landed, 16)
            pool.wait_ge(even_landed, EVEN_LOADS)
            pool.affine_select(out=sgu_w[:], in_=sgu_w[:], compare_op=ALU.is_ge, fill=0.0, base=0, pattern=[[0, SGT], [1, P]],
                               channel_multiplier=-1).then_inc(sgu_masked, 1)
            pool.affine_select(out=sgu_ws[:], in_=sgu_ws[:], compare_op=ALU.is_ge, fill=0.0, base=0, pattern=[[0, SGT], [1, NS]],
                               channel_multiplier=-1).then_inc(sgu_masked, 1)
            x_squares(DT, ffn_end(START["f0"]))
            pool.wait_ge(panel_done, S_EVEN)
            for t, name in ((k_cache, "k_cache"), (v_cache, "v_cache")):
                pool.dma_start(t[:], d[name]).then_inc(cache_landed, 16)
            pool.wait_ge(acc_read, EVEN_OUT)
            for name, t, c0, c1 in (("o_kp", 12, SEQ - WIN, SEQ), ("o_vp", 13, SEQ - WIN, SEQ), ("o_ks", 12, SEQ, T), ("o_vs", 13, SEQ, T)):
                pool.dma_start(d[name], pre[:, t, c0:c1]).then_inc(stored_even, 16)
            pool.wait_ge(v_ln_done, 5)
            pool.dma_start(d["o_sgu"], v_ln[0:NS, 4, :]).then_inc(stored_even, 16)
            x_squares(2 * DT, EVEN_OUT)
            pool.wait_ge(mix_done, EVEN_PIECES)
            pool.wait_ge(stored_even, 16 * 5)
            for t, name in ((w_uk, "w_uk"), (w_uv, "w_uv"), (perm, "perm"), (conv_w, "conv_w"), (q_gain, "q_gain"), (kv_gain, "kv_gain"),
                            (causal, "causal"), (causal_s, "causal_s")):
                pool.dma_start(t[:], d[name]).then_inc(odd_landed, 16)
            for t in range(CT):
                pool.dma_start(conv_zs[:, t, :, 0:2], d["conv_state"][:, t]).then_inc(odd_landed, 16)
            pool.dma_start(table[:], d["table"]).then_inc(table_landed, 16)
            x_squares(3 * DT, ffn_end(START["f1"]))
            x_squares(4 * DT, ffn_end(START["f2"]))
            pool.wait_ge(panel_done, S_ODD)
            for t, name in ((w_uk_t, "w_uk_t"), (cos, "cos"), (sin, "sin")):
                pool.dma_start(t[:], d[name]).then_inc(spare_landed, 16)
            for c in range(QT):
                k = 5 * DT + c
                pool.wait_ge(acc_read, CQ0 + c + 1)
                if c:
                    pool.wait_ge(sumsq_step, k)
                add_square(k, (prod if c % 2 else silu)[:], c == 0)
            for c in range(KT):
                k = 5 * DT + QT + c
                pool.wait_ge(acc_read, CKV0 + c + 1)
                if c == 0:
                    pool.wait_ge(stat_ready, stat(4) + 1)
                else:
                    pool.wait_ge(sumsq_step, k)
                add_square(k, ckv[:, c, :], c == 0)
            pool.dma_start(d["o_convp"], conv_z[:, :, SEQ:SEQ + 2]).then_inc(stored_odd, 16)
            pool.dma_start(d["o_convs"], conv_zs[:, :, :, DS:DS + 2]).then_inc(stored_odd, 16)
            pool.wait_ge(ckv_done, KT)
            pool.dma_start(d["o_ckv"], ckv[:]).then_inc(stored_odd, 16)
            pool.wait_ge(kpe_done, 1)
            pool.dma_start(d["o_kpe"], kpe[NOPE:QK, :]).then_inc(stored_odd, 16)
            x_squares(6 * DT, ODD_OUT)
            x_squares(7 * DT, ffn_end(START["f3"]))


def rope_tables():
    half = ROPE // 2
    pos = np.concatenate([np.arange(SEQ), np.tile(PAGES * PAGE + np.arange(DS), DB)]).astype(np.float32)
    inv = np.exp(np.float32(-np.log(10000.0)) * np.arange(half, dtype=np.float32) / np.float32(half)).astype(np.float32)
    ang = pos[None, :] * inv[:, None]
    cos, sin = (np.tile(f(ang).astype(np.float32), (2, 1)) for f in (np.cos, np.sin))
    swap = np.zeros((ROPE, ROPE), np.float32)
    for i in range(half):
        swap[half + i, i] = -1.0
        swap[i, half + i] = 1.0
    return cos, sin, swap


def constants():
    c = {"ident": np.eye(P, dtype=np.float32), "ones": np.ones((P, P), np.float32), "eps": np.full((P, 1), EPS, np.float32)}
    dist = 2 * WIN - 1 - np.arange(3 * WIN)
    n = np.maximum(dist, 0)
    exact = BUCKETS // 2
    large = exact + (np.log(np.maximum(n, 1).astype(np.float32) / exact) / np.log(WIN / exact) * (BUCKETS - exact)).astype(np.int32)
    bucket = np.where(n < exact, n, np.minimum(large, BUCKETS - 1))
    bucket = np.where((dist >= 0) & (dist <= WIN), bucket, BUCKETS)
    c["onehot"] = (bucket[None, :] == np.arange(BUCKETS + 1)[:, None]).astype(np.float32)
    cos, sin, swap = rope_tables()
    pad = lambda a: np.concatenate([np.zeros((NOPE, a.shape[1]), np.float32), a, np.zeros((P - QK, a.shape[1]), np.float32)])
    c["cos"], c["sin"], c["perm"] = pad(cos), pad(sin), pad(swap)
    q = np.arange(P)
    c["causal"] = np.where(q[None, :] <= q[:, None], 0.0, NEG).astype(np.float32)
    c["causal_s"] = np.where(np.arange(DS)[None, :] <= (q % DS)[:, None], 0.0, NEG).astype(np.float32)
    return c


def panels(w, m=P):
    *lead, k, cols = w.shape
    w = w.reshape(*lead, k // P, P, cols // m, m)
    n = len(lead)
    w = w.transpose(*range(n), n + 2, n + 1, n, n + 3)
    return np.ascontiguousarray(w).reshape(*lead, cols // m, P, k // P * m)


def features(v):
    v = v.reshape(*v.shape[:-1], v.shape[-1] // P, P)
    return np.ascontiguousarray(np.moveaxis(v, -1, 0))


def layout(i):
    a = constants()
    tok = np.concatenate([i["x_prompt"].reshape(SEQ, D), i["x_sample"].reshape(NS, D)], 0)
    a["xT"] = tok.T.reshape(DT, P, T).transpose(1, 0, 2)
    for f in (1, 2):
        g, u = panels(i[f"ffn{f}_w_gate"]), panels(i[f"ffn{f}_w_up"])
        a[f"gu{f}"] = np.stack([g, u], 2)
        dn = i[f"ffn{f}_w_down"]
        a[f"down{f}"] = panels(dn.reshape(dn.shape[0], CHUNKS, FT * P, D))
    a["gains"] = features(np.stack([i["ffn1_norm"][0], i["mix_norm"][0], i["ffn2_norm"][0], i["ffn1_norm"][1], i["mix_norm"][1],
                                    i["ffn2_norm"][1], i["final_norm"]]))
    q_w, kv_w = HEADS * HD, 2 * HD
    pair = np.concatenate([np.r_[t * HD:(t + 1) * HD, (GROUP + t) * HD:(GROUP + t + 1) * HD] for t in range(GROUP)])
    w = i["even_w_in"][0]
    u0 = q_w + 2 * kv_w
    order = np.concatenate([np.arange(u0 + SGW, u0 + 2 * SGW), np.arange(u0, u0 + SGW), pair, np.arange(q_w, u0)])
    a["even_in"] = panels(w[:, order])
    a["even_out"] = panels(i["even_w_out"][0][np.concatenate([pair, np.arange(q_w, q_w + SGW)])])
    a["rel"] = np.concatenate([i["rel_bias"], np.full((1, HEADS), NEG, np.float32)])
    a["sink"] = i["attn_sinks"][0]
    a["sink_s"] = np.repeat(i["attn_sinks"][0], DS)[:, None]
    a["ln_g"], a["ln_b"] = i["sgu_ln_g"][0], i["sgu_ln_b"][0]
    sw = i["sgu_w"][0]
    a["sgu_w"] = sw.transpose(2, 0, 1)
    ws = np.zeros((NS, SGT, NS), np.float32)
    for b in range(DB):
        ws[b * DS:(b + 1) * DS, :, b * DS:(b + 1) * DS] = sw[:, :DS, :DS].transpose(2, 0, 1)
    a["sgu_ws"] = ws
    a["sgu_b"] = i["sgu_b"]
    a["sgu_bs"] = np.tile(i["sgu_b"][:, :, :DS], (1, 1, DB))
    k, v = i["cache_swa_k"][0].reshape(DB, WIN, P), i["cache_swa_v"][0].reshape(DB, WIN, P)
    a["k_nat"], a["v_nat"] = k, v
    a["k_cache"], a["v_cache"] = k.transpose(2, 0, 1), v.transpose(1, 0, 2)
    c_w = CT * P
    w = i["odd_w_in"][0]
    tiles = [np.arange(s * c_w + t * P, s * c_w + (t + 1) * P) for t in range(CT) for s in (1, 2, 0)]
    k0 = 3 * c_w + Q_LORA + KV_LORA
    order = np.concatenate(tiles + [np.arange(3 * c_w, k0)] + [np.arange(k0, k0 + ROPE)] * 4)
    a["odd_in"] = panels(w[:, order])
    a["odd_out"] = panels(i["odd_w_out"][0])
    a["w_uq"] = panels(i["mla_w_uq"][0], QK)
    a["q_gain"], a["kv_gain"] = features(i["mla_q_norm"][0]), features(i["mla_kv_norm"][0])
    uk, uv = i["mla_w_uk"][0], i["mla_w_uv"][0]
    a["w_uk"] = uk.reshape(KT, P, HEADS * NOPE).transpose(1, 0, 2)
    a["w_uv"] = uv.reshape(KT, P, HEADS * VD).transpose(1, 0, 2)
    a["w_uk_t"] = uk.transpose(2, 1, 0)
    a["conv_w"] = features(i["conv_w"][0])
    a["conv_state"] = i["state_conv"][0].reshape(DB, 2, CT, P).transpose(3, 2, 0, 1)
    keys = np.concatenate([i["cache_mla_ckv"][0], i["cache_mla_kpe"][0]], -1)
    a["key_pool"] = keys.reshape(N_POOL, PAGE, 3, QK).transpose(0, 3, 2, 1)
    a["val_pool"] = i["cache_mla_ckv"][0]
    a["table"] = i["page_table"].reshape(1, DB * PAGES)
    return {k: np.ascontiguousarray(v) for k, v in a.items()}


OUTPUTS = {"o_y": (P, DT, T), "o_kp": (P, WIN), "o_vp": (P, WIN), "o_ks": (P, NS), "o_vs": (P, NS), "o_kc": (DB, WIN - DS, P),
           "o_vc": (DB, WIN - DS, P), "o_sgu": (NS, SGW), "o_convp": (P, CT, 2), "o_convs": (P, CT, DB, 2), "o_ckv": (P, KT, T),
           "o_kpe": (ROPE, T)}


def results(o):
    y = o["o_y"].transpose(2, 1, 0).reshape(T, D)
    heads = (2, HD)

    def window(cached, new):
        new = new.T.reshape(DB, DS, P)
        return np.concatenate([cached, new], 1).reshape(1, DB, WIN, *heads)
    ckv = o["o_ckv"].transpose(2, 1, 0).reshape(T, KV_LORA)
    kpe = o["o_kpe"].T
    return (y[:SEQ].reshape(1, SEQ, D), y[SEQ:].reshape(DB, DS, D),
            o["o_kp"].T.reshape(1, 1, WIN, *heads), o["o_vp"].T.reshape(1, 1, WIN, *heads),
            window(o["o_kc"], o["o_ks"]), window(o["o_vc"], o["o_vs"]),
            o["o_sgu"].reshape(1, DB, DS, SGW),
            o["o_convp"].transpose(2, 1, 0).reshape(1, 1, 2, CT * P),
            o["o_convs"].transpose(2, 3, 1, 0).reshape(1, DB, 2, CT * P),
            ckv[:SEQ].reshape(1, 1, SEQ, KV_LORA), kpe[:SEQ].reshape(1, 1, SEQ, ROPE),
            ckv[SEQ:].reshape(1, DB, DS, KV_LORA), kpe[SEQ:].reshape(1, DB, DS, ROPE))


def kernel(**inputs):
    import concourse.bacc as bacc
    from concourse.bass_utils import run_bass_kernel_spmd

    arrays = layout({k: np.asarray(v) for k, v in inputs.items()})
    nc = bacc.Bacc("TRN2", target_bir_lowering=False, num_devices=1)
    d = {k: nc.dram_tensor(k, v.shape, mybir.dt.from_np(v.dtype), kind="ExternalInput").ap() for k, v in arrays.items()}
    for k, shape in OUTPUTS.items():
        d[k] = nc.dram_tensor(k, shape, F32, kind="ExternalOutput").ap()
    d["dist"] = nc.dram_tensor("dist", (HEADS, P, 3 * WIN), F32, kind="Internal").ap()
    decoder_step(nc, d)
    return results(run_bass_kernel_spmd(nc, [arrays], core_ids=[0]).results[0])
```

```python
from contextlib import ExitStack

import numpy as np

import concourse.bass as bass
from concourse import mybir

F32 = mybir.dt.float32
F32R = mybir.dt.float32r
I32 = mybir.dt.int32
ACT = mybir.ActivationFunctionType
ALU = mybir.AluOpType
AX = mybir.AxisListType.X

P = 128
D = 1024
SEQ = 512
DB, DS = 8, 4
NS = DB * DS
T = SEQ + NS
TH = T // 2
DT = D // P
D_FF = 2816
CHUNKS = 2
FT = D_FF // P // CHUNKS
EPS = 1e-6
NEG = -1e30

HD = 64
HEADS = 8
GROUP = 4
WIN = 128
BUCKETS = 32
BLOCKS = SEQ // WIN
SGW = 512
SGT = SGW // P

CT = 4
Q_LORA = 768
QT = Q_LORA // P
KV_LORA = 256
KT = KV_LORA // P
NOPE, ROPE, VD = 64, 32, 64
QK = NOPE + ROPE
PAGES = 16
PAGE = 128
N_POOL = 160
UNIT = 4
UNITS = DB * PAGES // UNIT
UNIT_SLOTS = 13
EARLY_UNITS = 7
KT_SLOTS = 5
AT_MAX, AT_EXP, AT_TURN, AT_TURNED, AT_VALUES, AT_OUT = 3, 4, 12, 13, 14, 15
MLA_SCALE = float(QK) ** -0.5
SWA_SCALE = float(HD) ** -0.5

EVEN_IN = 14
ODD_IN = 3 * CT + QT + KT + 1

FFN_K = ([DT] * (2 * FT) + [FT] * DT) * CHUNKS
EVEN_K = [DT] * EVEN_IN + [DT] * DT
ODD_K = [DT] * ODD_IN + [QT] * HEADS + [DT] * DT
PANEL_K = FFN_K + EVEN_K + FFN_K + FFN_K + ODD_K + FFN_K
N_PANELS = len(PANEL_K)
START = dict(zip(("f0", "even", "f1", "f2", "odd", "f3"),
                 np.cumsum([0] + [len(k) for k in (FFN_K, EVEN_K, FFN_K, FFN_K, ODD_K)]).tolist()))
CONSTS = 4 * 16
N_NORMS = 7


def stat(norm):
    return norm + 1 if norm < 5 else norm + 3


def sumsq_steps(norm):
    return DT * (norm + 1) if norm < 5 else DT * (norm + 1) + QT + KT


def decoder_step(nc, d):
    ctx = ExitStack()
    with ctx:
        base = (nc.sbuf_base + 255) // 256 * 256
        top = [base]

        def at(name, shape, dt, offset):
            return nc.alloc_sbuf_tensor_at(name, shape, dt, offset=offset)

        def size(shape):
            return 4 * int(np.prod(shape[1:]))

        def place(name, shape, dt=F32):
            t = at(name, shape, dt, top[0])
            top[0] += (size(shape) + 31) // 32 * 32
            return t

        def v_ln_at(t):
            return t.manual_sbuf_range[0]

        x = place("x", [P, DT, T])
        region_h = top[0]
        hx_hi = place("hx_hi", [P, DT, T], F32R)
        hx_lo = place("hx_lo", [P, DT, T], F32R)
        end_h = top[0]
        region_hid = top[0]
        hid_hi = place("hid_hi", [P, FT, T], F32R)
        hid_lo = place("hid_lo", [P, FT, T], F32R)
        end_hid = top[0]
        raw = [place(f"raw{s}", [P, FT * P]) for s in range(2)]
        w_hi = [place(f"w_hi{s}", [P, FT * P], F32R) for s in range(2)]
        w_lo = [place(f"w_lo{s}", [P, FT * P], F32R) for s in range(2)]
        gate = place("gate", [P, T])
        silu = place("silu", [P, T])
        up = place("up", [P, T])
        prod = place("prod", [P, T])
        rinv = place("rinv", [P, T])
        rms = place("rms", [P, T])
        square = place("square", [P, T])
        sumsq = place("sumsq", [P, T])
        ident = place("ident", [P, P])
        ones = place("ones", [P, P])
        gains = place("gains", [P, N_NORMS, DT])
        eps = place("eps", [P, 1])
        region_e = top[0]
        end_e = nc.sbuf_usable_end

        def region(start, end):
            cur = [start]

            def put(name, shape, dt=F32):
                t = at(name, shape, dt, cur[0])
                cur[0] += (size(shape) + 31) // 32 * 32
                assert cur[0] <= end, (name, cur[0], end)
                return t
            return put

        put = region(region_hid, end_hid)
        mix_hi = put("mix_hi", [P, DT, T], F32R)
        mix_lo = put("mix_lo", [P, DT, T], F32R)
        spare = region_hid + 2 * size([P, DT, T])

        put = region(spare, end_hid)
        k_cache = put("k_cache", [P, DB, WIN])
        v_cache = put("v_cache", [P, DB, P])
        put = region(region_e, end_e)
        pre = put("pre", [P, EVEN_IN, T])
        bias = put("bias", [P, HEADS, 2 * WIN])
        bias_s = put("bias_s", [P, WIN + DS])
        sgu_w = put("sgu_w", [P, SGT, P])
        sgu_ws = put("sgu_ws", [NS, SGT, NS])
        sgu_b = put("sgu_b", [1, SGT, P])
        sgu_bs = put("sgu_bs", [1, SGT, NS])
        ln_g = put("ln_g", [P, SGW])
        ln_b = put("ln_b", [P, SGW])
        sink = put("sink", [P, HEADS])
        sink_s = put("sink_s", [P, 1])
        smax = put("smax", [P, HEADS])
        nmax = put("nmax", [P, HEADS])
        dsink = put("dsink", [P, HEADS])
        esink = put("esink", [P, HEADS])
        rsum = put("rsum", [P, HEADS])
        rden = put("rden", [P, HEADS])
        ln_st = put("ln_st", [P, 6])
        ln_mv = put("ln_mv", [P, 5, 2])
        ln_sd = put("ln_sd", [P, 5])
        ln_r = put("ln_r", [P, 5])
        v_ln = put("v_ln", [P, 5, SGW])
        put = region(v_ln_at(v_ln), end_e)
        rel = put("rel", [BUCKETS + 1, HEADS])
        onehot = put("onehot", [BUCKETS + 1, 3 * WIN])
        by_dist = put("by_dist", [HEADS, 3 * WIN])
        put = region(region_h, end_h)
        prob = [put(f"prob{s}", [P, HEADS, 2 * WIN]) for s in range(2)]
        prob_t = put("prob_t", [P, 2, HEADS, WIN])
        v_tok = put("v_tok", [P, BLOCKS, P])
        v_new = put("v_new", [DS, DB, P])
        prob_s = put("prob_s", [P, 2, WIN + DS])
        prob_st = put("prob_st", [P, 2, P])
        prob_st2 = put("prob_st2", [DS, 2, P])
        put = region(region_hid, end_hid)
        q_bd = at("q_bd", [P, DB, NS], F32, spare + 2 * size([P, DB, WIN]))

        put = region(spare, end_hid)
        w_uk_t = put("w_uk_t", [NOPE, HEADS, KV_LORA])
        cos = put("cos", [P, T])
        sin = put("sin", [P, T])
        put = region(region_e, end_e)
        cq_hi = put("cq_hi", [P, QT, T], F32R)
        cq_lo = put("cq_lo", [P, QT, T], F32R)
        end_cq = region_e + 2 * size([P, QT, T])
        ckv = put("ckv", [P, KT, T])
        kpe = put("kpe", [P, T])
        conv_z = put("conv_z", [P, CT, SEQ + 2])
        conv_zs = put("conv_zs", [P, CT, DB, DS + 2])
        w_uk = put("w_uk", [P, KT, HEADS * NOPE])
        w_uv = put("w_uv", [P, KT, HEADS * VD])
        perm = put("perm", [P, ROPE])
        conv_w = put("conv_w", [P, 3, CT])
        q_gain = put("q_gain", [P, QT])
        kv_gain = put("kv_gain", [P, KT])
        causal = put("causal", [P, P])
        causal_s = put("causal_s", [P, DS])
        qa = put("qa", [P, 3, DB, NS])
        qa_new = put("qa_new", [P, KT, DB, NS])
        o_lat = put("o_lat", [P, KT, HEADS, NS])
        s_new = put("s_new", [P, DS])
        mx = put("mx", [P, 8])
        nmx = put("nmx", [P, 4])
        sm = put("sm", [P, 8])
        rs = put("rs", [P, 4])
        table = put("table", [1, DB * PAGES], I32)
        put = region(region_h, end_h)
        qf = put("qf", [P, HEADS, T])
        kf = put("kf", [P, HEADS, SEQ])
        put = region(region_e, end_cq)
        v_mla = put("v_mla", [P, BLOCKS, HEADS * VD])
        p_mla = put("p_mla", [P, 10, P])
        p_mla_t = put("p_mla_t", [P, 10, P])
        pages = [put(f"page{s}", [P, KV_LORA + ROPE]) for s in range(6)]
        put = region(conv_z.manual_sbuf_range[0], conv_z.manual_sbuf_range[0] + size([P, CT, SEQ + 2]))
        pages += [put(f"page{s}", [P, KV_LORA + ROPE]) for s in range(6, 13)]
        put = region(gate.manual_sbuf_range[0], ident.manual_sbuf_range[0])
        pages += [put(f"page{s}", [P, KV_LORA + ROPE]) for s in range(13, EARLY_UNITS * UNIT)]
        put = region(region_e, end_cq)
        keys_t = [put(f"keys_t{s}", [QK, 3, PAGE]) for s in range(KT_SLOTS)]
        put = region(p_mla.manual_sbuf_range[0], end_cq)
        p_s = put("p_s", [P, PAGES * PAGE + DS])
        o_tok = put("o_tok", [P, KV_LORA])
        p_st2 = put("p_st2", [DS, 2, NS])
        assert p_st2.manual_sbuf_range[1] <= pages[0].manual_sbuf_range[0]
        put = region(region_h, end_h)
        pages += [put(f"page{s}", [P, KV_LORA + ROPE]) for s in range(EARLY_UNITS * UNIT, UNIT_SLOTS * UNIT)]
        ckv_new = at("ckv_new", [DS, DB, KV_LORA], F32, w_uk_t.manual_sbuf_range[0])
        p_st = [at(f"p_st{s}", [P, PAGES, NS], F32, t.manual_sbuf_range[0]) for s, t in enumerate((cos, sin))]
        y = at("y", [P, DT, T], F32, region_e)

        ps = ctx.enter_context(nc.psum_tensor("ps", [P, 8, 512], F32))
        ps_flat = ps[:].rearrange("p b c -> p (b c)")
        acc = [ps[:, 2 * s:2 * s + 2, :] for s in range(2)]

        def sem(name):
            return ctx.enter_context(nc.semaphore(name))

        raw_landed = [sem(f"raw_landed{s}") for s in range(2)]
        w_hi_done = sem("w_hi_done")
        w_lo_done = sem("w_lo_done")
        panel_done = sem("panel_done")
        acc_read = sem("acc_read")
        consts_landed = sem("consts_landed")
        x_landed = sem("x_landed")
        rel_landed = sem("rel_landed")
        dist_stored = sem("dist_stored")
        even_landed = sem("even_landed")
        cache_landed = sem("cache_landed")
        odd_landed = sem("odd_landed")
        spare_landed = sem("spare_landed")
        table_landed = sem("table_landed")
        pages_landed = [sem(f"pages_landed{s}") for s in range(UNIT_SLOTS)]
        copied = sem("copied")
        stored = sem("stored")
        stored_even = sem("stored_even")
        stored_odd = sem("stored_odd")
        stored_conv = sem("stored_conv")
        hx_hi_done = sem("hx_hi_done")
        hx_done = sem("hx_done")
        square_done = sem("square_done")
        sumsq_step = sem("sumsq_step")
        stat_ready = sem("stat_ready")
        rms_done = sem("rms_done")
        rinv_ready = sem("rinv_ready")
        silu_done = sem("silu_done")
        prod_ready = sem("prod_ready")
        hid_hi_done = sem("hid_hi_done")
        hid_done = sem("hid_done")
        mix_ready = sem("mix_ready")
        mix_hi_done = sem("mix_hi_done")
        mix_done = sem("mix_done")
        step = sem("step")
        dist_ready = sem("dist_ready")
        dist_copied = sem("dist_copied")
        sgu_masked = sem("sgu_masked")
        gelu_done = sem("gelu_done")
        g_turned = sem("g_turned")
        v_ln_read = sem("v_ln_read")
        ln_var = sem("ln_var")
        ln_sd_done = sem("ln_sd_done")
        v_ln_done = sem("v_ln_done")
        gate_sum = sem("gate_sum")
        v_turned = sem("v_turned")
        v_tok_done = sem("v_tok_done")
        swa_scored = sem("swa_scored")
        swa_biased = sem("swa_biased")
        swa_max = sem("swa_max")
        swa_exp = sem("swa_exp")
        swa_prob = sem("swa_prob")
        swa_turned = sem("swa_turned")
        swa_copied = sem("swa_copied")
        swa_out = sem("swa_out")
        q_bd_ready = sem("q_bd_ready")
        cq_hi_done = sem("cq_hi_done")
        cq_done = sem("cq_done")
        ckv_done = sem("ckv_done")
        rotated = sem("rotated")
        q_done = sem("q_done")
        kpe_done = sem("kpe_done")
        kf_ready = sem("kf_ready")
        kf_done = sem("kf_done")
        vm_ready = sem("vm_ready")
        vm_done = sem("vm_done")
        mla_scored = sem("mla_scored")
        mla_max = sem("mla_max")
        mla_exp = sem("mla_exp")
        mla_prob = sem("mla_prob")
        mla_turned = sem("mla_turned")
        mla_copied = sem("mla_copied")
        mla_out = sem("mla_out")
        qa_ready = sem("qa_ready")
        qa_done = sem("qa_done")
        new_turned = sem("new_turned")
        new_copied = sem("new_copied")
        page_turned = sem("page_turned")
        keys_copied = [sem(f"keys_copied{s}") for s in range(2)]
        page_scored = sem("page_scored")
        s_new_ready = sem("s_new_ready")
        s_max = sem("s_max")
        s_exp = sem("s_exp")
        s_turned = sem("s_turned")
        s_copied = sem("s_copied")
        values_done = sem("values_done")
        o_tok_done = sem("o_tok_done")
        o_turned = sem("o_turned")
        s_out = sem("s_out")
        o_lat_done = sem("o_lat_done")
        y_done = sem("y_done")

        def halves(t2d):
            return t2d.rearrange("p (a b) -> p a b", a=2)

        def acc_of(slot, rows=P):
            return acc[slot][0:rows, :, 0:TH]

        def tile_of(t3d, i):
            return t3d[:, bass.ds(i, 1), :].rearrange("p a t -> p (a t)")

        def swa_halves(n):
            return (1,) if n == 0 else (0, 1)

        def swa_units(n):
            return sum(2 * len(swa_halves(b)) for b in range(n))

        FFNS = ((START["f0"], 0, 0), (START["f1"], 1, 2), (START["f2"], 2, 3), (START["f3"], 3, 5))
        S_EVEN, S_ODD = START["even"], START["odd"]
        EVEN_OUT, ODD_UQ = S_EVEN + EVEN_IN, S_ODD + ODD_IN
        ODD_OUT = ODD_UQ + HEADS
        LAST_G, LAST_U = S_EVEN + SGT, S_EVEN + 2 * SGT
        CQ0, CKV0, KPE = S_ODD + 3 * CT, S_ODD + 3 * CT + QT, S_ODD + 3 * CT + QT + KT
        EVEN_PIECES = BLOCKS + SGT + 1
        ODD_PIECES = CT + HEADS + 1
        SGU_PIECE, SWA_PIECE, SWA_S_PIECE = 0, SGT, SGT + BLOCKS
        CONV_PIECE, MLA_PIECE, MLA_S_PIECE = EVEN_PIECES, EVEN_PIECES + CT, EVEN_PIECES + CT + HEADS

        TURN_ORDER = [(j, i) for j in range(BLOCKS) for i in range(j, BLOCKS)]
        EVEN_LOADS = 16 * (1 + 4 + 7 + 4)
        ODD_LOADS = 16 * (8 + CT)

        def panel_cols(n):
            return PANEL_K[n] * (QK if ODD_UQ <= n < ODD_OUT else P)

        def load_pages(eng, u):
            if u == 0 or u == 2:
                eng.wait_ge(table_landed, 16)
                eng.wait_ge(q_done, HEADS)
                eng.wait_ge(stored_conv, 32)
            if u in (EARLY_UNITS, EARLY_UNITS + 1):
                eng.wait_ge(qa_ready, 1)
                eng.wait_ge(qa_done, 1)
            if u >= UNIT_SLOTS:
                eng.wait_ge(values_done, (u - UNIT_SLOTS) * UNIT // PAGES + 1)
            for g in range(UNIT * u, UNIT * (u + 1)):
                page = eng.value_load(table[0:1, g:g + 1], min_val=0, max_val=N_POOL - 1)
                eng.dma_start(pages[g % len(pages)][:], d["page_pool"][bass.ds(page, 1)].rearrange("a p c -> (a p) c"))\
                   .then_inc(pages_landed[u % UNIT_SLOTS], 16)

        block = ctx.enter_context(nc.Block())

        @block.sync
        def _(sp):
            def load_panel(n, slot, cols, src, first=False):
                if not first:
                    sp.wait_ge(w_lo_done, n - 1)
                sp.dma_start(raw[slot][:, 0:cols], src).then_inc(raw_landed[slot], 16)

            def load_ffn(start, gu, down, layer, first=False):
                for c in range(CHUNKS):
                    n0 = start + c * (2 * FT + DT)
                    i0 = 0
                    if first and c == 0:
                        for s in range(2):
                            load_panel(n0 + s, s, DT * P, gu[layer, 0, s], first=True)
                        i0 = 1
                    with sp.Fori(i0, FT) as i:
                        for s in range(2):
                            load_panel(n0 + 2 * i + s, (n0 + s) % 2, DT * P, gu[layer, c * FT + i, s])
                    with sp.Fori(0, DT // 2) as i:
                        for s in range(2):
                            load_panel(n0 + 2 * FT + 2 * i + s, (n0 + s) % 2, FT * P, down[layer, c, 2 * i + s])

            def load_matrix(start, w, first=0, end=None):
                for t in range(first, w.shape[0] if end is None else end):
                    load_panel(start + t, (start + t) % 2, panel_cols(start + t), w[t])

            sp.dma_start(x[:], d["xT"]).then_inc(x_landed, 16)
            load_ffn(START["f0"], d["gu1"], d["down1"], 0, first=True)
            load_matrix(S_EVEN, d["even_in"])
            sp.dma_start(d["o_kc"], d["k_nat"][:, DS:WIN]).then_inc(copied, 16)
            sp.dma_start(d["o_vc"], d["v_nat"][:, DS:WIN]).then_inc(copied, 16)
            load_matrix(EVEN_OUT, d["even_out"])
            load_ffn(START["f1"], d["gu2"], d["down2"], 0)
            load_ffn(START["f2"], d["gu1"], d["down1"], 1)
            load_matrix(S_ODD, d["odd_in"])
            load_matrix(ODD_UQ, d["w_uq"])
            load_matrix(ODD_OUT, d["odd_out"], 0, 2)

            for u in range(UNITS):
                if u % UNIT_SLOTS % 3 != 2:
                    load_pages(sp, u)
            load_matrix(ODD_OUT, d["odd_out"], 2)
            load_ffn(START["f3"], d["gu2"], d["down2"], 1)
            for t in range(DT):
                sp.wait_ge(y_done, t + 1)
                sp.dma_start(d["o_y"][:, t, :], y[:, t, :]).then_inc(stored, 16)
            sp.wait_ge(stored, 16 * DT)
            sp.wait_ge(copied, 32)
            sp.wait_ge(stored_even, 16 * 5)
            sp.wait_ge(stored_conv, 16 * 2)
            sp.wait_ge(stored_odd, 16 * 2)

        @block.tensor
        def _(pe):
            def panel(n, slot, rhs_hi, rhs_lo, k, wait_input=None, m=P):
                pe.wait_ge(w_lo_done, n + 1)
                if not (isinstance(n, int) and n < 2):
                    pe.wait_ge(acc_read, n - 1)
                for t in range(k):
                    if wait_input is not None:
                        wait_input(t)
                    hi, lo = w_hi[slot][:, t * m:(t + 1) * m], w_lo[slot][:, t * m:(t + 1) * m]
                    for w, r, one in ((hi, rhs_hi, 0), (hi, rhs_lo, 1), (lo, rhs_hi, 2)):
                        for a in range(2):
                            last = pe.matmul(acc[slot][0:m, a, 0:TH], w, r[:, t, a * TH:(a + 1) * TH],
                                             start=(t == 0 and one == 0), stop=(t == k - 1 and one == 2))
                last.then_inc(panel_done, 1)

            def stats(steps):
                pe.wait_ge(sumsq_step, steps)
                for a in range(2):
                    last = pe.matmul(ps[:, 4 + a, 0:TH], ones[:], sumsq[:, a * TH:(a + 1) * TH], start=True, stop=True)
                last.then_inc(stat_ready, 1)

            def ffn(start, f, norm):
                for c in range(CHUNKS):
                    n0 = start + c * (2 * FT + DT)
                    done = (f * CHUNKS + c) * FT
                    i0 = 0
                    if c == 0:
                        def split_input(t):
                            pe.wait_ge(hx_done, DT * norm + t + 1)
                        panel(n0, n0 % 2, hx_hi, hx_lo, DT, split_input)
                        stats(sumsq_steps(norm))
                        panel(n0 + 1, (n0 + 1) % 2, hx_hi, hx_lo, DT)
                        i0 = 1
                    with pe.Fori(i0, FT) as i:
                        for s in range(2):
                            panel(n0 + 2 * i + s, (n0 + s) % 2, hx_hi, hx_lo, DT)
                    n1 = n0 + 2 * FT

                    def hidden(t):
                        pe.wait_ge(hid_done, done + t + 1)
                    panel(n1, n1 % 2, hid_hi, hid_lo, FT, hidden)
                    panel(n1 + 1, (n1 + 1) % 2, hid_hi, hid_lo, FT)
                    with pe.Fori(1, DT // 2) as i:
                        for s in range(2):
                            panel(n1 + 2 * i + s, (n1 + s) % 2, hid_hi, hid_lo, FT)

            def mixer_out(start, pieces):
                pe.wait_ge(mix_done, pieces)
                for t in range(DT):
                    panel(start + t, (start + t) % 2, mix_hi, mix_lo, DT)

            def by_distance():
                pe.wait_ge(rel_landed, 32)
                pe.matmul(ps[0:HEADS, 7, 0:3 * WIN], rel[:], onehot[:], start=True, stop=True).then_inc(dist_ready, 1)

            def turn_g(tt):
                rows = P if tt < BLOCKS else NS
                if tt == 0:
                    pe.wait_ge(gelu_done, SGT)
                    pe.wait_ge(rms_done, stat(1))
                if tt >= 4:
                    pe.wait_ge(v_ln_read, tt - 3)
                for g in range(SGT):
                    last = pe.transpose(ps[0:rows, 4 + tt % 4, g * P:(g + 1) * P], pre[:, g, tt * P:tt * P + rows], ident[:])
                last.then_inc(g_turned, 1)

            def gate_matmul(g):
                b0 = 4 + 2 * (g % 2)
                if g == 0:
                    pe.wait_ge(v_ln_done, 5)
                    pe.wait_ge(sgu_masked, 2)
                if g >= 2:
                    pe.wait_ge(mix_ready, SGU_PIECE + g - 1)
                for c in range(BLOCKS):
                    out = ps[:, b0, c * P:(c + 1) * P]
                    pe.matmul(out, ones[0:1, :], sgu_b[:, g, :], start=True, stop=False)
                    pe.matmul(out, v_ln[:, c, g * P:(g + 1) * P], sgu_w[:, g, :], start=False, stop=True)
                out = ps[:, b0 + 1, 0:NS]
                pe.matmul(out, ones[0:1, :], sgu_bs[:, g, :], start=True, stop=False)
                pe.matmul(out, v_ln[0:NS, 4, g * P:(g + 1) * P], sgu_ws[:, g, :], start=False, stop=True)\
                  .then_inc(gate_sum, 1)

            def turn_v():
                pe.wait_ge(acc_read, EVEN_OUT)
                pe.wait_ge(mix_ready, SGU_PIECE + SGT)
                for n in range(BLOCKS):
                    pe.transpose(ps[:, 4, n * P:(n + 1) * P], pre[:, 13, n * P:(n + 1) * P], ident[:])
                for b in range(DB):
                    last = pe.transpose(ps[0:DS, 5 + b // 4, (b % 4) * P:(b % 4 + 1) * P],
                                        pre[:, 13, SEQ + b * DS:SEQ + (b + 1) * DS], ident[:])
                last.then_inc(v_turned, 1)

            def swa_score(n):
                if n == 0:
                    pe.wait_ge(acc_read, EVEN_OUT)
                if n:
                    pe.wait_ge(swa_biased, n)
                k0 = swa_halves(n)[0]
                for h in range(HEADS):
                    r = HD * (h // GROUP)
                    last = pe.matmul(ps_flat[:, h * 2 * WIN + k0 * WIN:(h + 1) * 2 * WIN],
                                     pre[r:r + HD, 8 + h % GROUP, n * WIN:(n + 1) * WIN],
                                     pre[r:r + HD, 12, (n - 1 + k0) * WIN:(n + 1) * WIN], start=True, stop=True)
                last.then_inc(swa_scored, 1)

            def swa_values(n):
                pe.wait_ge(swa_prob, n + 1)
                if n == 0:
                    pe.wait_ge(v_tok_done, 2)
                u = swa_units(n)
                for kv in range(2):
                    for j in swa_halves(n):
                        if u >= 3:
                            pe.wait_ge(swa_copied, u - 2)
                        for hh in range(GROUP):
                            last = pe.transpose(ps[:, 4 + u % 3, hh * WIN:(hh + 1) * WIN],
                                                prob[n % 2][:, kv * GROUP + hh, j * WIN:(j + 1) * WIN], ident[:])
                        last.then_inc(swa_turned, 1)
                        u += 1
                if n:
                    pe.wait_ge(mix_done, SWA_PIECE + n)
                u = swa_units(n)
                for kv in range(2):
                    for j in swa_halves(n):
                        u += 1
                        pe.wait_ge(swa_copied, u)
                        last = pe.matmul(ps[kv * HD:(kv + 1) * HD, 7, :], v_tok[:, n - 1 + j, kv * HD:(kv + 1) * HD],
                                         prob_t[:, j, kv * GROUP:(kv + 1) * GROUP, :], start=(j == swa_halves(n)[0]), stop=(j == 1))
                last.then_inc(swa_out, 1)

            def swa_sample_score():
                pe.wait_ge(swa_biased, BLOCKS)
                pe.wait_ge(q_bd_ready, 1)
                pe.wait_ge(cache_landed, 32)
                for b in range(DB):
                    r = NS * (b % 4)
                    pe.matmul(ps[r:r + NS, b // 4, 0:WIN], q_bd[:, b, :], k_cache[:, b, :], start=True, stop=True)
                    last = pe.matmul(ps[r:r + NS, b // 4, WIN:WIN + DS], q_bd[:, b, :],
                                     pre[:, 12, SEQ + b * DS:SEQ + (b + 1) * DS], start=True, stop=True)
                last.then_inc(swa_scored, 1)

            def swa_sample_values():
                pe.wait_ge(swa_prob, BLOCKS + 1)
                pe.wait_ge(swa_copied, swa_units(BLOCKS))
                for g in range(2):
                    pe.transpose(ps[:, 4, g * P:(g + 1) * P], prob_s[:, g, 0:WIN], ident[:])
                    last = pe.transpose(ps[0:DS, 5, g * P:(g + 1) * P], prob_s[:, g, WIN:WIN + DS], ident[:])
                last.then_inc(swa_turned, 1)
                pe.wait_ge(swa_copied, swa_units(BLOCKS) + 2)
                pe.wait_ge(mix_done, SWA_PIECE + BLOCKS)
                for b in range(DB):
                    r = NS * (b % 4)
                    pe.matmul(ps[:, 7, b * NS:(b + 1) * NS], v_cache[:, b, :], prob_st[:, b // 4, r:r + NS],
                              start=True, stop=False)
                    last = pe.matmul(ps[:, 7, b * NS:(b + 1) * NS], v_new[:, b, :], prob_st2[:, b // 4, r:r + NS],
                                     start=False, stop=True)
                last.then_inc(swa_out, 1)

            def even():
                def split_input(t):
                    pe.wait_ge(hx_done, DT + t + 1)
                for t in range(EVEN_IN):
                    n = S_EVEN + t
                    panel(n, n % 2, hx_hi, hx_lo, DT, split_input if t == 0 else None)
                    if t == 0:
                        stats(sumsq_steps(1))
                        pe.wait_ge(even_landed, EVEN_LOADS)
                    if SGT + 1 <= t <= SGT + 5:
                        turn_g(t - SGT - 1)
                swa_score(0)
                for g in range(SGT):
                    gate_matmul(g)
                turn_v()
                for n in range(BLOCKS):
                    if n + 1 < BLOCKS:
                        swa_score(n + 1)
                    else:
                        swa_sample_score()
                    swa_values(n)
                swa_sample_values()
                mixer_out(EVEN_OUT, EVEN_PIECES)

            def rotate(src, h):
                for a in range(2):
                    last = pe.matmul(ps[NOPE:QK, 6 + a, 0:TH], perm[NOPE:QK, :], src[NOPE:QK, a * TH:(a + 1) * TH],
                                     start=True, stop=True)
                last.then_inc(rotated, 1)

            def nope_keys(h):
                if h >= 2:
                    pe.wait_ge(kf_done, h)
                for c in range(KT):
                    last = pe.matmul(ps[0:NOPE, 4 + h % 2, :], w_uk[:, c, h * NOPE:(h + 1) * NOPE], ckv[:, c, 0:SEQ],
                                     start=(c == 0), stop=(c == KT - 1))
                last.then_inc(kf_ready, 1)

            def mla_values_of(j):
                if j == 0:
                    pe.wait_ge(q_done, HEADS)
                if j >= 2:
                    pe.wait_ge(vm_done, j - 1)
                for c in range(KT):
                    last = pe.matmul(ps[:, 6 + j % 2, :], ckv[:, c, j * P:(j + 1) * P], w_uv[:, c, :],
                                     start=(c == 0), stop=(c == KT - 1))
                last.then_inc(vm_ready, 1)

            def mla_score(h):
                if h == 0:
                    pe.wait_ge(kf_done, HEADS + 1)
                    pe.wait_ge(q_done, HEADS)
                else:
                    pe.wait_ge(mla_exp, h)
                for i in range(BLOCKS):
                    last = pe.matmul(ps[:, i, 0:(i + 1) * P], qf[0:QK, h, i * P:(i + 1) * P], kf[0:QK, h, 0:(i + 1) * P],
                                     start=True, stop=True)
                last.then_inc(mla_scored, 1)

            def mla_values(h):
                pe.wait_ge(mla_prob, h + 1)
                if h:
                    pe.wait_ge(mla_copied, h)
                else:
                    pe.wait_ge(vm_done, BLOCKS)
                for s, (j, i) in enumerate(TURN_ORDER):
                    last = pe.transpose(ps[:, 4 + s // 4, (s % 4) * P:(s % 4 + 1) * P], p_mla[:, i * (i + 1) // 2 + j, :], ident[:])
                last.then_inc(mla_turned, 1)
                pe.wait_ge(mla_copied, h + 1)
                if h >= 2:
                    pe.wait_ge(mix_done, MLA_PIECE + h - 1)
                r = VD * (h % 2)
                for j in range(BLOCKS):
                    s = TURN_ORDER.index((j, j))
                    last = pe.matmul(ps[r:r + VD, 7, j * P:SEQ], v_mla[:, j, h * VD:(h + 1) * VD], p_mla_t[:, s:s + BLOCKS - j, :],
                                     start=(j == 0), stop=(j == BLOCKS - 1))
                last.then_inc(mla_out, 1)

            def absorb():
                pe.wait_ge(mla_copied, HEADS)
                for h in range(HEADS):
                    q_h = qf[0:NOPE, h, SEQ:T]
                    for j in range(2):
                        pe.matmul(ps[0:QK, 4, (j * HEADS + h) * NS:(j * HEADS + h + 1) * NS], w_uk_t[:, h, j * QK:(j + 1) * QK], q_h,
                                  start=True, stop=True)
                    pe.matmul(ps[0:NOPE, 5, h * NS:(h + 1) * NS], w_uk_t[:, h, 2 * QK:KV_LORA], q_h, start=True, stop=True)
                    for c in range(KT):
                        last = pe.matmul(ps[:, 6, (c * HEADS + h) * NS:(c * HEADS + h + 1) * NS], w_uk_t[:, h, c * P:(c + 1) * P], q_h,
                                         start=True, stop=True)
                last.then_inc(qa_ready, 1)

            def turn_new():
                pe.wait_ge(qa_done, 1)
                pe.wait_ge(mix_done, MLA_PIECE + HEADS)
                for b in range(DB):
                    for c in range(KT):
                        s = b * KT + c
                        last = pe.transpose(ps[0:DS, 4 + s // 4, (s % 4) * P:(s % 4 + 1) * P],
                                            ckv[:, c, SEQ + b * DS:SEQ + (b + 1) * DS], ident[:])
                last.then_inc(new_turned, 1)

            def turn_page(g):
                u = g // UNIT
                if g % UNIT == 0:
                    pe.wait_ge(pages_landed[u % UNIT_SLOTS], 16 * UNIT * (u // UNIT_SLOTS + 1))
                if g < 2:
                    pe.wait_ge(new_copied, 1)
                else:
                    pe.wait_ge(keys_copied[g % 2], g // 2)
                for j in range(3):
                    last = pe.transpose(ps[0:QK, 4 + g % 2, j * PAGE:(j + 1) * PAGE], pages[g % len(pages)][:, j * QK:(j + 1) * QK], ident[:])
                last.then_inc(page_turned, 1)

            def score_page(g):
                b, p = g // PAGES, g % PAGES
                r = NS * (b % 4)
                pe.wait_ge(keys_copied[g % 2], g // 2 + 1)
                if g == 0:
                    pe.wait_ge(mla_exp, HEADS)
                if p == 0 and b >= 4:
                    pe.wait_ge(s_exp, b - 3)
                for j in range(3):
                    last = pe.matmul(ps_flat[r:r + NS, p * PAGE:(p + 1) * PAGE], qa[0:QK, j, b, :], keys_t[g % KT_SLOTS][:, j, :],
                                     start=(j == 0), stop=(j == 2))
                last.then_inc(page_scored, 1)

            def score_new(b):
                r = NS * (b % 4)
                if b >= 4:
                    pe.wait_ge(o_tok_done, b - 3)
                new = ps[r:r + NS, 7, KV_LORA:KV_LORA + DS]
                for c in range(KT):
                    pe.matmul(new, qa_new[:, c, b, :], ckv[:, c, SEQ + b * DS:SEQ + (b + 1) * DS], start=(c == 0), stop=False)
                pe.matmul(new, qa[NOPE:QK, 2, b, :], kpe[NOPE:QK, SEQ + b * DS:SEQ + (b + 1) * DS], start=False, stop=True)\
                  .then_inc(s_new_ready, 1)

            def turn_probs(b):
                r = NS * (b % 4)
                pe.wait_ge(s_exp, b + 1)
                if b:
                    pe.wait_ge(s_copied, b)
                    pe.wait_ge(o_tok_done, b)
                if b == 5:
                    pe.wait_ge(o_lat_done, 1)
                one = ident[r:r + NS, r:r + NS]
                for p in range(PAGES):
                    pe.transpose(ps[:, 6, p * NS:(p + 1) * NS], p_s[r:r + NS, p * PAGE:(p + 1) * PAGE], one)
                pe.transpose(ps[0:DS, 7, KV_LORA + NS:KV_LORA + 2 * NS], p_s[r:r + NS, PAGES * PAGE:PAGES * PAGE + DS], one)\
                  .then_inc(s_turned, 1)

            def page_values(b):
                r = NS * (b % 4)
                pe.wait_ge(s_copied, b + 1)
                out = ps[r:r + NS, 7, 0:KV_LORA]
                for p in range(PAGES):
                    pe.matmul(out, p_st[b % 2][:, p, :], pages[(b * PAGES + p) % len(pages)][:, 0:KV_LORA], start=(p == 0), stop=False)
                pe.matmul(out, p_st2[:, b % 2, :], ckv_new[:, b, :], start=False, stop=True).then_inc(values_done, 1)

            def turn_latents(g):
                pe.wait_ge(o_tok_done, 4 * g + 4)
                for c in range(KT):
                    last = pe.transpose(ps[:, 6, c * P:(c + 1) * P], o_tok[:, c * P:(c + 1) * P], ident[:])
                last.then_inc(o_turned, 1)

            def sample():
                for b in range(DB + 1):
                    for p in range(PAGES):
                        g = b * PAGES + p
                        if b < DB:
                            turn_page(g)
                        if 2 <= g < DB * PAGES + 2:
                            score_page(g - 2)
                        if b and p == 1:
                            score_new(b - 1)
                        if b and p == AT_TURN:
                            turn_probs(b - 1)
                        if b and p == AT_VALUES:
                            page_values(b - 1)
                        if b == 5 and p == 0:
                            turn_latents(0)
                turn_latents(1)

            def sample_out():
                pe.wait_ge(o_lat_done, 2)
                for h in range(HEADS):
                    r = VD * (h % 2)
                    for c in range(KT):
                        last = pe.matmul(ps[r:r + VD, 4, (h // 2) * NS:(h // 2 + 1) * NS], w_uv[:, c, h * VD:(h + 1) * VD], o_lat[:, c, h, :],
                                         start=(c == 0), stop=(c == KT - 1))
                last.then_inc(s_out, 1)

            def odd():
                def split_input(t):
                    pe.wait_ge(hx_done, 4 * DT + t + 1)
                for t in range(ODD_IN):
                    n = S_ODD + t
                    panel(n, n % 2, hx_hi, hx_lo, DT, split_input if t == 0 else None)
                    if t == 0:
                        stats(sumsq_steps(4))
                    if n == CKV0 + 1:
                        pe.wait_ge(rms_done, stat(4))
                        stats(DT * 5 + QT)
                for h in range(HEADS):
                    n = ODD_UQ + h

                    def split_cq(t):
                        pe.wait_ge(cq_done, t + 1)
                    panel(n, n % 2, cq_hi, cq_lo, QT, split_cq if h == 0 else None, m=QK)
                    if h == 0:
                        pe.wait_ge(rms_done, stat(4) + 1)
                        stats(DT * 5 + QT + KT)
                        pe.wait_ge(spare_landed, 48)
                        pe.wait_ge(acc_read, KPE + 1)
                        rotate(kpe, 0)
                    else:
                        pe.wait_ge(acc_read, n)
                        if h == 1:
                            pe.wait_ge(kpe_done, 1)
                        else:
                            pe.wait_ge(q_done, h - 1)
                        rotate(qf[:, h - 1, :], h)
                pe.wait_ge(acc_read, ODD_OUT)
                pe.wait_ge(q_done, HEADS - 1)
                rotate(qf[:, HEADS - 1, :], HEADS)
                pe.wait_ge(ckv_done, KT)
                for h in range(HEADS):
                    nope_keys(h)
                for j in range(BLOCKS):
                    mla_values_of(j)
                mla_score(0)
                for h in range(HEADS):
                    if h + 1 < HEADS:
                        mla_score(h + 1)
                    mla_values(h)
                absorb()
                turn_new()
                sample()
                sample_out()
                mixer_out(ODD_OUT, EVEN_PIECES + ODD_PIECES)

            by_distance()
            pe.wait_ge(consts_landed, CONSTS)
            ffn(*FFNS[0])
            even()
            ffn(*FFNS[1])
            ffn(*FFNS[2])
            odd()
            ffn(*FFNS[3])
            stats(sumsq_steps(6))

        @block.scalar
        def _(act):
            def split_hi(n, slot, cols):
                act.wait_ge(raw_landed[slot], 8 * (n - slot) + 16)
                if not (isinstance(n, int) and n < 2):
                    act.wait_ge(panel_done, n - 1)
                act.activation(w_hi[slot][:, 0:cols], raw[slot][:, 0:cols], ACT.Copy).then_inc(w_hi_done, 1)

            def split_next(n):
                if n + 2 < N_PANELS:
                    split_hi(n + 2, n % 2, panel_cols(n + 2))

            def root(k, terms):
                act.wait_ge(stat_ready, k)
                if k > 1:
                    act.wait_ge(rinv_ready, k - 1)
                act.activation(halves(rms[:]), ps[:, 4:6, 0:TH], ACT.Sqrt, scale=1.0 / terms, bias=eps[:, 0:1])\
                   .then_inc(rms_done, 1)

            def input_hi(norm, m):
                act.activation(tile_of(hx_hi, m), tile_of(x, m), ACT.Copy, scale=gains[:, norm, bass.ds(m, 1)])\
                   .then_inc(hx_hi_done, 1)

            def ffn(start, f, norm):
                for c in range(CHUNKS):
                    n0 = start + c * (2 * FT + DT)
                    h0 = (f * CHUNKS + c) * FT

                    def tile(i, cols):
                        split_hi(n0 + 2 * i + 2, n0 % 2, cols)
                        act.wait_ge(acc_read, n0 + 2 * i + 1)
                        act.activation(silu[:], gate[:], ACT.Silu).then_inc(silu_done, 1)
                        split_hi(n0 + 2 * i + 3, (n0 + 1) % 2, cols)
                        act.wait_ge(prod_ready, h0 + i + 1)
                        act.activation(tile_of(hid_hi, i), prod[:], ACT.Copy).then_inc(hid_hi_done, 1)
                    if c == 0:
                        root(stat(norm), D)
                    with act.Fori(0, FT - 1) as i:
                        tile(i, DT * P)
                    tile(FT - 1, FT * P)
                    n1 = n0 + 2 * FT

                    def final_input(m):
                        if c == CHUNKS - 1 and norm + 1 < N_NORMS - 1:
                            act.wait_ge(acc_read, n1 + m + 1)
                            input_hi(norm + 1, m)
                    with act.Fori(0, DT // 2 - 1) as i:
                        for s in range(2):
                            split_hi(n1 + 2 * i + s + 2, (n1 + s) % 2, FT * P)
                            final_input(2 * i + s)
                    for m in (DT - 2, DT - 1):
                        split_next(n1 + m)
                        final_input(m)

            def mixer_out(start, norm):
                for m in range(DT):
                    split_next(start + m)
                    act.wait_ge(acc_read, start + m + 1)
                    input_hi(norm + 1, m)

            def mix_upper(out, src, ready, count):
                act.wait_ge(ready, count)
                act.activation(out, src, ACT.Copy).then_inc(mix_hi_done, 1)

            def swa_exps(n):
                act.wait_ge(swa_max, n + 1)
                lo = swa_halves(n)[0] * WIN
                for h in range(HEADS):
                    act.activation(prob[n % 2][:, h, lo:2 * WIN], prob[n % 2][:, h, lo:2 * WIN], ACT.Exp,
                                   bias=nmax[:, h:h + 1], accum_out=rsum[:, h:h + 1])
                act.activation(esink[:], dsink[:], ACT.Exp).then_inc(swa_exp, 1)

            def swa_copies(n):
                u = swa_units(n)
                if n:
                    act.wait_ge(swa_out, n)
                for kv in range(2):
                    for j in swa_halves(n):
                        act.wait_ge(swa_turned, u + 1)
                        act.activation(prob_t[:, j, kv * GROUP:(kv + 1) * GROUP, :].rearrange("p h q -> p (h q)"), ps[:, 4 + u % 3, :], ACT.Copy)\
                           .then_inc(swa_copied, 1)
                        u += 1

            def swa_upper(n):
                mix_upper(mix_hi[:, 0:GROUP, n * WIN:(n + 1) * WIN],
                          ps[:, 7, :].rearrange("p (h q) -> p h q", h=GROUP), swa_out, n + 1)

            def even():
                for t in range(EVEN_IN):
                    n = S_EVEN + t
                    if t == 0:
                        root(stat(1), D)
                    split_next(n)
                    if t < 2 * SGT:
                        act.wait_ge(acc_read, n + 1)
                        act.activation(pre[:, t, :], pre[:, t, :], ACT.Gelu).then_inc(gelu_done, 1)
                    if t == SGT + 6:
                        act.wait_ge(ln_var, 1)
                        act.activation(ln_sd[:, 0:4], ln_mv[:, 0:4, 1], ACT.Sqrt, bias=eps[:, 0:1])
                        act.activation(ln_sd[0:NS, 4:5], ln_mv[0:NS, 4, 1:2], ACT.Sqrt, bias=eps[0:NS, 0:1]).then_inc(ln_sd_done, 1)
                swa_exps(0)
                for g in range(SGT):
                    mix_upper(mix_hi[:, GROUP + g, :], (up if g % 2 else prod)[:], mix_ready, g + 1)
                act.wait_ge(v_turned, 1)
                act.activation(v_tok[:].rearrange("p n c -> p (n c)"), ps[:, 4, :], ACT.Copy).then_inc(v_tok_done, 1)
                act.activation(v_new[:].rearrange("p (a b) c -> p a (b c)", a=2), ps[0:DS, 5:7, :], ACT.Copy).then_inc(v_tok_done, 1)
                for n in range(BLOCKS):
                    swa_copies(n)
                    if n + 1 < BLOCKS:
                        swa_exps(n + 1)
                    else:
                        act.wait_ge(swa_max, BLOCKS + 1)
                        for g in range(2):
                            act.activation(prob_s[:, g, :], prob_s[:, g, :], ACT.Exp, bias=nmax[:, g:g + 1], accum_out=rsum[:, g:g + 1])
                        act.activation(esink[:, 0:2], dsink[:, 0:2], ACT.Exp).then_inc(swa_exp, 1)
                    swa_upper(n)
                act.wait_ge(swa_turned, swa_units(BLOCKS) + 1)
                act.activation(prob_st[:].rearrange("p g r -> p (g r)"), ps[:, 4, 0:2 * P], ACT.Copy).then_inc(swa_copied, 1)
                act.activation(prob_st2[:].rearrange("p g r -> p (g r)"), ps[0:DS, 5, 0:2 * P], ACT.Copy).then_inc(swa_copied, 1)
                act.wait_ge(swa_out, BLOCKS + 1)
                for kv in range(2):
                    r = kv * HD
                    last = act.activation(mix_hi[r:r + HD, 0:GROUP, SEQ:T].rearrange("p h (b t) -> p b h t", b=DB),
                                          ps[r:r + HD, 7, 0:DB * NS].rearrange("p (b g h t) -> p b g h t", b=DB, g=2, h=GROUP)[:, :, kv],
                                          ACT.Copy)
                last.then_inc(mix_hi_done, 1)
                mixer_out(EVEN_OUT, 1)

            def odd():
                for t in range(ODD_IN):
                    n = S_ODD + t
                    if t == 0:
                        root(stat(4), D)
                    split_next(n)
                    if t < 3 * CT and t % 3 == 2:
                        mix_upper(mix_hi[:, t // 3, :], prod[:], mix_ready, SGT + t // 3 + 1)
                    if CQ0 <= n < CKV0:
                        c = n - CQ0
                        act.wait_ge(acc_read, n + 1)
                        act.activation(cq_hi[:, c, :], (prod if c % 2 else silu)[:], ACT.Copy, scale=q_gain[:, c:c + 1]).then_inc(cq_hi_done, 1)
                    if n == KPE:
                        root(stat(4) + 1, Q_LORA)
                for h in range(HEADS):
                    split_next(ODD_UQ + h)
                    if h == 0:
                        root(stat(4) + 2, KV_LORA)
                    if h == 1:
                        act.wait_ge(kpe_done, 1)
                        for hh in range(HEADS):
                            last = act.activation(kf[NOPE:QK, hh, :], kpe[NOPE:QK, 0:SEQ], ACT.Copy)
                        last.then_inc(kf_done, 1)
                for h in range(HEADS):
                    act.wait_ge(kf_ready, h + 1)
                    act.activation(kf[0:NOPE, h, :], ps[0:NOPE, 4 + h % 2, :], ACT.Copy).then_inc(kf_done, 1)
                for j in range(BLOCKS):
                    act.wait_ge(vm_ready, j + 1)
                    act.activation(v_mla[:, j, :], ps[:, 6 + j % 2, :], ACT.Copy).then_inc(vm_done, 1)

                def exps(h):
                    act.wait_ge(mla_max, h + 1)
                    if h:
                        act.wait_ge(mla_turned, h)
                    for i in range(BLOCKS):
                        s = i * (i + 1) // 2
                        last = act.activation(p_mla[:, s:s + i + 1, :].rearrange("p j k -> p (j k)"), ps[:, i, 0:(i + 1) * P], ACT.Exp,
                                              bias=nmx[:, i:i + 1], scale=MLA_SCALE, accum_out=sm[:, i:i + 1])
                    last.then_inc(mla_exp, 1)
                exps(0)
                for h in range(HEADS):
                    act.wait_ge(mla_turned, h + 1)
                    if h:
                        act.wait_ge(mla_out, h)
                    flat = p_mla_t[:].rearrange("p s q -> p (s q)")
                    last = act.activation(flat, ps_flat[:, 4 * 512:4 * 512 + 10 * P], ACT.Copy)
                    last.then_inc(mla_copied, 1)
                    if h + 1 < HEADS:
                        exps(h + 1)
                    r = VD * (h % 2)
                    mix_upper(mix_hi[r:r + VD, CT + h // 2, 0:SEQ], ps[r:r + VD, 7, :], mla_out, h + 1)
                act.wait_ge(new_turned, 1)
                act.activation(ckv_new[:].rearrange("p b c -> p (b c)"), ps_flat[0:DS, 4 * 512:8 * 512], ACT.Copy).then_inc(new_copied, 1)

                for b in range(DB + 1):
                    r = NS * ((b - 1) % 4)
                    for p in range(PAGES):
                        g = b * PAGES + p
                        if b < DB and p % 2:
                            act.wait_ge(page_turned, g + 1)
                            if g >= KT_SLOTS:
                                act.wait_ge(page_scored, g - KT_SLOTS + 1)
                            act.activation(keys_t[g % KT_SLOTS][:].rearrange("p j k -> p (j k)"), ps[0:QK, 5, 0:3 * PAGE], ACT.Copy)\
                               .then_inc(keys_copied[1], 1)
                        if b and p == AT_EXP:
                            act.wait_ge(s_max, b)
                        if b and AT_EXP <= p < AT_EXP + 8 and p % 2 == 0:
                            q = (p - AT_EXP) // 2
                            act.activation(p_s[r:r + NS, q * 4 * PAGE:(q + 1) * 4 * PAGE], ps[r:r + NS, q, :], ACT.Exp,
                                           bias=nmx[r:r + NS, 3:4], scale=MLA_SCALE, accum_out=sm[r:r + NS, q:q + 1])
                        if b and p == AT_EXP + 6:
                            act.activation(p_s[r:r + NS, PAGES * PAGE:PAGES * PAGE + DS], s_new[r:r + NS, :], ACT.Exp,
                                           bias=nmx[r:r + NS, 3:4], scale=MLA_SCALE, accum_out=sm[r:r + NS, 4:5]).then_inc(s_exp, 1)
                        if b and p == AT_TURNED:
                            act.wait_ge(s_turned, b)
                            if b >= 3:
                                act.wait_ge(values_done, b - 2)
                            act.activation(p_st2[:, (b - 1) % 2, :], ps[0:DS, 7, KV_LORA + NS:KV_LORA + 2 * NS], ACT.Copy)
                            act.activation(p_st[(b - 1) % 2][:].rearrange("p j r -> p (j r)"), ps[:, 6, :], ACT.Copy).then_inc(s_copied, 1)
                mix_upper(mix_hi[:, CT:2 * CT, SEQ:T], ps[:, 4, 0:CT * NS].rearrange("p (h t) -> p h t", h=CT), s_out, 1)
                mixer_out(ODD_OUT, 4)

            act.wait_ge(consts_landed, CONSTS)
            act.wait_ge(x_landed, 16)
            for t in range(DT):
                input_hi(0, t)
            split_hi(0, 0, DT * P)
            split_hi(1, 1, DT * P)
            ffn(*FFNS[0])
            even()
            ffn(*FFNS[1])
            ffn(*FFNS[2])
            odd()
            ffn(*FFNS[3])
            root(stat(6), D)

        @block.vector
        def _(dve):
            steps = [0]

            def link(ins):
                steps[0] += 1
                ins.then_inc(step, 1)
                dve.wait_ge(step, steps[0])

            def split_lo(n, slot, cols):
                dve.wait_ge(w_hi_done, n + 1)
                dve.tensor_tensor(w_lo[slot][:, 0:cols], raw[slot][:, 0:cols], w_hi[slot][:, 0:cols].bitcast(F32),
                                  ALU.subtract).then_inc(w_lo_done, 1)

            def split_next(n):
                if n + 2 < N_PANELS:
                    split_lo(n + 2, n % 2, panel_cols(n + 2))

            def invert(k, out=None):
                dve.wait_ge(rms_done, k)
                dve.reciprocal((rinv if out is None else out)[:], rms[:]).then_inc(rinv_ready, 1)
                dve.wait_ge(rinv_ready, k)

            def scaled(n, out, by, rows=P):
                dve.wait_ge(panel_done, n + 1)
                dve.tensor_tensor(halves(out), acc_of(n % 2, rows), halves(by), ALU.mult).then_inc(acc_read, 1)

            def input_lo(norm, m):
                dve.wait_ge(hx_hi_done, DT * norm + m + 1)
                dve.scalar_tensor_tensor(out=tile_of(hx_lo, m), in0=tile_of(x, m), scalar=gains[:, norm, bass.ds(m, 1)],
                                         in1=tile_of(hx_hi, m).bitcast(F32), op0=ALU.mult, op1=ALU.subtract).then_inc(hx_done, 1)

            def add_to_x(n, slot, m, factor):
                dve.wait_ge(panel_done, n + 1)
                xm = halves(tile_of(x, m))
                dve.scalar_tensor_tensor(out=xm, in0=acc_of(slot), scalar=factor, in1=xm, op0=ALU.mult, op1=ALU.add)\
                   .then_inc(acc_read, 1)

            def mix_lower(piece, out, src, hi):
                dve.wait_ge(mix_hi_done, piece + 1)
                dve.tensor_tensor(out, src, hi.bitcast(F32), ALU.subtract).then_inc(mix_done, 1)

            def ffn(start, f, norm):
                for c in range(CHUNKS):
                    n0 = start + c * (2 * FT + DT)
                    h0 = (f * CHUNKS + c) * FT

                    def tile(i, cols):
                        dve.wait_ge(panel_done, n0 + 2 * i + 1)
                        dve.tensor_tensor(halves(gate[:]), acc_of(n0 % 2), halves(rinv[:]), ALU.mult).then_inc(acc_read, 1)
                        split_lo(n0 + 2 * i + 2, n0 % 2, cols)
                        dve.wait_ge(panel_done, n0 + 2 * i + 2)
                        dve.tensor_tensor(halves(up[:]), acc_of((n0 + 1) % 2), halves(rinv[:]), ALU.mult).then_inc(acc_read, 1)
                        dve.wait_ge(silu_done, h0 + i + 1)
                        dve.wait_ge(acc_read, n0 + 2 * i + 2)
                        dve.tensor_tensor(prod[:], up[:], silu[:], ALU.mult).then_inc(prod_ready, 1)
                        split_lo(n0 + 2 * i + 3, (n0 + 1) % 2, cols)
                        dve.wait_ge(hid_hi_done, h0 + i + 1)
                        dve.tensor_tensor(tile_of(hid_lo, i), prod[:], tile_of(hid_hi, i).bitcast(F32), ALU.subtract).then_inc(hid_done, 1)
                    if c == 0:
                        invert(stat(norm))
                    with dve.Fori(0, FT - 1) as i:
                        tile(i, DT * P)
                    tile(FT - 1, FT * P)
                    n1 = n0 + 2 * FT

                    def final_input(m):
                        if c == CHUNKS - 1 and norm + 1 < N_NORMS - 1:
                            input_lo(norm + 1, m)
                    with dve.Fori(0, DT // 2 - 1) as i:
                        for s in range(2):
                            add_to_x(n1 + 2 * i + s, (n1 + s) % 2, 2 * i + s, 0.5)
                            split_lo(n1 + 2 * i + s + 2, (n1 + s) % 2, FT * P)
                            final_input(2 * i + s)
                    for m in (DT - 2, DT - 1):
                        add_to_x(n1 + m, (n1 + m) % 2, m, 0.5)
                        split_next(n1 + m)
                        final_input(m)

            def mixer_out(start, norm):
                for m in range(DT):
                    add_to_x(start + m, (start + m) % 2, m, 1.0)
                    split_next(start + m)
                    input_lo(norm + 1, m)

            def turned_g(tt):
                rows = P if tt < BLOCKS else NS
                dve.wait_ge(g_turned, tt + 1)
                dve.tensor_copy(v_ln[0:rows, tt, :], ps[0:rows, 4 + tt % 4, :]).then_inc(v_ln_read, 1)
                dve.wait_ge(v_ln_read, tt + 1)
                link(dve.bn_stats(ln_st[0:rows, :], v_ln[0:rows, tt, :]))
                stats_of = dve.bn_aggr(ln_mv[0:rows, tt, :], ln_st[0:rows, :])
                if tt == BLOCKS:
                    stats_of.then_inc(ln_var, 1)
                else:
                    link(stats_of)

            def normed_g(tt):
                rows = P if tt < BLOCKS else NS
                v = v_ln[0:rows, tt, :]
                link(dve.tensor_scalar(v, v, ln_mv[0:rows, tt, 0:1], ln_r[0:rows, tt:tt + 1], ALU.subtract, ALU.mult))
                link(dve.tensor_tensor(v, v, ln_g[0:rows, :], ALU.mult))
                dve.tensor_tensor(v, v, ln_b[0:rows, :], ALU.add).then_inc(v_ln_done, 1)

            def gated(g):
                out = (up if g % 2 else prod)
                dve.wait_ge(gate_sum, g + 1)
                if g >= 2:
                    dve.wait_ge(mix_done, SGU_PIECE + g - 1)
                b0 = 4 + 2 * (g % 2)
                dve.tensor_tensor(out[:, 0:SEQ], ps[:, b0, :], pre[:, SGT + g, 0:SEQ], ALU.mult)
                dve.tensor_tensor(out[:, SEQ:T], ps[:, b0 + 1, 0:NS], pre[:, SGT + g, SEQ:T], ALU.mult).then_inc(mix_ready, 1)

            def gated_lower(g):
                mix_lower(SGU_PIECE + g, mix_lo[:, GROUP + g, :], (up if g % 2 else prod)[:], mix_hi[:, GROUP + g, :])

            def maxima(p3, cols, sinks):
                link(dve.tensor_reduce(smax[:, 0:cols], p3, AX, ALU.max))
                link(dve.tensor_tensor(smax[:, 0:cols], smax[:, 0:cols], sinks, ALU.max))
                link(dve.tensor_scalar(nmax[:, 0:cols], smax[:, 0:cols], -1.0, None, ALU.mult))
                dve.tensor_tensor(dsink[:, 0:cols], sinks, smax[:, 0:cols], ALU.subtract).then_inc(swa_max, 1)

            def swa_softmax_in(n):
                dve.wait_ge(swa_scored, n + 1)
                if n >= 2:
                    dve.wait_ge(swa_turned, swa_units(n - 1))
                lo = swa_halves(n)[0] * WIN
                p3 = prob[n % 2][:, :, lo:2 * WIN]
                dve.scalar_tensor_tensor(out=p3, in0=ps_flat[:, 0:HEADS * 2 * WIN].rearrange("p (h k) -> p h k", h=HEADS)[:, :, lo:2 * WIN],
                                         scalar=SWA_SCALE, in1=bias[:, :, lo:2 * WIN], op0=ALU.mult, op1=ALU.add).then_inc(swa_biased, 1)
                dve.wait_ge(swa_biased, n + 1)
                maxima(p3, HEADS, sink[:])

            def swa_softmax_out(n):
                dve.wait_ge(swa_exp, n + 1)
                link(dve.tensor_tensor(rsum[:], rsum[:], esink[:], ALU.add))
                link(dve.reciprocal(rden[:], rsum[:]))
                lo = swa_halves(n)[0] * WIN
                for h in range(HEADS):
                    p = prob[n % 2][:, h, lo:2 * WIN]
                    last = dve.tensor_scalar(p, p, rden[:, h:h + 1], None, ALU.mult)
                last.then_inc(swa_prob, 1)

            def swa_lower(n):
                mix_lower(SWA_PIECE + n, mix_lo[:, 0:GROUP, n * WIN:(n + 1) * WIN],
                          ps[:, 7, :].rearrange("p (h q) -> p h q", h=GROUP), mix_hi[:, 0:GROUP, n * WIN:(n + 1) * WIN])

            def sample_softmax_in():
                dve.wait_ge(swa_scored, BLOCKS + 1)
                for g in range(2):
                    last = dve.scalar_tensor_tensor(out=prob_s[:, g, :], in0=ps[:, g, 0:WIN + DS], scalar=SWA_SCALE, in1=bias_s[:],
                                                    op0=ALU.mult, op1=ALU.add)
                link(last)
                link(dve.tensor_reduce(smax[:, 0:2], prob_s[:], AX, ALU.max))
                link(dve.tensor_scalar(smax[:, 0:2], smax[:, 0:2], sink_s[:, 0:1], None, ALU.max))
                link(dve.tensor_scalar(nmax[:, 0:2], smax[:, 0:2], -1.0, None, ALU.mult))
                dve.tensor_scalar(dsink[:, 0:2], nmax[:, 0:2], sink_s[:, 0:1], None, ALU.add).then_inc(swa_max, 1)

            def sample_softmax_out():
                dve.wait_ge(swa_exp, BLOCKS + 1)
                link(dve.tensor_tensor(rsum[:, 0:2], rsum[:, 0:2], esink[:, 0:2], ALU.add))
                link(dve.reciprocal(rden[:, 0:2], rsum[:, 0:2]))
                for g in range(2):
                    last = dve.tensor_scalar(prob_s[:, g, :], prob_s[:, g, :], rden[:, g:g + 1], None, ALU.mult)
                last.then_inc(swa_prob, 1)

            def even():
                for t in range(EVEN_IN):
                    n = S_EVEN + t
                    if t == 0:
                        invert(stat(1))
                        dve.wait_ge(even_landed, EVEN_LOADS)
                    scaled(n, pre[:, t, :], rinv[:])
                    split_next(n)
                    if t == 1:
                        link(dve.memset(q_bd[:], 0.0))
                    if SGT + 2 <= t <= SGT + 6:
                        turned_g(t - SGT - 2)
                    if t == SGT + 7:
                        dve.wait_ge(ln_sd_done, 1)
                        link(dve.reciprocal(ln_r[:, 0:4], ln_sd[:, 0:4]))
                        link(dve.reciprocal(ln_r[0:NS, 4:5], ln_sd[0:NS, 4:5]))
                        normed_g(0)
                        normed_g(1)
                    if t == SGT + 8:
                        dve.wait_ge(acc_read, n + 1)
                        for kv in range(2):
                            r = kv * HD
                            last = dve.tensor_copy(
                                q_bd[r:r + HD, :, kv * GROUP * DS:(kv + 1) * GROUP * DS].rearrange("p b (h t) -> p b h t", h=GROUP),
                                pre[r:r + HD, 8:12, SEQ:T].rearrange("p h (b t) -> p b h t", b=DB))
                        last.then_inc(q_bd_ready, 1)
                        normed_g(2)
                        normed_g(3)
                    if t == SGT + 9:
                        normed_g(4)
                swa_softmax_in(0)
                for g in range(SGT):
                    gated(g)
                    if g:
                        gated_lower(g - 1)
                gated_lower(SGT - 1)
                swa_softmax_out(0)
                for n in range(BLOCKS):
                    if n + 1 < BLOCKS:
                        swa_softmax_in(n + 1)
                        swa_softmax_out(n + 1)
                    else:
                        sample_softmax_in()
                        sample_softmax_out()
                    swa_lower(n)
                for kv in range(2):
                    r = kv * HD
                    if kv == 0:
                        dve.wait_ge(mix_hi_done, SWA_S_PIECE + 1)
                    last = dve.tensor_tensor(mix_lo[r:r + HD, 0:GROUP, SEQ:T].rearrange("p h (b t) -> p b h t", b=DB),
                                             ps[r:r + HD, 7, 0:DB * NS].rearrange("p (b g h t) -> p b g h t", b=DB, g=2, h=GROUP)[:, :, kv],
                                             mix_hi[r:r + HD, 0:GROUP, SEQ:T].bitcast(F32).rearrange("p h (b t) -> p b h t", b=DB), ALU.subtract)
                last.then_inc(mix_done, 1)
                mixer_out(EVEN_OUT, 1)

            def convolve(t):
                zs = conv_zs[:, t]
                out = prod[:, 0:SEQ]
                out_s = prod[:, SEQ:T].rearrange("p (b s) -> p b s", b=DB)
                link(dve.tensor_scalar(out, conv_z[:, t, 0:SEQ], conv_w[:, 0, t:t + 1], None, ALU.mult))
                link(dve.tensor_scalar(out_s, zs[:, :, 0:DS], conv_w[:, 0, t:t + 1], None, ALU.mult))
                for j in range(1, 3):
                    link(dve.scalar_tensor_tensor(out=out, in0=conv_z[:, t, j:j + SEQ], scalar=conv_w[:, j, t:t + 1], in1=out,
                                                  op0=ALU.mult, op1=ALU.add))
                    link(dve.scalar_tensor_tensor(out=out_s, in0=zs[:, :, j:j + DS], scalar=conv_w[:, j, t:t + 1], in1=out_s,
                                                  op0=ALU.mult, op1=ALU.add))
                dve.tensor_tensor(prod[:], prod[:], silu[:], ALU.mult).then_inc(mix_ready, 1)

            def rope(t2d, count):
                r = slice(NOPE, QK)
                dve.wait_ge(rotated, count)
                dve.tensor_tensor(halves(silu[r, :]), ps[r, 6:8, 0:TH], halves(sin[r, :]), ALU.mult)
                link(dve.tensor_tensor(prod[r, :], t2d, cos[r, :], ALU.mult))
                return dve.tensor_tensor(t2d, prod[r, :], silu[r, :], ALU.add)

            def mla_maxima(h):
                dve.wait_ge(mla_scored, h + 1)
                diag = ps_flat[:, 0:BLOCKS * 640].rearrange("p (i c) -> p i c", i=BLOCKS)[:, :, 0:P]
                link(dve.tensor_tensor(diag, diag, causal[:].unsqueeze(1).to_broadcast([P, BLOCKS, P]), ALU.add))
                for i in range(BLOCKS):
                    last = dve.tensor_reduce(mx[:, i:i + 1], ps[:, i, 0:(i + 1) * P], AX, ALU.max)
                link(last)
                dve.tensor_scalar(nmx[:], mx[:, 0:BLOCKS], -MLA_SCALE, None, ALU.mult).then_inc(mla_max, 1)

            def mla_normalise(h):
                dve.wait_ge(mla_exp, h + 1)
                link(dve.reciprocal(rs[:], sm[:, 0:BLOCKS]))
                for i in range(BLOCKS):
                    p = p_mla[:, i * (i + 1) // 2:(i + 1) * (i + 2) // 2, :].rearrange("p j k -> p (j k)")
                    last = dve.tensor_scalar(p, p, rs[:, i:i + 1], None, ALU.mult)
                last.then_inc(mla_prob, 1)

            def mla_lower(h):
                r = VD * (h % 2)
                mix_lower(MLA_PIECE + h, mix_lo[r:r + VD, CT + h // 2, 0:SEQ], ps[r:r + VD, 7, :], mix_hi[r:r + VD, CT + h // 2, 0:SEQ])

            def sample_max(b, q):
                r = NS * (b % 4)
                dve.wait_ge(page_scored, b * PAGES + 4 * q + 4)
                return dve.tensor_reduce(mx[r:r + NS, q:q + 1], ps[r:r + NS, q, :], AX, ALU.max)

            def sample_maxima(b):
                r = slice(NS * (b % 4), NS * (b % 4) + NS)
                sample_max(b, 3)
                dve.wait_ge(s_new_ready, b + 1)
                link(dve.tensor_tensor(s_new[r, :], ps[r, 7, KV_LORA:KV_LORA + DS], causal_s[r, :], ALU.add))
                link(dve.tensor_reduce(mx[r, 4:5], s_new[r, :], AX, ALU.max))
                link(dve.tensor_reduce(mx[r, 5:6], mx[r, 0:5], AX, ALU.max))
                dve.tensor_scalar(nmx[r, 3:4], mx[r, 5:6], -MLA_SCALE, None, ALU.mult).then_inc(s_max, 1)

            def sample_tokens(b):
                r = slice(NS * (b % 4), NS * (b % 4) + NS)
                dve.wait_ge(values_done, b + 1)
                link(dve.tensor_reduce(rs[r, 0:1], sm[r, 0:5], AX, ALU.add))
                link(dve.reciprocal(rs[r, 1:2], rs[r, 0:1]))
                dve.tensor_scalar(o_tok[r, :], ps[r, 7, 0:KV_LORA], rs[r, 1:2], None, ALU.mult).then_inc(o_tok_done, 1)

            def sample_latents(g):
                dve.wait_ge(o_turned, g + 1)
                for c in range(KT):
                    last = dve.tensor_copy(o_lat[:, c].rearrange("p h (b t) -> p b h t", b=DB)[:, 4 * g:4 * g + 4],
                                           ps[:, 6, c * P:(c + 1) * P].rearrange("p (b h t) -> p b h t", b=4, h=HEADS))
                last.then_inc(o_lat_done, 1)

            def sample():
                for b in range(DB + 1):
                    for p in range(PAGES):
                        g = b * PAGES + p
                        if b < DB and p % 2 == 0:
                            dve.wait_ge(page_turned, g + 1)
                            if g >= KT_SLOTS:
                                dve.wait_ge(page_scored, g - KT_SLOTS + 1)
                            dve.tensor_copy(keys_t[g % KT_SLOTS][:].rearrange("p j k -> p (j k)"), ps[0:QK, 4, 0:3 * PAGE])\
                               .then_inc(keys_copied[0], 1)
                        if b < DB and p in (7, 11, 15):
                            sample_max(b, p // 4 - 1)
                        if b and p == AT_MAX:
                            sample_maxima(b - 1)
                        if b and p == AT_OUT:
                            sample_tokens(b - 1)
                        if b == 5 and p == 2:
                            sample_latents(0)
                sample_latents(1)

            def odd():
                for t in range(ODD_IN):
                    n = S_ODD + t
                    if t == 0:
                        invert(stat(4))
                        dve.wait_ge(odd_landed, ODD_LOADS)
                        link(dve.memset(conv_z[:, :, 0:2], 0.0))
                    if t < 3 * CT:
                        scaled(n, (gate, up, silu)[t % 3][:], rinv[:])
                        split_next(n)
                        dve.wait_ge(acc_read, n + 1)
                        if t % 3 == 1:
                            link(dve.tensor_tensor(conv_z[:, t // 3, 2:SEQ + 2], gate[:, 0:SEQ], up[:, 0:SEQ], ALU.mult))
                            link(dve.tensor_tensor(conv_zs[:, t // 3, :, 2:DS + 2], gate[:, SEQ:T].rearrange("p (b s) -> p b s", b=DB),
                                                   up[:, SEQ:T].rearrange("p (b s) -> p b s", b=DB), ALU.mult))
                        if t % 3 == 2:
                            convolve(t // 3)
                            mix_lower(CONV_PIECE + t // 3, mix_lo[:, t // 3, :], prod[:], mix_hi[:, t // 3, :])
                    elif n < CKV0:
                        c = n - CQ0
                        if c >= 2:
                            dve.wait_ge(square_done, 5 * DT + c - 1)
                        buf = prod if c % 2 else silu
                        scaled(n, buf[:], rinv[:])
                        split_next(n)
                        dve.wait_ge(cq_hi_done, c + 1)
                        dve.wait_ge(acc_read, n + 1)
                        dve.scalar_tensor_tensor(out=cq_lo[:, c, :], in0=buf[:], scalar=q_gain[:, c:c + 1], in1=cq_hi[:, c, :].bitcast(F32),
                                                 op0=ALU.mult, op1=ALU.subtract).then_inc(cq_done, 1)
                    else:
                        scaled(n, kpe[:] if n == KPE else ckv[:, n - CKV0, :], rinv[:])
                        split_next(n)
                invert(stat(4) + 1, gate)
                for h in range(HEADS):
                    n = ODD_UQ + h
                    dve.wait_ge(panel_done, n + 1)
                    dve.tensor_tensor(halves(qf[0:QK, h, :]), acc_of(n % 2, QK), halves(gate[0:QK, :]), ALU.mult).then_inc(acc_read, 1)
                    split_next(n)
                    if h == 0:
                        invert(stat(4) + 2, up)
                        for c in range(KT):
                            dve.wait_ge(square_done, 5 * DT + QT + KT)
                            dve.scalar_tensor_tensor(out=ckv[:, c, :], in0=ckv[:, c, :], scalar=kv_gain[:, c:c + 1], in1=up[:],
                                                     op0=ALU.mult, op1=ALU.mult).then_inc(ckv_done, 1)
                        dve.wait_ge(spare_landed, 48)
                        rope(kpe[NOPE:QK, :], 1).then_inc(kpe_done, 1)
                    else:
                        rope(qf[NOPE:QK, h - 1, :], h + 1).then_inc(q_done, 1)
                rope(qf[NOPE:QK, HEADS - 1, :], HEADS + 1).then_inc(q_done, 1)
                mla_maxima(0)
                mla_normalise(0)
                for h in range(HEADS):
                    if h + 1 < HEADS:
                        mla_maxima(h + 1)
                        mla_normalise(h + 1)
                    mla_lower(h)
                dve.wait_ge(qa_ready, 1)
                for j in range(3):
                    rows = QK if j < 2 else NOPE
                    src = ps[0:rows, 4, j * HEADS * NS:(j + 1) * HEADS * NS] if j < 2 else ps[0:rows, 5, 0:HEADS * NS]
                    dve.tensor_copy(qa[0:rows, j].rearrange("p b (h t) -> p b h t", h=HEADS), src.rearrange("p (h b t) -> p b h t", h=HEADS, b=DB))
                for c in range(KT):
                    dve.tensor_copy(qa_new[:, c].rearrange("p b (h t) -> p b h t", h=HEADS),
                                    ps[:, 6, c * HEADS * NS:(c + 1) * HEADS * NS].rearrange("p (h b t) -> p b h t", h=HEADS, b=DB))
                dve.tensor_copy(qa[NOPE:QK, 2].rearrange("p b (h t) -> p b h t", h=HEADS),
                                qf[NOPE:QK, :, SEQ:T].rearrange("p h (b t) -> p b h t", b=DB)).then_inc(qa_done, 1)
                sample()
                mix_lower(MLA_S_PIECE, mix_lo[:, CT:2 * CT, SEQ:T], ps[:, 4, 0:CT * NS].rearrange("p (h t) -> p h t", h=CT), mix_hi[:, CT:2 * CT, SEQ:T])
                mixer_out(ODD_OUT, 4)

            dve.wait_ge(dist_ready, 1)
            dve.tensor_copy(by_dist[:], ps[0:HEADS, 7, 0:3 * WIN]).then_inc(dist_copied, 1)
            dve.wait_ge(consts_landed, CONSTS)
            for t in range(DT):
                input_lo(0, t)
            split_lo(0, 0, DT * P)
            split_lo(1, 1, DT * P)
            ffn(*FFNS[0])
            even()
            ffn(*FFNS[1])
            ffn(*FFNS[2])
            odd()
            ffn(*FFNS[3])
            invert(stat(6))
            for t in range(DT):
                dve.scalar_tensor_tensor(out=y[:, t, :], in0=x[:, t, :], scalar=gains[:, N_NORMS - 1, t:t + 1], in1=rinv[:],
                                         op0=ALU.mult, op1=ALU.mult).then_inc(y_done, 1)

        @block.gpsimd
        def _(pool):
            def add_square(k, src, first):
                pool.tensor_tensor(sumsq[:] if first else square[:], src, src, ALU.mult).then_inc(square_done, 1)
                pool.wait_ge(square_done, k + 1)
                if first:
                    pool.nop().then_inc(sumsq_step, 1)
                else:
                    pool.tensor_tensor(sumsq[:], sumsq[:], square[:], ALU.add).then_inc(sumsq_step, 1)

            def x_squares(k0, n1):
                pool.wait_ge(acc_read, n1 + 1)
                add_square(k0, x[:, 0, :], True)
                with pool.Fori(1, DT) as m:
                    pool.wait_ge(acc_read, n1 + m + 1)
                    pool.wait_ge(sumsq_step, k0 + m)
                    add_square(k0 + m, tile_of(x, m), False)

            def ffn_end(start):
                return start + CHUNKS * (2 * FT + DT) - DT

            for t, name in ((rel, "rel"), (onehot, "onehot")):
                pool.dma_start(t[:], d[name]).then_inc(rel_landed, 16)
            for t, name in ((ident, "ident"), (ones, "ones"), (gains, "gains"), (eps, "eps")):
                pool.dma_start(t[:], d[name]).then_inc(consts_landed, 16)
            pool.wait_ge(x_landed, 16)
            add_square(0, x[:, 0, :], True)
            with pool.Fori(1, DT) as m:
                pool.wait_ge(sumsq_step, m)
                add_square(m, tile_of(x, m), False)
            pool.wait_ge(dist_copied, 1)
            pool.dma_start(d["dist"], by_dist[:].unsqueeze(1).to_broadcast([HEADS, P, 3 * WIN])).then_inc(dist_stored, 16)
            pool.wait_ge(dist_stored, 16)
            dist = d["dist"]
            row = P * 3 * WIN
            pool.dma_start(bias[:], bass.AP(dist.tensor, P - 1, [[3 * WIN - 1, P], [row, HEADS], [1, 2 * WIN]])).then_inc(even_landed, 16)
            for b4 in range(4):
                pool.dma_start(bias_s[b4 * NS:(b4 + 1) * NS, :], bass.AP(dist.tensor, P - 1, [[row, HEADS], [3 * WIN - 1, DS], [1, WIN + DS]]))\
                    .then_inc(even_landed, 16)
            for t, name in ((sgu_w, "sgu_w"), (sgu_ws, "sgu_ws"), (sgu_b, "sgu_b"), (sgu_bs, "sgu_bs"), (ln_g, "ln_g"), (ln_b, "ln_b"),
                            (sink, "sink")):
                src = d[name] if name not in ("ln_g", "ln_b", "sink") else d[name].partition_broadcast(P)
                pool.dma_start(t[:], src).then_inc(even_landed, 16)
            for b4 in range(4):
                pool.dma_start(sink_s[b4 * NS:(b4 + 1) * NS, :], d["sink_s"]).then_inc(even_landed, 16)
            pool.wait_ge(even_landed, EVEN_LOADS)
            pool.affine_select(out=sgu_w[:], in_=sgu_w[:], compare_op=ALU.is_ge, fill=0.0, base=0, pattern=[[0, SGT], [1, P]],
                               channel_multiplier=-1).then_inc(sgu_masked, 1)
            pool.affine_select(out=sgu_ws[:], in_=sgu_ws[:], compare_op=ALU.is_ge, fill=0.0, base=0, pattern=[[0, SGT], [1, NS]],
                               channel_multiplier=-1).then_inc(sgu_masked, 1)
            x_squares(DT, ffn_end(START["f0"]))
            pool.wait_ge(panel_done, S_EVEN)
            for t, name in ((k_cache, "k_cache"), (v_cache, "v_cache")):
                pool.dma_start(t[:], d[name]).then_inc(cache_landed, 16)
            pool.wait_ge(acc_read, EVEN_OUT)
            for name, t, c0, c1 in (("o_kp", 12, SEQ - WIN, SEQ), ("o_vp", 13, SEQ - WIN, SEQ), ("o_ks", 12, SEQ, T), ("o_vs", 13, SEQ, T)):
                pool.dma_start(d[name], pre[:, t, c0:c1]).then_inc(stored_even, 16)
            pool.wait_ge(v_ln_done, 5)
            pool.dma_start(d["o_sgu"], v_ln[0:NS, 4, :]).then_inc(stored_even, 16)
            x_squares(2 * DT, EVEN_OUT)
            pool.wait_ge(mix_done, EVEN_PIECES)
            pool.wait_ge(stored_even, 16 * 5)
            for t, name in ((w_uk, "w_uk"), (w_uv, "w_uv"), (perm, "perm"), (conv_w, "conv_w"), (q_gain, "q_gain"), (kv_gain, "kv_gain"),
                            (causal, "causal"), (causal_s, "causal_s")):
                pool.dma_start(t[:], d[name]).then_inc(odd_landed, 16)
            for t in range(CT):
                pool.dma_start(conv_zs[:, t, :, 0:2], d["conv_state"][:, t]).then_inc(odd_landed, 16)
            pool.dma_start(table[:], d["table"]).then_inc(table_landed, 16)
            x_squares(3 * DT, ffn_end(START["f1"]))
            x_squares(4 * DT, ffn_end(START["f2"]))
            pool.wait_ge(panel_done, S_ODD)
            for t, name in ((w_uk_t, "w_uk_t"), (cos, "cos"), (sin, "sin")):
                pool.dma_start(t[:], d[name]).then_inc(spare_landed, 16)
            for c in range(QT):
                k = 5 * DT + c
                pool.wait_ge(acc_read, CQ0 + c + 1)
                if c:
                    pool.wait_ge(sumsq_step, k)
                add_square(k, (prod if c % 2 else silu)[:], c == 0)
            for c in range(KT):
                k = 5 * DT + QT + c
                pool.wait_ge(acc_read, CKV0 + c + 1)
                if c == 0:
                    pool.wait_ge(stat_ready, stat(4) + 1)
                else:
                    pool.wait_ge(sumsq_step, k)
                add_square(k, ckv[:, c, :], c == 0)
            pool.dma_start(d["o_convp"], conv_z[:, :, SEQ:SEQ + 2]).then_inc(stored_conv, 16)
            pool.dma_start(d["o_convs"], conv_zs[:, :, :, DS:DS + 2]).then_inc(stored_conv, 16)
            pool.wait_ge(ckv_done, KT)
            pool.dma_start(d["o_ckv"], ckv[:]).then_inc(stored_odd, 16)
            pool.wait_ge(kpe_done, 1)
            pool.dma_start(d["o_kpe"], kpe[NOPE:QK, :]).then_inc(stored_odd, 16)
            for u in range(UNITS):
                if u % UNIT_SLOTS % 3 == 2:
                    load_pages(pool, u)
            x_squares(6 * DT, ODD_OUT)
            x_squares(7 * DT, ffn_end(START["f3"]))


def rope_tables():
    half = ROPE // 2
    pos = np.concatenate([np.arange(SEQ), np.tile(PAGES * PAGE + np.arange(DS), DB)]).astype(np.float32)
    inv = np.exp(np.float32(-np.log(10000.0)) * np.arange(half, dtype=np.float32) / np.float32(half)).astype(np.float32)
    ang = pos[None, :] * inv[:, None]
    cos, sin = (np.tile(f(ang).astype(np.float32), (2, 1)) for f in (np.cos, np.sin))
    swap = np.zeros((ROPE, ROPE), np.float32)
    for i in range(half):
        swap[half + i, i] = -1.0
        swap[i, half + i] = 1.0
    return cos, sin, swap


def constants():
    c = {"ident": np.eye(P, dtype=np.float32), "ones": np.ones((P, P), np.float32), "eps": np.full((P, 1), EPS, np.float32)}
    dist = 2 * WIN - 1 - np.arange(3 * WIN)
    n = np.maximum(dist, 0)
    exact = BUCKETS // 2
    large = exact + (np.log(np.maximum(n, 1).astype(np.float32) / exact) / np.log(WIN / exact) * (BUCKETS - exact)).astype(np.int32)
    bucket = np.where(n < exact, n, np.minimum(large, BUCKETS - 1))
    bucket = np.where((dist >= 0) & (dist <= WIN), bucket, BUCKETS)
    c["onehot"] = (bucket[None, :] == np.arange(BUCKETS + 1)[:, None]).astype(np.float32)
    cos, sin, swap = rope_tables()
    pad = lambda a: np.concatenate([np.zeros((NOPE, a.shape[1]), np.float32), a, np.zeros((P - QK, a.shape[1]), np.float32)])
    c["cos"], c["sin"], c["perm"] = pad(cos), pad(sin), pad(swap)
    q = np.arange(P)
    c["causal"] = np.where(q[None, :] <= q[:, None], 0.0, NEG).astype(np.float32)
    c["causal_s"] = np.where(np.arange(DS)[None, :] <= (q % DS)[:, None], 0.0, NEG).astype(np.float32)
    return c


def panels(w, m=P):
    *lead, k, cols = w.shape
    w = w.reshape(*lead, k // P, P, cols // m, m)
    n = len(lead)
    w = w.transpose(*range(n), n + 2, n + 1, n, n + 3)
    return np.ascontiguousarray(w).reshape(*lead, cols // m, P, k // P * m)


def features(v):
    v = v.reshape(*v.shape[:-1], v.shape[-1] // P, P)
    return np.ascontiguousarray(np.moveaxis(v, -1, 0))


def layout(i):
    a = constants()
    tok = np.concatenate([i["x_prompt"].reshape(SEQ, D), i["x_sample"].reshape(NS, D)], 0)
    a["xT"] = tok.T.reshape(DT, P, T).transpose(1, 0, 2)
    for f in (1, 2):
        g, u = panels(i[f"ffn{f}_w_gate"]), panels(i[f"ffn{f}_w_up"])
        a[f"gu{f}"] = np.stack([g, u], 2)
        dn = i[f"ffn{f}_w_down"]
        a[f"down{f}"] = panels(dn.reshape(dn.shape[0], CHUNKS, FT * P, D))
    a["gains"] = features(np.stack([i["ffn1_norm"][0], i["mix_norm"][0], i["ffn2_norm"][0], i["ffn1_norm"][1], i["mix_norm"][1],
                                    i["ffn2_norm"][1], i["final_norm"]]))
    q_w, kv_w = HEADS * HD, 2 * HD
    pair = np.concatenate([np.r_[t * HD:(t + 1) * HD, (GROUP + t) * HD:(GROUP + t + 1) * HD] for t in range(GROUP)])
    w = i["even_w_in"][0]
    u0 = q_w + 2 * kv_w
    order = np.concatenate([np.arange(u0 + SGW, u0 + 2 * SGW), np.arange(u0, u0 + SGW), pair, np.arange(q_w, u0)])
    a["even_in"] = panels(w[:, order])
    a["even_out"] = panels(i["even_w_out"][0][np.concatenate([pair, np.arange(q_w, q_w + SGW)])])
    a["rel"] = np.concatenate([i["rel_bias"], np.full((1, HEADS), NEG, np.float32)])
    a["sink"] = i["attn_sinks"][0]
    a["sink_s"] = np.repeat(i["attn_sinks"][0], DS)[:, None]
    a["ln_g"], a["ln_b"] = i["sgu_ln_g"][0], i["sgu_ln_b"][0]
    sw = i["sgu_w"][0]
    a["sgu_w"] = sw.transpose(2, 0, 1)
    ws = np.zeros((NS, SGT, NS), np.float32)
    for b in range(DB):
        ws[b * DS:(b + 1) * DS, :, b * DS:(b + 1) * DS] = sw[:, :DS, :DS].transpose(2, 0, 1)
    a["sgu_ws"] = ws
    a["sgu_b"] = i["sgu_b"]
    a["sgu_bs"] = np.tile(i["sgu_b"][:, :, :DS], (1, 1, DB))
    k, v = i["cache_swa_k"][0].reshape(DB, WIN, P), i["cache_swa_v"][0].reshape(DB, WIN, P)
    a["k_nat"], a["v_nat"] = k, v
    a["k_cache"], a["v_cache"] = k.transpose(2, 0, 1), v.transpose(1, 0, 2)
    c_w = CT * P
    w = i["odd_w_in"][0]
    tiles = [np.arange(s * c_w + t * P, s * c_w + (t + 1) * P) for t in range(CT) for s in (1, 2, 0)]
    k0 = 3 * c_w + Q_LORA + KV_LORA
    order = np.concatenate(tiles + [np.arange(3 * c_w, k0)] + [np.arange(k0, k0 + ROPE)] * 4)
    a["odd_in"] = panels(w[:, order])
    a["odd_out"] = panels(i["odd_w_out"][0])
    a["w_uq"] = panels(i["mla_w_uq"][0], QK)
    a["q_gain"], a["kv_gain"] = features(i["mla_q_norm"][0]), features(i["mla_kv_norm"][0])
    uk, uv = i["mla_w_uk"][0], i["mla_w_uv"][0]
    a["w_uk"] = uk.reshape(KT, P, HEADS * NOPE).transpose(1, 0, 2)
    a["w_uv"] = uv.reshape(KT, P, HEADS * VD).transpose(1, 0, 2)
    a["w_uk_t"] = uk.transpose(2, 1, 0)
    a["conv_w"] = features(i["conv_w"][0])
    a["conv_state"] = i["state_conv"][0].reshape(DB, 2, CT, P).transpose(3, 2, 0, 1)
    a["page_pool"] = np.concatenate([i["cache_mla_ckv"][0], i["cache_mla_kpe"][0]], -1)
    a["table"] = i["page_table"].reshape(1, DB * PAGES)
    return {k: np.ascontiguousarray(v) for k, v in a.items()}


OUTPUTS = {"o_y": (P, DT, T), "o_kp": (P, WIN), "o_vp": (P, WIN), "o_ks": (P, NS), "o_vs": (P, NS), "o_kc": (DB, WIN - DS, P),
           "o_vc": (DB, WIN - DS, P), "o_sgu": (NS, SGW), "o_convp": (P, CT, 2), "o_convs": (P, CT, DB, 2), "o_ckv": (P, KT, T),
           "o_kpe": (ROPE, T)}


def results(o):
    y = o["o_y"].transpose(2, 1, 0).reshape(T, D)
    heads = (2, HD)

    def window(cached, new):
        new = new.T.reshape(DB, DS, P)
        return np.concatenate([cached, new], 1).reshape(1, DB, WIN, *heads)
    ckv = o["o_ckv"].transpose(2, 1, 0).reshape(T, KV_LORA)
    kpe = o["o_kpe"].T
    return (y[:SEQ].reshape(1, SEQ, D), y[SEQ:].reshape(DB, DS, D),
            o["o_kp"].T.reshape(1, 1, WIN, *heads), o["o_vp"].T.reshape(1, 1, WIN, *heads),
            window(o["o_kc"], o["o_ks"]), window(o["o_vc"], o["o_vs"]),
            o["o_sgu"].reshape(1, DB, DS, SGW),
            o["o_convp"].transpose(2, 1, 0).reshape(1, 1, 2, CT * P),
            o["o_convs"].transpose(2, 3, 1, 0).reshape(1, DB, 2, CT * P),
            ckv[:SEQ].reshape(1, 1, SEQ, KV_LORA), kpe[:SEQ].reshape(1, 1, SEQ, ROPE),
            ckv[SEQ:].reshape(1, DB, DS, KV_LORA), kpe[SEQ:].reshape(1, DB, DS, ROPE))


def kernel(**inputs):
    import concourse.bacc as bacc
    from concourse.bass_utils import run_bass_kernel_spmd

    arrays = layout({k: np.asarray(v) for k, v in inputs.items()})
    nc = bacc.Bacc("TRN2", target_bir_lowering=False, num_devices=1)
    d = {k: nc.dram_tensor(k, v.shape, mybir.dt.from_np(v.dtype), kind="ExternalInput").ap() for k, v in arrays.items()}
    for k, shape in OUTPUTS.items():
        d[k] = nc.dram_tensor(k, shape, F32, kind="ExternalOutput").ap()
    d["dist"] = nc.dram_tensor("dist", (HEADS, P, 3 * WIN), F32, kind="Internal").ap()
    decoder_step(nc, d)
    return results(run_bass_kernel_spmd(nc, [arrays], core_ids=[0]).results[0])
```

```python
from contextlib import ExitStack

import numpy as np

import concourse.bass as bass
from concourse import mybir

F32 = mybir.dt.float32
F32R = mybir.dt.float32r
I32 = mybir.dt.int32
ACT = mybir.ActivationFunctionType
ALU = mybir.AluOpType
AX = mybir.AxisListType.X

P = 128
D = 1024
SEQ = 512
DB, DS = 8, 4
NS = DB * DS
T = SEQ + NS
TH = T // 2
DT = D // P
D_FF = 2816
CHUNKS = 2
FT = D_FF // P // CHUNKS
EPS = 1e-6
NEG = -1e30

HD = 64
HEADS = 8
GROUP = 4
WIN = 128
BUCKETS = 32
BLOCKS = SEQ // WIN
SGW = 512
SGT = SGW // P

CT = 4
Q_LORA = 768
QT = Q_LORA // P
KV_LORA = 256
KT = KV_LORA // P
NOPE, ROPE, VD = 64, 32, 64
QK = NOPE + ROPE
PAGES = 16
PAGE = 128
N_POOL = 160
UNIT = 4
UNITS = DB * PAGES // UNIT
UNIT_SLOTS = 13
EARLY_UNITS = 7
KT_SLOTS = 5
AT_MAX, AT_EXP, AT_TURN, AT_TURNED, AT_VALUES, AT_OUT = 3, 4, 12, 13, 14, 15
MLA_SCALE = float(QK) ** -0.5
SWA_SCALE = float(HD) ** -0.5

EVEN_IN = 14
Q_TILE, K_TILE, V_TILE, U_TILE = 4, 8, 9, 10
ODD_IN = 3 * CT + QT + KT + 1

FFN_K = ([DT] * (2 * FT) + [FT] * DT) * CHUNKS
EVEN_K = [DT] * EVEN_IN + [DT] * DT
ODD_K = [DT] * ODD_IN + [QT] * HEADS + [DT] * DT
PANEL_K = FFN_K + EVEN_K + FFN_K + FFN_K + ODD_K + FFN_K
N_PANELS = len(PANEL_K)
START = dict(zip(("f0", "even", "f1", "f2", "odd", "f3"),
                 np.cumsum([0] + [len(k) for k in (FFN_K, EVEN_K, FFN_K, FFN_K, ODD_K)]).tolist()))
CONSTS = 2 * 16
X_PIECE = 2
POOL_TILES = 3
N_NORMS = 7


def stat(norm):
    return norm + 1 if norm < 5 else norm + 3


def sumsq_steps(norm):
    return POOL_TILES + DT * norm + (0 if norm < 5 else QT + KT)


def decoder_step(nc, d):
    ctx = ExitStack()
    with ctx:
        base = (nc.sbuf_base + 255) // 256 * 256
        top = [base]

        def at(name, shape, dt, offset):
            return nc.alloc_sbuf_tensor_at(name, shape, dt, offset=offset)

        def size(shape):
            return 4 * int(np.prod(shape[1:]))

        def place(name, shape, dt=F32):
            t = at(name, shape, dt, top[0])
            top[0] += (size(shape) + 31) // 32 * 32
            return t

        x = place("x", [P, DT, T])
        region_h = top[0]
        hx_hi = place("hx_hi", [P, DT, T], F32R)
        hx_lo = place("hx_lo", [P, DT, T], F32R)
        end_h = top[0]
        region_hid = top[0]
        hid_hi = place("hid_hi", [P, FT, T], F32R)
        hid_lo = place("hid_lo", [P, FT, T], F32R)
        end_hid = top[0]
        raw = [place(f"raw{s}", [P, FT * P]) for s in range(2)]
        w_hi = [place(f"w_hi{s}", [P, FT * P], F32R) for s in range(2)]
        w_lo = [place(f"w_lo{s}", [P, FT * P], F32R) for s in range(2)]
        gate = place("gate", [P, T])
        silu = place("silu", [P, T])
        up = place("up", [P, T])
        prod = place("prod", [P, T])
        rinv = place("rinv", [P, T])
        rms = place("rms", [P, T])
        square = place("square", [P, T])
        sumsq = place("sumsq", [P, T])
        ident = place("ident", [P, P])
        ones = place("ones", [P, P])
        gains = place("gains", [P, N_NORMS, DT])
        eps = place("eps", [P, 1])
        region_e = top[0]
        end_e = nc.sbuf_usable_end

        def region(start, end):
            cur = [start]

            def put(name, shape, dt=F32):
                t = at(name, shape, dt, cur[0])
                cur[0] += (size(shape) + 31) // 32 * 32
                assert cur[0] <= end, (name, cur[0], end)
                return t
            return put

        put = region(region_hid, end_hid)
        mix_hi = put("mix_hi", [P, DT, T], F32R)
        mix_lo = put("mix_lo", [P, DT, T], F32R)
        spare = region_hid + 2 * size([P, DT, T])

        put = region(spare, end_hid)
        k_cache = put("k_cache", [P, DB, WIN])
        v_cache = put("v_cache", [P, DB, P])
        put = region(region_e, end_e)
        pre = put("pre", [P, EVEN_IN, T])
        bias = put("bias", [P, HEADS, 2 * WIN])
        bias_s = put("bias_s", [P, WIN + DS])
        sgu_w = put("sgu_w", [P, SGT, P])
        sgu_ws = put("sgu_ws", [NS, SGT, NS])
        sgu_b = put("sgu_b", [1, SGT, P])
        sgu_bs = put("sgu_bs", [1, SGT, NS])
        ln_g = put("ln_g", [P, SGW])
        ln_b = put("ln_b", [P, SGW])
        sink = put("sink", [P, HEADS])
        sink_s = put("sink_s", [P, 1])
        smax = put("smax", [P, HEADS])
        nmax = put("nmax", [P, HEADS])
        dsink = put("dsink", [P, HEADS])
        esink = put("esink", [P, HEADS])
        rsum = put("rsum", [P, HEADS])
        rden = put("rden", [P, HEADS])
        ln_st = put("ln_st", [P, 6])
        ln_mv = put("ln_mv", [P, 5, 2])
        ln_sd = put("ln_sd", [P, 5])
        ln_r = put("ln_r", [P, 5])
        v_ln = put("v_ln", [P, 5, SGW])
        put = region(v_ln.manual_sbuf_range[0], end_e)
        rel = put("rel", [BUCKETS + 1, HEADS])
        onehot = put("onehot", [BUCKETS + 1, 3 * WIN])
        by_dist = put("by_dist", [HEADS, 3 * WIN])
        put = region(region_h, end_h)
        prob = [put(f"prob{s}", [P, HEADS, 2 * WIN]) for s in range(2)]
        prob_t = put("prob_t", [P, 2, HEADS, WIN])
        v_tok = put("v_tok", [P, BLOCKS, P])
        v_new = put("v_new", [DS, DB, P])
        prob_s = put("prob_s", [P, 2, WIN + DS])
        prob_st = put("prob_st", [P, 2, P])
        prob_st2 = put("prob_st2", [DS, 2, P])
        put = region(region_hid, end_hid)
        q_bd = at("q_bd", [P, DB, NS], F32, spare + 2 * size([P, DB, WIN]))

        put = region(spare, end_hid)
        w_uk_t = put("w_uk_t", [NOPE, HEADS, KV_LORA])
        cos = put("cos", [P, T])
        sin = put("sin", [P, T])
        put = region(region_e, end_e)
        cq_hi = put("cq_hi", [P, QT, T], F32R)
        cq_lo = put("cq_lo", [P, QT, T], F32R)
        end_cq = region_e + 2 * size([P, QT, T])
        ckv = put("ckv", [P, KT, T])
        kpe = put("kpe", [P, T])
        conv_z = put("conv_z", [P, CT, SEQ + 2])
        conv_zs = put("conv_zs", [P, CT, DB, DS + 2])
        w_uk = put("w_uk", [P, KT, HEADS * NOPE])
        w_uv = put("w_uv", [P, KT, HEADS * VD])
        perm = put("perm", [P, ROPE])
        conv_w = put("conv_w", [P, 3, CT])
        q_gain = put("q_gain", [P, QT])
        kv_gain = put("kv_gain", [P, KT])
        causal = put("causal", [P, P])
        causal_s = put("causal_s", [P, DS])
        qa = put("qa", [P, 3, DB, NS])
        qa_new = put("qa_new", [P, KT, DB, NS])
        o_lat = put("o_lat", [P, KT, HEADS, NS])
        s_new = put("s_new", [P, DS])
        mx = put("mx", [P, 8])
        nmx = put("nmx", [P, 4])
        sm = put("sm", [P, 8])
        rs = put("rs", [P, 4])
        table = put("table", [1, DB * PAGES], I32)
        put = region(region_h, end_h)
        qf = put("qf", [P, HEADS, T])
        kf = put("kf", [P, HEADS, SEQ])
        put = region(region_e, end_cq)
        v_mla = put("v_mla", [P, BLOCKS, HEADS * VD])
        p_mla = put("p_mla", [P, 10, P])
        p_mla_t = put("p_mla_t", [P, 10, P])
        pages = [put(f"page{s}", [P, KV_LORA + ROPE]) for s in range(6)]
        put = region(conv_z.manual_sbuf_range[0], conv_z.manual_sbuf_range[0] + size([P, CT, SEQ + 2]))
        pages += [put(f"page{s}", [P, KV_LORA + ROPE]) for s in range(6, 13)]
        put = region(gate.manual_sbuf_range[0], ident.manual_sbuf_range[0])
        pages += [put(f"page{s}", [P, KV_LORA + ROPE]) for s in range(13, EARLY_UNITS * UNIT)]
        put = region(region_e, end_cq)
        keys_t = [put(f"keys_t{s}", [QK, 3, PAGE]) for s in range(KT_SLOTS)]
        put = region(p_mla.manual_sbuf_range[0], end_cq)
        p_s = put("p_s", [P, PAGES * PAGE + DS])
        o_tok = put("o_tok", [P, KV_LORA])
        p_st2 = put("p_st2", [DS, 2, NS])
        assert p_st2.manual_sbuf_range[1] <= pages[0].manual_sbuf_range[0]
        put = region(region_h, end_h)
        pages += [put(f"page{s}", [P, KV_LORA + ROPE]) for s in range(EARLY_UNITS * UNIT, UNIT_SLOTS * UNIT)]
        ckv_new = at("ckv_new", [DS, DB, KV_LORA], F32, w_uk_t.manual_sbuf_range[0])
        p_st = [at(f"p_st{s}", [P, PAGES, NS], F32, t.manual_sbuf_range[0]) for s, t in enumerate((cos, sin))]
        y = at("y", [P, DT, T], F32, region_e)

        ps = ctx.enter_context(nc.psum_tensor("ps", [P, 8, 512], F32))
        ps_flat = ps[:].rearrange("p b c -> p (b c)")
        acc = [ps[:, 2 * s:2 * s + 2, :] for s in range(2)]

        def sem(name):
            return ctx.enter_context(nc.semaphore(name))

        raw_landed = [sem(f"raw_landed{s}") for s in range(2)]
        w_hi_done = sem("w_hi_done")
        w_lo_done = sem("w_lo_done")
        panel_done = sem("panel_done")
        acc_read = sem("acc_read")
        consts_landed = sem("consts_landed")
        gains_landed = sem("gains_landed")
        x_landed = [sem(f"x_landed{s}") for s in range(DT // X_PIECE)]
        late_squared = sem("late_squared")
        others_added = sem("others_added")
        rel_landed = sem("rel_landed")
        dist_stored = sem("dist_stored")
        even_landed = sem("even_landed")
        cache_landed = sem("cache_landed")
        odd_landed = sem("odd_landed")
        spare_landed = sem("spare_landed")
        table_landed = sem("table_landed")
        pages_landed = [sem(f"pages_landed{s}") for s in range(UNIT_SLOTS)]
        copied = sem("copied")
        stored = sem("stored")
        stored_even = sem("stored_even")
        stored_odd = sem("stored_odd")
        stored_conv = sem("stored_conv")
        hx_hi_done = sem("hx_hi_done")
        hx_done = sem("hx_done")
        square_done = sem("square_done")
        sumsq_step = sem("sumsq_step")
        stat_ready = sem("stat_ready")
        rms_done = sem("rms_done")
        rinv_ready = sem("rinv_ready")
        silu_done = sem("silu_done")
        prod_ready = sem("prod_ready")
        hid_hi_done = sem("hid_hi_done")
        hid_done = sem("hid_done")
        mix_ready = sem("mix_ready")
        mix_hi_done = sem("mix_hi_done")
        mix_done = sem("mix_done")
        step = sem("step")
        dist_ready = sem("dist_ready")
        dist_copied = sem("dist_copied")
        sgu_masked = sem("sgu_masked")
        gelu_done = sem("gelu_done")
        g_turned = sem("g_turned")
        v_ln_read = sem("v_ln_read")
        ln_var = sem("ln_var")
        ln_sd_done = sem("ln_sd_done")
        v_ln_done = sem("v_ln_done")
        gate_sum = sem("gate_sum")
        v_turned = sem("v_turned")
        v_tok_done = sem("v_tok_done")
        swa_scored = sem("swa_scored")
        swa_biased = sem("swa_biased")
        swa_max = sem("swa_max")
        swa_exp = sem("swa_exp")
        swa_prob = sem("swa_prob")
        swa_turned = sem("swa_turned")
        swa_copied = sem("swa_copied")
        swa_out = sem("swa_out")
        q_bd_ready = sem("q_bd_ready")
        cq_hi_done = sem("cq_hi_done")
        cq_done = sem("cq_done")
        ckv_done = sem("ckv_done")
        rotated = sem("rotated")
        q_done = sem("q_done")
        kpe_done = sem("kpe_done")
        kf_ready = sem("kf_ready")
        kf_done = sem("kf_done")
        vm_ready = sem("vm_ready")
        vm_done = sem("vm_done")
        mla_scored = sem("mla_scored")
        mla_max = sem("mla_max")
        mla_exp = sem("mla_exp")
        mla_prob = sem("mla_prob")
        mla_turned = sem("mla_turned")
        mla_copied = sem("mla_copied")
        mla_out = sem("mla_out")
        qa_ready = sem("qa_ready")
        qa_done = sem("qa_done")
        new_turned = sem("new_turned")
        new_copied = sem("new_copied")
        page_turned = sem("page_turned")
        keys_copied = [sem(f"keys_copied{s}") for s in range(2)]
        page_scored = sem("page_scored")
        s_new_ready = sem("s_new_ready")
        s_max = sem("s_max")
        s_exp = sem("s_exp")
        s_turned = sem("s_turned")
        s_copied = sem("s_copied")
        values_done = sem("values_done")
        o_tok_done = sem("o_tok_done")
        o_turned = sem("o_turned")
        s_out = sem("s_out")
        o_lat_done = sem("o_lat_done")
        y_done = sem("y_done")

        def halves(t2d):
            return t2d.rearrange("p (a b) -> p a b", a=2)

        def acc_of(slot, rows=P):
            return acc[slot][0:rows, :, 0:TH]

        def tile_of(t3d, i):
            return t3d[:, bass.ds(i, 1), :].rearrange("p a t -> p (a t)")

        def swa_halves(n):
            return (1,) if n == 0 else (0, 1)

        def swa_units(n):
            return sum(2 * len(swa_halves(b)) for b in range(n))

        FFNS = ((START["f0"], 0, 0), (START["f1"], 1, 2), (START["f2"], 2, 3), (START["f3"], 3, 5))
        S_EVEN, S_ODD = START["even"], START["odd"]
        EVEN_OUT, ODD_UQ = S_EVEN + EVEN_IN, S_ODD + ODD_IN
        ODD_OUT = ODD_UQ + HEADS
        LAST_G, LAST_U = S_EVEN + SGT, S_EVEN + 2 * SGT
        CQ0, CKV0, KPE = S_ODD + 3 * CT, S_ODD + 3 * CT + QT, S_ODD + 3 * CT + QT + KT
        EVEN_PIECES = BLOCKS + SGT + 1
        ODD_PIECES = CT + HEADS + 1
        SGU_PIECE, SWA_PIECE, SWA_S_PIECE = 0, SGT, SGT + BLOCKS
        CONV_PIECE, MLA_PIECE, MLA_S_PIECE = EVEN_PIECES, EVEN_PIECES + CT, EVEN_PIECES + CT + HEADS

        SWA_TILES, SGU_TILES = list(range(GROUP)), list(range(GROUP, DT))
        CONV_TILES, MLA_TILES = list(range(CT)), list(range(CT, DT))

        TURN_ORDER = [(j, i) for j in range(BLOCKS) for i in range(j, BLOCKS)]
        BY_LENGTH = list(reversed(range(BLOCKS)))
        EVEN_LOADS = 16 * (1 + 4 + 7 + 4)
        ODD_LOADS = 16 * (8 + CT)

        def panel_cols(n):
            return PANEL_K[n] * (QK if ODD_UQ <= n < ODD_OUT else P)

        def load_pages(eng, u):
            if u == 0 or u == 2:
                eng.wait_ge(table_landed, 16)
                eng.wait_ge(q_done, HEADS)
                eng.wait_ge(stored_conv, 32)
            if u in (EARLY_UNITS, EARLY_UNITS + 1):
                eng.wait_ge(mla_scored, BLOCKS * HEADS)
                eng.wait_ge(qa_done, 1)
            if u >= UNIT_SLOTS:
                eng.wait_ge(values_done, (u - UNIT_SLOTS) * UNIT // PAGES + 1)
            for g in range(UNIT * u, UNIT * (u + 1)):
                page = eng.value_load(table[0:1, g:g + 1], min_val=0, max_val=N_POOL - 1)
                eng.dma_start(pages[g % len(pages)][:], d["page_pool"][bass.ds(page, 1)].rearrange("a p c -> (a p) c"))\
                   .then_inc(pages_landed[u % UNIT_SLOTS], 16)

        page_bank, bank_before = [], []
        for g in range(DB * PAGES):
            used = {bank: (max(i for i, k in enumerate(page_bank) if k == bank) if bank in page_bank else -1)
                    for bank in ((4, 5, 6) if g // PAGES not in (0, 5) and g % PAGES < 9 else (4, 5))}
            page_bank.append(min(used, key=used.get))
            bank_before.append(used[page_bank[-1]])

        late_square = (up, prod, gate, silu, rms)

        block = ctx.enter_context(nc.Block())

        @block.sync
        def _(sp):
            def load_panel(n, slot, cols, src, first=False):
                if not first:
                    sp.wait_ge(w_lo_done, n - 1)
                sp.dma_start(raw[slot][:, 0:cols], src).then_inc(raw_landed[slot], 16)

            def load_ffn(start, gu, down, layer, first=False):
                for c in range(CHUNKS):
                    n0 = start + c * (2 * FT + DT)
                    i0 = 0
                    if first and c == 0:
                        i0 = 1
                    with sp.Fori(i0, FT) as i:
                        for s in range(2):
                            load_panel(n0 + 2 * i + s, (n0 + s) % 2, DT * P, gu[layer, c * FT + i, s])
                    with sp.Fori(0, DT // 2) as i:
                        for s in range(2):
                            load_panel(n0 + 2 * FT + 2 * i + s, (n0 + s) % 2, FT * P, down[layer, c, 2 * i + s])

            def load_matrix(start, w, first=0, end=None):
                for t in range(first, w.shape[0] if end is None else end):
                    load_panel(start + t, (start + t) % 2, panel_cols(start + t), w[t])

            for t, name in ((gains, "gains"), (eps, "eps")):
                sp.dma_start(t[:], d[name]).then_inc(gains_landed, 16)
            for c in range(DT // X_PIECE):
                if c % 2 == 0:
                    load_panel(c // 2, c // 2, DT * P, d["gu1"][0, 0, c // 2], first=True)
                piece = slice(c * X_PIECE, (c + 1) * X_PIECE)
                sp.dma_start(x[:, piece, :], d["xT"][:, piece, :]).then_inc(x_landed[c], 16)
            load_ffn(START["f0"], d["gu1"], d["down1"], 0, first=True)
            load_matrix(S_EVEN, d["even_in"])
            sp.dma_start(d["o_kc"], d["k_nat"][:, DS:WIN]).then_inc(copied, 16)
            sp.dma_start(d["o_vc"], d["v_nat"][:, DS:WIN]).then_inc(copied, 16)
            load_matrix(EVEN_OUT, d["even_out"])
            load_ffn(START["f1"], d["gu2"], d["down2"], 0)
            load_ffn(START["f2"], d["gu1"], d["down1"], 1)
            load_matrix(S_ODD, d["odd_in"])
            load_matrix(ODD_UQ, d["w_uq"])
            load_matrix(ODD_OUT, d["odd_out"], 0, 2)

            for u in range(UNITS):
                if u % UNIT_SLOTS % 3 != 2:
                    load_pages(sp, u)
            load_matrix(ODD_OUT, d["odd_out"], 2)
            load_ffn(START["f3"], d["gu2"], d["down2"], 1)
            for t in range(DT):
                sp.wait_ge(y_done, t + 1)
                sp.dma_start(d["o_y"][:, t, :], y[:, t, :]).then_inc(stored, 16)
            sp.wait_ge(stored, 16 * DT)
            sp.wait_ge(copied, 32)
            sp.wait_ge(stored_even, 16 * 5)
            sp.wait_ge(stored_conv, 16 * 2)
            sp.wait_ge(stored_odd, 16 * 2)

        @block.tensor
        def _(pe):
            def panel(n, slot, rhs_hi, rhs_lo, tiles, wait_input=None, m=P, begin=True, end=True):
                if begin:
                    pe.wait_ge(w_lo_done, n + 1)
                    if not (isinstance(n, int) and n < 2):
                        pe.wait_ge(acc_read, n - 1)
                for t in tiles:
                    if wait_input is not None:
                        wait_input(t)
                    hi, lo = w_hi[slot][:, t * m:(t + 1) * m], w_lo[slot][:, t * m:(t + 1) * m]
                    for w, r, one in ((hi, rhs_hi, 0), (hi, rhs_lo, 1), (lo, rhs_hi, 2)):
                        for a in range(2):
                            last = pe.matmul(acc[slot][0:m, a, 0:TH], w, r[:, t, a * TH:(a + 1) * TH],
                                             start=(begin and t == tiles[0] and one == 0), stop=(end and t == tiles[-1] and one == 2))
                if end:
                    last.then_inc(panel_done, 1)

            def stats(steps, others=0):
                pe.wait_ge(sumsq_step, steps)
                for a in range(2):
                    last = pe.matmul(ps[:, 4 + a, 0:TH], ones[:], sumsq[:, a * TH:(a + 1) * TH], start=True, stop=not others)
                if others:
                    pe.wait_ge(others_added, others)
                    for a in range(2):
                        last = pe.matmul(ps[:, 4 + a, 0:TH], ones[:], up[:, a * TH:(a + 1) * TH], start=False, stop=True)
                last.then_inc(stat_ready, 1)

            def ffn(start, f, norm):
                for c in range(CHUNKS):
                    n0 = start + c * (2 * FT + DT)
                    done = (f * CHUNKS + c) * FT
                    i0 = 0
                    if c == 0:
                        def split_input(t):
                            pe.wait_ge(hx_done, DT * norm + t + 1)
                        panel(n0, n0 % 2, hx_hi, hx_lo, range(DT), split_input)
                        if f == 0:
                            pe.wait_ge(consts_landed, CONSTS)
                        stats(sumsq_steps(norm), others=1 if f == 0 else 0)
                        panel(n0 + 1, (n0 + 1) % 2, hx_hi, hx_lo, range(DT))
                        if f == 0:
                            by_distance()
                        i0 = 1
                    with pe.Fori(i0, FT) as i:
                        for s in range(2):
                            panel(n0 + 2 * i + s, (n0 + s) % 2, hx_hi, hx_lo, range(DT))
                    n1 = n0 + 2 * FT

                    def hidden(t):
                        pe.wait_ge(hid_done, done + t + 1)
                    panel(n1, n1 % 2, hid_hi, hid_lo, range(FT), hidden)
                    panel(n1 + 1, (n1 + 1) % 2, hid_hi, hid_lo, range(FT))
                    with pe.Fori(1, DT // 2) as i:
                        for s in range(2):
                            panel(n1 + 2 * i + s, (n1 + s) % 2, hid_hi, hid_lo, range(FT))

            def mixer_out_begin(start, tiles, pieces):
                pe.wait_ge(mix_done, pieces)
                for t in range(2):
                    panel(start + t, (start + t) % 2, mix_hi, mix_lo, tiles, end=False)

            def mixer_out(start, early, late, pieces):
                pe.wait_ge(mix_done, pieces)
                for t in range(2):
                    panel(start + t, (start + t) % 2, mix_hi, mix_lo, late, begin=False)
                for t in range(2, DT):
                    panel(start + t, (start + t) % 2, mix_hi, mix_lo, early + late)

            def by_distance():
                pe.wait_ge(rel_landed, 32)
                pe.matmul(ps[0:HEADS, 7, 0:3 * WIN], rel[:], onehot[:], start=True, stop=True).then_inc(dist_ready, 1)

            def turn_g(tt):
                rows = P if tt < BLOCKS else NS
                if tt == 0:
                    pe.wait_ge(gelu_done, SGT)
                    pe.wait_ge(rms_done, stat(1))
                if tt >= 4:
                    pe.wait_ge(v_ln_read, tt - 3)
                for g in range(SGT):
                    last = pe.transpose(ps[0:rows, 4 + tt % 4, g * P:(g + 1) * P], pre[:, g, tt * P:tt * P + rows], ident[:])
                last.then_inc(g_turned, 1)

            def gate_matmul(g):
                b0 = 4 + 2 * (g % 2)
                if g == 0:
                    pe.wait_ge(v_ln_done, 5)
                    pe.wait_ge(sgu_masked, 2)
                if g >= 2:
                    pe.wait_ge(mix_ready, SGU_PIECE + g - 1)
                for c in range(BLOCKS):
                    out = ps[:, b0, c * P:(c + 1) * P]
                    pe.matmul(out, ones[0:1, :], sgu_b[:, g, :], start=True, stop=False)
                    pe.matmul(out, v_ln[:, c, g * P:(g + 1) * P], sgu_w[:, g, :], start=False, stop=True)
                out = ps[:, b0 + 1, 0:NS]
                pe.matmul(out, ones[0:1, :], sgu_bs[:, g, :], start=True, stop=False)
                pe.matmul(out, v_ln[0:NS, 4, g * P:(g + 1) * P], sgu_ws[:, g, :], start=False, stop=True)\
                  .then_inc(gate_sum, 1)

            def turn_v():
                pe.wait_ge(acc_read, EVEN_OUT)
                pe.wait_ge(mix_ready, SGU_PIECE + SGT)
                for n in range(BLOCKS):
                    pe.transpose(ps[:, 4, n * P:(n + 1) * P], pre[:, V_TILE, n * P:(n + 1) * P], ident[:])
                for b in range(DB):
                    last = pe.transpose(ps[0:DS, 5 + b // 4, (b % 4) * P:(b % 4 + 1) * P],
                                        pre[:, V_TILE, SEQ + b * DS:SEQ + (b + 1) * DS], ident[:])
                last.then_inc(v_turned, 1)

            def swa_score(n):
                if n == 0:
                    pe.wait_ge(acc_read, EVEN_OUT)
                k0 = swa_halves(n)[0]
                for h in range(HEADS):
                    if n and h % GROUP == 0:
                        pe.wait_ge(swa_biased, 2 * (n - 1) + h // GROUP + 1)
                    r = HD * (h // GROUP)
                    last = pe.matmul(ps_flat[:, h * 2 * WIN + k0 * WIN:(h + 1) * 2 * WIN],
                                     pre[r:r + HD, Q_TILE + h % GROUP, n * WIN:(n + 1) * WIN],
                                     pre[r:r + HD, K_TILE, (n - 1 + k0) * WIN:(n + 1) * WIN], start=True, stop=True)
                    if h % GROUP == GROUP - 1:
                        last.then_inc(swa_scored, 1)

            def swa_values(n):
                if n == 0:
                    pe.wait_ge(v_tok_done, 2)
                u = swa_units(n)
                for kv in range(2):
                    pe.wait_ge(swa_prob, 2 * n + kv + 1)
                    for j in swa_halves(n):
                        if u >= 3:
                            pe.wait_ge(swa_copied, u - 2)
                        for hh in range(GROUP):
                            last = pe.transpose(ps[:, 4 + u % 3, hh * WIN:(hh + 1) * WIN],
                                                prob[n % 2][:, kv * GROUP + hh, j * WIN:(j + 1) * WIN], ident[:])
                        last.then_inc(swa_turned, 1)
                        u += 1
                if n:
                    pe.wait_ge(mix_done, SWA_PIECE + n)
                u = swa_units(n)
                for kv in range(2):
                    for j in swa_halves(n):
                        u += 1
                        pe.wait_ge(swa_copied, u)
                        last = pe.matmul(ps[kv * HD:(kv + 1) * HD, 7, :], v_tok[:, n - 1 + j, kv * HD:(kv + 1) * HD],
                                         prob_t[:, j, kv * GROUP:(kv + 1) * GROUP, :], start=(j == swa_halves(n)[0]), stop=(j == 1))
                last.then_inc(swa_out, 1)

            def swa_sample_score():
                pe.wait_ge(swa_biased, 2 * BLOCKS)
                pe.wait_ge(q_bd_ready, 1)
                pe.wait_ge(cache_landed, 32)
                for b in range(DB):
                    r = NS * (b % 4)
                    pe.matmul(ps[r:r + NS, b // 4, 0:WIN], q_bd[:, b, :], k_cache[:, b, :], start=True, stop=True)
                    last = pe.matmul(ps[r:r + NS, b // 4, WIN:WIN + DS], q_bd[:, b, :],
                                     pre[:, K_TILE, SEQ + b * DS:SEQ + (b + 1) * DS], start=True, stop=True)
                last.then_inc(swa_scored, 1)

            def swa_sample_values():
                pe.wait_ge(swa_prob, 2 * BLOCKS + 1)
                pe.wait_ge(swa_copied, swa_units(BLOCKS))
                for g in range(2):
                    pe.transpose(ps[:, 4, g * P:(g + 1) * P], prob_s[:, g, 0:WIN], ident[:])
                    last = pe.transpose(ps[0:DS, 5, g * P:(g + 1) * P], prob_s[:, g, WIN:WIN + DS], ident[:])
                last.then_inc(swa_turned, 1)
                mixer_out_begin(EVEN_OUT, SGU_TILES, SGU_PIECE + SGT)
                pe.wait_ge(swa_copied, swa_units(BLOCKS) + 2)
                pe.wait_ge(mix_done, SWA_PIECE + BLOCKS)
                for b in range(DB):
                    r = NS * (b % 4)
                    pe.matmul(ps[:, 7, b * NS:(b + 1) * NS], v_cache[:, b, :], prob_st[:, b // 4, r:r + NS],
                              start=True, stop=False)
                    last = pe.matmul(ps[:, 7, b * NS:(b + 1) * NS], v_new[:, b, :], prob_st2[:, b // 4, r:r + NS],
                                     start=False, stop=True)
                last.then_inc(swa_out, 1)

            def even():
                def split_input(t):
                    pe.wait_ge(hx_done, DT + t + 1)
                for t in range(EVEN_IN):
                    n = S_EVEN + t
                    panel(n, n % 2, hx_hi, hx_lo, range(DT), split_input if t == 0 else None)
                    if t == 0:
                        stats(sumsq_steps(1))
                        pe.wait_ge(even_landed, EVEN_LOADS)
                    if SGT <= t <= SGT + 4:
                        turn_g(t - SGT)
                for g in range(SGT):
                    gate_matmul(g)
                    if g == 0:
                        swa_score(0)
                turn_v()
                for n in range(BLOCKS):
                    if n + 1 < BLOCKS:
                        swa_score(n + 1)
                    else:
                        swa_sample_score()
                    swa_values(n)
                swa_sample_values()
                mixer_out(EVEN_OUT, SGU_TILES, SWA_TILES, EVEN_PIECES)

            def rotate(src, h):
                for a in range(2):
                    last = pe.matmul(ps[NOPE:QK, 6 + a, 0:TH], perm[NOPE:QK, :], src[NOPE:QK, a * TH:(a + 1) * TH],
                                     start=True, stop=True)
                last.then_inc(rotated, 1)

            def nope_keys(p):
                if p >= 2:
                    pe.wait_ge(kf_done, 2 * p - 1)
                for c in range(KT):
                    last = pe.matmul(ps[:, 4 + p % 2, :], w_uk[:, c, p * P:(p + 1) * P], ckv[:, c, 0:SEQ],
                                     start=(c == 0), stop=(c == KT - 1))
                last.then_inc(kf_ready, 1)

            def mla_values_of(j):
                if j == 1:
                    pe.wait_ge(qa_done, 1)
                if j >= 2:
                    pe.wait_ge(vm_done, j - 1)
                for c in range(KT):
                    last = pe.matmul(ps[:, 7 - j % 2, :], ckv[:, c, j * P:(j + 1) * P], w_uv[:, c, :],
                                     start=(c == 0), stop=(c == KT - 1))
                last.then_inc(vm_ready, 1)

            def mla_score(h):
                if h == 0:
                    pe.wait_ge(kf_done, HEADS + 1)
                    pe.wait_ge(q_done, HEADS)
                for k, i in enumerate(BY_LENGTH):
                    if h:
                        pe.wait_ge(mla_exp, BLOCKS * (h - 1) + k + 1)
                    pe.matmul(ps[:, i, 0:(i + 1) * P], qf[0:QK, h, i * P:(i + 1) * P], kf[0:QK, h, 0:(i + 1) * P],
                              start=True, stop=True).then_inc(mla_scored, 1)

            def mla_turn(h):
                if h:
                    pe.wait_ge(mla_copied, 3 * h)
                else:
                    pe.wait_ge(vm_done, BLOCKS)
                for k, i in enumerate(BY_LENGTH):
                    pe.wait_ge(mla_prob, BLOCKS * h + k + 1)
                    for j in range(i + 1):
                        s = TURN_ORDER.index((j, i))
                        last = pe.transpose(ps[:, 4 + s // 4, (s % 4) * P:(s % 4 + 1) * P], p_mla[:, i * (i + 1) // 2 + j, :], ident[:])
                last.then_inc(mla_turned, 1)

            def mla_values(h):
                if h >= 2:
                    pe.wait_ge(mix_done, MLA_PIECE + h - 1)
                r = VD * (h % 2)
                for j in range(BLOCKS):
                    s = TURN_ORDER.index((j, j))
                    pe.wait_ge(mla_copied, 3 * h + (s + BLOCKS - j - 1) // 4 + 1)
                    last = pe.matmul(ps[r:r + VD, 7, j * P:SEQ], v_mla[:, j, h * VD:(h + 1) * VD], p_mla_t[:, s:s + BLOCKS - j, :],
                                     start=(j == 0), stop=(j == BLOCKS - 1))
                last.then_inc(mla_out, 1)

            def absorb():
                pe.wait_ge(kf_done, HEADS + 1)
                pe.wait_ge(q_done, HEADS)
                for h in range(HEADS):
                    q_h = qf[0:NOPE, h, SEQ:T]
                    for j in range(2):
                        pe.matmul(ps[0:QK, 4, (j * HEADS + h) * NS:(j * HEADS + h + 1) * NS], w_uk_t[:, h, j * QK:(j + 1) * QK], q_h,
                                  start=True, stop=True)
                    pe.matmul(ps[0:NOPE, 5, h * NS:(h + 1) * NS], w_uk_t[:, h, 2 * QK:KV_LORA], q_h, start=True, stop=True)
                    for c in range(KT):
                        last = pe.matmul(ps[:, 6, (c * HEADS + h) * NS:(c * HEADS + h + 1) * NS], w_uk_t[:, h, c * P:(c + 1) * P], q_h,
                                         start=True, stop=True)
                last.then_inc(qa_ready, 1)

            def turn_new(half):
                if half == 0:
                    pe.wait_ge(mla_copied, 3 * HEADS)
                    pe.wait_ge(mix_done, MLA_PIECE + HEADS)
                else:
                    pe.wait_ge(new_copied, 1)
                for s in range(4 * KT):
                    b, c = 4 * half + s // KT, s % KT
                    last = pe.transpose(ps[0:DS, 6 + s // 4, (s % 4) * P:(s % 4 + 1) * P],
                                        ckv[:, c, SEQ + b * DS:SEQ + (b + 1) * DS], ident[:])
                last.then_inc(new_turned, 1)

            def turn_page(g):
                u = g // UNIT
                if g % UNIT == 0:
                    pe.wait_ge(pages_landed[u % UNIT_SLOTS], 16 * UNIT * (u // UNIT_SLOTS + 1))
                before = bank_before[g]
                if before >= 0:
                    pe.wait_ge(keys_copied[before % 2], before // 2 + 1)
                elif page_bank[g] < 6:
                    pe.wait_ge(mla_copied, 3 * HEADS)
                else:
                    pe.wait_ge(new_copied, 2)
                if page_bank[g] == 6 and g // PAGES >= 2:
                    pe.wait_ge(s_copied, g // PAGES - 1)
                for j in range(3):
                    last = pe.transpose(ps[0:QK, page_bank[g], j * PAGE:(j + 1) * PAGE], pages[g % len(pages)][:, j * QK:(j + 1) * QK], ident[:])
                last.then_inc(page_turned, 1)

            def score_page(g):
                b, p = g // PAGES, g % PAGES
                r = NS * (b % 4)
                pe.wait_ge(keys_copied[g % 2], g // 2 + 1)
                if g == 0:
                    pe.wait_ge(mla_exp, BLOCKS * HEADS)
                if p == 0 and b >= 4:
                    pe.wait_ge(s_exp, b - 3)
                for j in range(3):
                    last = pe.matmul(ps_flat[r:r + NS, p * PAGE:(p + 1) * PAGE], qa[0:QK, j, b, :], keys_t[g % KT_SLOTS][:, j, :],
                                     start=(j == 0), stop=(j == 2))
                last.then_inc(page_scored, 1)

            def score_new(b):
                r = NS * (b % 4)
                if b == 0:
                    pe.wait_ge(new_copied, 2)
                if b >= 4:
                    pe.wait_ge(o_tok_done, b - 3)
                new = ps[r:r + NS, 7, KV_LORA:KV_LORA + DS]
                for c in range(KT):
                    pe.matmul(new, qa_new[:, c, b, :], ckv[:, c, SEQ + b * DS:SEQ + (b + 1) * DS], start=(c == 0), stop=False)
                pe.matmul(new, qa[NOPE:QK, 2, b, :], kpe[NOPE:QK, SEQ + b * DS:SEQ + (b + 1) * DS], start=False, stop=True)\
                  .then_inc(s_new_ready, 1)

            def turn_probs(b):
                r = NS * (b % 4)
                pe.wait_ge(s_exp, b + 1)
                if b:
                    pe.wait_ge(s_copied, b)
                    pe.wait_ge(o_tok_done, b)
                last = [g for g in range(min((b + 1) * PAGES + AT_TURN + 1, DB * PAGES)) if page_bank[g] == 6][-1:]
                for g in last:
                    pe.wait_ge(keys_copied[g % 2], g // 2 + 1)
                if b == 5:
                    pe.wait_ge(o_lat_done, 1)
                one = ident[r:r + NS, r:r + NS]
                for p in range(PAGES):
                    pe.transpose(ps[:, 6, p * NS:(p + 1) * NS], p_s[r:r + NS, p * PAGE:(p + 1) * PAGE], one)
                pe.transpose(ps[0:DS, 7, KV_LORA + NS:KV_LORA + 2 * NS], p_s[r:r + NS, PAGES * PAGE:PAGES * PAGE + DS], one)\
                  .then_inc(s_turned, 1)

            def page_values(b):
                r = NS * (b % 4)
                pe.wait_ge(s_copied, b + 1)
                out = ps[r:r + NS, 7, 0:KV_LORA]
                for p in range(PAGES):
                    pe.matmul(out, p_st[b % 2][:, p, :], pages[(b * PAGES + p) % len(pages)][:, 0:KV_LORA], start=(p == 0), stop=False)
                pe.matmul(out, p_st2[:, b % 2, :], ckv_new[:, b, :], start=False, stop=True).then_inc(values_done, 1)

            def turn_latents(g):
                pe.wait_ge(o_tok_done, 4 * g + 4)
                pe.wait_ge(s_copied, 4 * g + 4)
                for c in range(KT):
                    last = pe.transpose(ps[:, 6, c * P:(c + 1) * P], o_tok[:, c * P:(c + 1) * P], ident[:])
                last.then_inc(o_turned, 1)

            def sample():
                for b in range(DB + 1):
                    for p in range(PAGES):
                        g = b * PAGES + p
                        if b < DB:
                            turn_page(g)
                        if 2 <= g < DB * PAGES + 2:
                            score_page(g - 2)
                        if b == 0 and p == 6:
                            turn_new(1)
                        if b and p == 1:
                            score_new(b - 1)
                        if b and p == AT_TURN:
                            turn_probs(b - 1)
                        if b and p == AT_VALUES:
                            page_values(b - 1)
                        if b == 5 and p == 0:
                            turn_latents(0)
                mixer_out_begin(ODD_OUT, CONV_TILES, CONV_PIECE + CT)
                turn_latents(1)

            def sample_out():
                pe.wait_ge(o_lat_done, 2)
                for h in range(HEADS):
                    r = VD * (h % 2)
                    for c in range(KT):
                        last = pe.matmul(ps[r:r + VD, 4, (h // 2) * NS:(h // 2 + 1) * NS], w_uv[:, c, h * VD:(h + 1) * VD], o_lat[:, c, h, :],
                                         start=(c == 0), stop=(c == KT - 1))
                last.then_inc(s_out, 1)

            def odd():
                def split_input(t):
                    pe.wait_ge(hx_done, 4 * DT + t + 1)
                for t in range(ODD_IN):
                    n = S_ODD + t
                    panel(n, n % 2, hx_hi, hx_lo, range(DT), split_input if t == 0 else None)
                    if t == 0:
                        stats(sumsq_steps(4))
                    if n == CKV0:
                        pe.wait_ge(rms_done, stat(4))
                        stats(sumsq_steps(4) + QT)
                for h in range(HEADS):
                    n = ODD_UQ + h

                    def split_cq(t):
                        pe.wait_ge(cq_done, t + 1)
                    panel(n, n % 2, cq_hi, cq_lo, range(QT), split_cq if h == 0 else None, m=QK)
                    if h == 0:
                        pe.wait_ge(rms_done, stat(4) + 1)
                        stats(sumsq_steps(4) + QT + KT)
                        pe.wait_ge(spare_landed, 48)
                        pe.wait_ge(acc_read, KPE + 1)
                        rotate(kpe, 0)
                    else:
                        pe.wait_ge(acc_read, n)
                        if h == 1:
                            pe.wait_ge(kpe_done, 1)
                        else:
                            pe.wait_ge(q_done, h - 1)
                        rotate(qf[:, h - 1, :], h)
                pe.wait_ge(ckv_done, KT)
                nope_keys(0)
                nope_keys(1)
                pe.wait_ge(acc_read, ODD_OUT)
                pe.wait_ge(q_done, HEADS - 1)
                rotate(qf[:, HEADS - 1, :], HEADS)
                nope_keys(2)
                nope_keys(3)
                mla_score(0)
                absorb()
                for j in range(BLOCKS):
                    mla_values_of(j)
                for h in range(HEADS):
                    mla_turn(h)
                    if h + 1 < HEADS:
                        mla_score(h + 1)
                    mla_values(h)
                turn_new(0)
                sample()
                sample_out()
                mixer_out(ODD_OUT, CONV_TILES, MLA_TILES, EVEN_PIECES + ODD_PIECES)

            ffn(*FFNS[0])
            even()
            ffn(*FFNS[1])
            ffn(*FFNS[2])
            odd()
            ffn(*FFNS[3])
            stats(sumsq_steps(6) - 1, others=2)

        @block.scalar
        def _(act):
            def split_hi(n, slot, cols):
                act.wait_ge(raw_landed[slot], 8 * (n - slot) + 16)
                if not (isinstance(n, int) and n < 2):
                    act.wait_ge(panel_done, n - 1)
                act.activation(w_hi[slot][:, 0:cols], raw[slot][:, 0:cols], ACT.Copy).then_inc(w_hi_done, 1)

            def split_next(n):
                if n + 2 < N_PANELS:
                    split_hi(n + 2, n % 2, panel_cols(n + 2))

            def root(k, terms):
                act.wait_ge(stat_ready, k)
                if k > 1:
                    act.wait_ge(rinv_ready, k - 1)
                act.activation(halves(rms[:]), ps[:, 4:6, 0:TH], ACT.Sqrt, scale=1.0 / terms, bias=eps[:, 0:1])\
                   .then_inc(rms_done, 1)

            def input_hi(norm, m):
                act.activation(tile_of(hx_hi, m), tile_of(x, m), ACT.Copy, scale=gains[:, norm, bass.ds(m, 1)])\
                   .then_inc(hx_hi_done, 1)

            def ffn(start, f, norm):
                for c in range(CHUNKS):
                    n0 = start + c * (2 * FT + DT)
                    h0 = (f * CHUNKS + c) * FT

                    def tile(i, cols):
                        split_hi(n0 + 2 * i + 2, n0 % 2, cols)
                        act.wait_ge(acc_read, n0 + 2 * i + 1)
                        act.activation(silu[:], gate[:], ACT.Silu).then_inc(silu_done, 1)
                        split_hi(n0 + 2 * i + 3, (n0 + 1) % 2, cols)
                        act.wait_ge(prod_ready, h0 + i + 1)
                        act.activation(tile_of(hid_hi, i), prod[:], ACT.Copy).then_inc(hid_hi_done, 1)
                    if c == 0:
                        root(stat(norm), D)
                    with act.Fori(0, FT - 1) as i:
                        tile(i, DT * P)
                    tile(FT - 1, FT * P)
                    n1 = n0 + 2 * FT

                    def final_input(m):
                        if c == CHUNKS - 1 and norm + 1 < N_NORMS - 1:
                            act.wait_ge(acc_read, n1 + m + 1)
                            input_hi(norm + 1, m)
                    with act.Fori(0, DT // 2 - 1) as i:
                        for s in range(2):
                            split_hi(n1 + 2 * i + s + 2, (n1 + s) % 2, FT * P)
                            final_input(2 * i + s)
                    for m in (DT - 2, DT - 1):
                        split_next(n1 + m)
                        final_input(m)

            def mixer_out(start, norm):
                for m in range(DT):
                    split_next(start + m)
                    act.wait_ge(acc_read, start + m + 1)
                    input_hi(norm + 1, m)

            def mix_upper(out, src, ready, count):
                act.wait_ge(ready, count)
                act.activation(out, src, ACT.Copy).then_inc(mix_hi_done, 1)

            def swa_exps(n):
                lo = swa_halves(n)[0] * WIN
                for kv in range(2):
                    act.wait_ge(swa_max, 2 * n + kv + 1)
                    for h in range(kv * GROUP, (kv + 1) * GROUP):
                        act.activation(prob[n % 2][:, h, lo:2 * WIN], prob[n % 2][:, h, lo:2 * WIN], ACT.Exp,
                                       bias=nmax[:, h:h + 1], accum_out=rsum[:, h:h + 1])
                    four = slice(kv * GROUP, (kv + 1) * GROUP)
                    act.activation(esink[:, four], dsink[:, four], ACT.Exp).then_inc(swa_exp, 1)

            def swa_copies(n):
                u = swa_units(n)
                if n:
                    act.wait_ge(swa_out, n)
                for kv in range(2):
                    for j in swa_halves(n):
                        act.wait_ge(swa_turned, u + 1)
                        act.activation(prob_t[:, j, kv * GROUP:(kv + 1) * GROUP, :].rearrange("p h q -> p (h q)"), ps[:, 4 + u % 3, :], ACT.Copy)\
                           .then_inc(swa_copied, 1)
                        u += 1

            def swa_upper(n):
                mix_upper(mix_hi[:, 0:GROUP, n * WIN:(n + 1) * WIN],
                          ps[:, 7, :].rearrange("p (h q) -> p h q", h=GROUP), swa_out, n + 1)

            def even():
                for t in range(EVEN_IN):
                    n = S_EVEN + t
                    if t == 0:
                        root(stat(1), D)
                    split_next(n)
                    if t < SGT or t >= U_TILE:
                        act.wait_ge(acc_read, n + 1)
                        act.activation(pre[:, t, :], pre[:, t, :], ACT.Gelu).then_inc(gelu_done, 1)
                    if t == SGT + 5:
                        act.wait_ge(ln_var, 1)
                        act.activation(ln_sd[:, 0:4], ln_mv[:, 0:4, 1], ACT.Sqrt, bias=eps[:, 0:1])
                        act.activation(ln_sd[0:NS, 4:5], ln_mv[0:NS, 4, 1:2], ACT.Sqrt, bias=eps[0:NS, 0:1]).then_inc(ln_sd_done, 1)
                for g in range(SGT):
                    mix_upper(mix_hi[:, GROUP + g, :], (up if g % 2 else prod)[:], mix_ready, g + 1)
                    if g == 0:
                        swa_exps(0)
                act.wait_ge(v_turned, 1)
                act.activation(v_tok[:].rearrange("p n c -> p (n c)"), ps[:, 4, :], ACT.Copy).then_inc(v_tok_done, 1)
                act.activation(v_new[:].rearrange("p (a b) c -> p a (b c)", a=2), ps[0:DS, 5:7, :], ACT.Copy).then_inc(v_tok_done, 1)
                for n in range(BLOCKS):
                    swa_copies(n)
                    if n + 1 < BLOCKS:
                        swa_exps(n + 1)
                    else:
                        act.wait_ge(swa_max, 2 * BLOCKS + 1)
                        for g in range(2):
                            act.activation(prob_s[:, g, :], prob_s[:, g, :], ACT.Exp, bias=nmax[:, g:g + 1], accum_out=rsum[:, g:g + 1])
                        act.activation(esink[:, 0:2], dsink[:, 0:2], ACT.Exp).then_inc(swa_exp, 1)
                    swa_upper(n)
                act.wait_ge(swa_turned, swa_units(BLOCKS) + 1)
                act.activation(prob_st[:].rearrange("p g r -> p (g r)"), ps[:, 4, 0:2 * P], ACT.Copy).then_inc(swa_copied, 1)
                act.activation(prob_st2[:].rearrange("p g r -> p (g r)"), ps[0:DS, 5, 0:2 * P], ACT.Copy).then_inc(swa_copied, 1)
                act.wait_ge(swa_out, BLOCKS + 1)
                for kv in range(2):
                    r = kv * HD
                    last = act.activation(mix_hi[r:r + HD, 0:GROUP, SEQ:T].rearrange("p h (b t) -> p b h t", b=DB),
                                          ps[r:r + HD, 7, 0:DB * NS].rearrange("p (b g h t) -> p b g h t", b=DB, g=2, h=GROUP)[:, :, kv],
                                          ACT.Copy)
                last.then_inc(mix_hi_done, 1)
                mixer_out(EVEN_OUT, 1)

            def odd():
                for t in range(ODD_IN):
                    n = S_ODD + t
                    if t == 0:
                        root(stat(4), D)
                    if n == CKV0 + 1:
                        root(stat(4) + 1, Q_LORA)
                    split_next(n)
                    if t < 3 * CT and t % 3 == 2:
                        mix_upper(mix_hi[:, t // 3, :], prod[:], mix_ready, SGT + t // 3 + 1)
                    if CQ0 <= n < CKV0:
                        c = n - CQ0
                        act.wait_ge(acc_read, n + 1)
                        act.activation(cq_hi[:, c, :], (prod if c % 2 else silu)[:], ACT.Copy, scale=q_gain[:, c:c + 1]).then_inc(cq_hi_done, 1)
                for h in range(HEADS):
                    split_next(ODD_UQ + h)
                    if h == 0:
                        root(stat(4) + 2, KV_LORA)
                    if h == 1:
                        act.wait_ge(kpe_done, 1)
                        for hh in range(HEADS):
                            last = act.activation(kf[NOPE:QK, hh, :], kpe[NOPE:QK, 0:SEQ], ACT.Copy)
                        last.then_inc(kf_done, 1)
                for h in range(HEADS):
                    act.wait_ge(kf_ready, h // 2 + 1)
                    r = NOPE * (h % 2)
                    act.activation(kf[0:NOPE, h, :], ps[r:r + NOPE, 4 + h // 2 % 2, :], ACT.Copy).then_inc(kf_done, 1)
                def values_of(j):
                    act.wait_ge(vm_ready, j + 1)
                    act.activation(v_mla[:, j, :], ps[:, 7 - j % 2, :], ACT.Copy).then_inc(vm_done, 1)

                def exps(h):
                    for k, i in enumerate(BY_LENGTH):
                        act.wait_ge(mla_max, BLOCKS * h + k + 1)
                        s = i * (i + 1) // 2
                        act.activation(p_mla[:, s:s + i + 1, :].rearrange("p j k -> p (j k)"), ps[:, i, 0:(i + 1) * P], ACT.Exp,
                                       bias=nmx[:, i:i + 1], scale=MLA_SCALE, accum_out=sm[:, i:i + 1]).then_inc(mla_exp, 1)
                values_of(0)
                values_of(1)
                exps(0)
                values_of(2)
                values_of(3)
                for h in range(HEADS):
                    act.wait_ge(mla_turned, h + 1)
                    if h:
                        act.wait_ge(mla_out, h)
                    for c in range(3):
                        n = min(4, len(TURN_ORDER) - 4 * c)
                        act.activation(p_mla_t[:, 4 * c:4 * c + n, :].rearrange("p s q -> p (s q)"), ps[:, 4 + c, 0:n * P], ACT.Copy)\
                           .then_inc(mla_copied, 1)
                    if h + 1 < HEADS:
                        exps(h + 1)
                    r = VD * (h % 2)
                    mix_upper(mix_hi[r:r + VD, CT + h // 2, 0:SEQ], ps[r:r + VD, 7, :], mla_out, h + 1)

                def copy_new(half):
                    act.wait_ge(new_turned, half + 1)
                    act.activation(ckv_new[:, 4 * half:4 * half + 4, :].rearrange("p b c -> p (b c)"), ps_flat[0:DS, 6 * 512:8 * 512], ACT.Copy)\
                       .then_inc(new_copied, 1)
                copy_new(0)

                for b in range(DB + 1):
                    r = NS * ((b - 1) % 4)
                    for p in range(PAGES):
                        g = b * PAGES + p
                        if b < DB and p % 2:
                            act.wait_ge(page_turned, g + 1)
                            if g >= KT_SLOTS:
                                act.wait_ge(page_scored, g - KT_SLOTS + 1)
                            act.activation(keys_t[g % KT_SLOTS][:].rearrange("p j k -> p (j k)"), ps[0:QK, page_bank[g], 0:3 * PAGE], ACT.Copy)\
                               .then_inc(keys_copied[1], 1)
                        if b == 0 and p == 7:
                            copy_new(1)
                        if b and p == AT_EXP:
                            act.wait_ge(s_max, b)
                        if b and AT_EXP <= p < AT_EXP + 8 and p % 2 == 0:
                            q = (p - AT_EXP) // 2
                            act.activation(p_s[r:r + NS, q * 4 * PAGE:(q + 1) * 4 * PAGE], ps[r:r + NS, q, :], ACT.Exp,
                                           bias=nmx[r:r + NS, 3:4], scale=MLA_SCALE, accum_out=sm[r:r + NS, q:q + 1])
                        if b and p == AT_EXP + 6:
                            act.activation(p_s[r:r + NS, PAGES * PAGE:PAGES * PAGE + DS], s_new[r:r + NS, :], ACT.Exp,
                                           bias=nmx[r:r + NS, 3:4], scale=MLA_SCALE, accum_out=sm[r:r + NS, 4:5]).then_inc(s_exp, 1)
                        if b and p == AT_TURNED:
                            act.wait_ge(s_turned, b)
                            if b >= 3:
                                act.wait_ge(values_done, b - 2)
                            act.activation(p_st2[:, (b - 1) % 2, :], ps[0:DS, 7, KV_LORA + NS:KV_LORA + 2 * NS], ACT.Copy)
                            act.activation(p_st[(b - 1) % 2][:].rearrange("p j r -> p (j r)"), ps[:, 6, :], ACT.Copy).then_inc(s_copied, 1)
                mix_upper(mix_hi[:, CT:2 * CT, SEQ:T], ps[:, 4, 0:CT * NS].rearrange("p (h t) -> p h t", h=CT), s_out, 1)
                mixer_out(ODD_OUT, 4)

            act.wait_ge(gains_landed, 32)
            split_hi(0, 0, DT * P)
            for t in range(DT):
                if t % X_PIECE == 0:
                    act.wait_ge(x_landed[t // X_PIECE], 16)
                input_hi(0, t)
                if t >= POOL_TILES:
                    act.activation(late_square[t - POOL_TILES][:], x[:, t, :], ACT.Square).then_inc(late_squared, 1)
                if t == POOL_TILES:
                    split_hi(1, 1, DT * P)
            ffn(*FFNS[0])
            even()
            ffn(*FFNS[1])
            ffn(*FFNS[2])
            odd()
            ffn(*FFNS[3])
            root(stat(6), D)

        @block.vector
        def _(dve):
            steps = [0]

            def link(ins):
                steps[0] += 1
                ins.then_inc(step, 1)
                dve.wait_ge(step, steps[0])

            def split_lo(n, slot, cols):
                dve.wait_ge(w_hi_done, n + 1)
                dve.tensor_tensor(w_lo[slot][:, 0:cols], raw[slot][:, 0:cols], w_hi[slot][:, 0:cols].bitcast(F32),
                                  ALU.subtract).then_inc(w_lo_done, 1)

            def split_next(n):
                if n + 2 < N_PANELS:
                    split_lo(n + 2, n % 2, panel_cols(n + 2))

            def invert(k, out=None):
                dve.wait_ge(rms_done, k)
                dve.reciprocal((rinv if out is None else out)[:], rms[:]).then_inc(rinv_ready, 1)
                dve.wait_ge(rinv_ready, k)

            def scaled(n, out, by, rows=P):
                dve.wait_ge(panel_done, n + 1)
                dve.tensor_tensor(halves(out), acc_of(n % 2, rows), halves(by), ALU.mult).then_inc(acc_read, 1)

            def input_lo(norm, m):
                dve.wait_ge(hx_hi_done, DT * norm + m + 1)
                dve.scalar_tensor_tensor(out=tile_of(hx_lo, m), in0=tile_of(x, m), scalar=gains[:, norm, bass.ds(m, 1)],
                                         in1=tile_of(hx_hi, m).bitcast(F32), op0=ALU.mult, op1=ALU.subtract).then_inc(hx_done, 1)

            def add_to_x(n, slot, m, factor):
                dve.wait_ge(panel_done, n + 1)
                xm = halves(tile_of(x, m))
                dve.scalar_tensor_tensor(out=xm, in0=acc_of(slot), scalar=factor, in1=xm, op0=ALU.mult, op1=ALU.add)\
                   .then_inc(acc_read, 1)

            def mix_lower(piece, out, src, hi):
                dve.wait_ge(mix_hi_done, piece + 1)
                dve.tensor_tensor(out, src, hi.bitcast(F32), ALU.subtract).then_inc(mix_done, 1)

            def ffn(start, f, norm):
                for c in range(CHUNKS):
                    n0 = start + c * (2 * FT + DT)
                    h0 = (f * CHUNKS + c) * FT

                    def tile(i, cols):
                        dve.wait_ge(panel_done, n0 + 2 * i + 1)
                        dve.tensor_tensor(halves(gate[:]), acc_of(n0 % 2), halves(rinv[:]), ALU.mult).then_inc(acc_read, 1)
                        split_lo(n0 + 2 * i + 2, n0 % 2, cols)
                        dve.wait_ge(panel_done, n0 + 2 * i + 2)
                        dve.tensor_tensor(halves(up[:]), acc_of((n0 + 1) % 2), halves(rinv[:]), ALU.mult).then_inc(acc_read, 1)
                        dve.wait_ge(silu_done, h0 + i + 1)
                        dve.wait_ge(acc_read, n0 + 2 * i + 2)
                        dve.tensor_tensor(prod[:], up[:], silu[:], ALU.mult).then_inc(prod_ready, 1)
                        split_lo(n0 + 2 * i + 3, (n0 + 1) % 2, cols)
                        dve.wait_ge(hid_hi_done, h0 + i + 1)
                        dve.tensor_tensor(tile_of(hid_lo, i), prod[:], tile_of(hid_hi, i).bitcast(F32), ALU.subtract).then_inc(hid_done, 1)
                    if c == 0:
                        invert(stat(norm))
                    with dve.Fori(0, FT - 1) as i:
                        tile(i, DT * P)
                    tile(FT - 1, FT * P)
                    if n0 == 0:
                        dve.wait_ge(dist_ready, 1)
                        dve.tensor_copy(by_dist[:], ps[0:HEADS, 7, 0:3 * WIN]).then_inc(dist_copied, 1)
                    n1 = n0 + 2 * FT

                    def final_input(m):
                        if c == CHUNKS - 1 and norm + 1 < N_NORMS - 1:
                            input_lo(norm + 1, m)
                    with dve.Fori(0, DT // 2 - 1) as i:
                        for s in range(2):
                            add_to_x(n1 + 2 * i + s, (n1 + s) % 2, 2 * i + s, 0.5)
                            split_lo(n1 + 2 * i + s + 2, (n1 + s) % 2, FT * P)
                            final_input(2 * i + s)
                    for m in (DT - 2, DT - 1):
                        add_to_x(n1 + m, (n1 + m) % 2, m, 0.5)
                        split_next(n1 + m)
                        final_input(m)

            def mixer_out(start, norm):
                for m in range(DT):
                    add_to_x(start + m, (start + m) % 2, m, 1.0)
                    split_next(start + m)
                    input_lo(norm + 1, m)

            def turned_g(tt):
                rows = P if tt < BLOCKS else NS
                dve.wait_ge(g_turned, tt + 1)
                dve.tensor_copy(v_ln[0:rows, tt, :], ps[0:rows, 4 + tt % 4, :]).then_inc(v_ln_read, 1)
                dve.wait_ge(v_ln_read, tt + 1)
                link(dve.bn_stats(ln_st[0:rows, :], v_ln[0:rows, tt, :]))
                stats_of = dve.bn_aggr(ln_mv[0:rows, tt, :], ln_st[0:rows, :])
                if tt == BLOCKS:
                    stats_of.then_inc(ln_var, 1)
                else:
                    link(stats_of)

            def normed_g(tt):
                rows = P if tt < BLOCKS else NS
                v = v_ln[0:rows, tt, :]
                link(dve.tensor_scalar(v, v, ln_mv[0:rows, tt, 0:1], ln_r[0:rows, tt:tt + 1], ALU.subtract, ALU.mult))
                link(dve.tensor_tensor(v, v, ln_g[0:rows, :], ALU.mult))
                dve.tensor_tensor(v, v, ln_b[0:rows, :], ALU.add).then_inc(v_ln_done, 1)

            def gated(g):
                out = (up if g % 2 else prod)
                dve.wait_ge(gate_sum, g + 1)
                dve.wait_ge(gelu_done, SGT + g + 1)
                if g >= 2:
                    dve.wait_ge(mix_done, SGU_PIECE + g - 1)
                b0 = 4 + 2 * (g % 2)
                dve.tensor_tensor(out[:, 0:SEQ], ps[:, b0, :], pre[:, U_TILE + g, 0:SEQ], ALU.mult)
                dve.tensor_tensor(out[:, SEQ:T], ps[:, b0 + 1, 0:NS], pre[:, U_TILE + g, SEQ:T], ALU.mult).then_inc(mix_ready, 1)

            def gated_lower(g):
                mix_lower(SGU_PIECE + g, mix_lo[:, GROUP + g, :], (up if g % 2 else prod)[:], mix_hi[:, GROUP + g, :])

            def swa_softmax_in(n):
                lo = swa_halves(n)[0] * WIN
                if n >= 2:
                    dve.wait_ge(swa_turned, swa_units(n - 1))
                for kv in range(2):
                    four = slice(kv * GROUP, (kv + 1) * GROUP)
                    dve.wait_ge(swa_scored, 2 * n + kv + 1)
                    scores = ps_flat[:, 0:HEADS * 2 * WIN].rearrange("p (h k) -> p h k", h=HEADS)
                    dve.scalar_tensor_tensor(out=prob[n % 2][:, four, lo:2 * WIN], in0=scores[:, four, lo:2 * WIN], scalar=SWA_SCALE,
                                             in1=bias[:, four, lo:2 * WIN], op0=ALU.mult, op1=ALU.add).then_inc(swa_biased, 1)
                for kv in range(2):
                    four = slice(kv * GROUP, (kv + 1) * GROUP)
                    dve.wait_ge(swa_biased, 2 * n + kv + 1)
                    link(dve.tensor_reduce(smax[:, four], prob[n % 2][:, four, lo:2 * WIN], AX, ALU.max))
                    link(dve.tensor_tensor(smax[:, four], smax[:, four], sink[:, four], ALU.max))
                    dve.tensor_scalar(nmax[:, four], smax[:, four], -1.0, None, ALU.mult)
                    dve.tensor_tensor(dsink[:, four], sink[:, four], smax[:, four], ALU.subtract).then_inc(swa_max, 1)

            def swa_softmax_out(n):
                lo = swa_halves(n)[0] * WIN
                for kv in range(2):
                    four = slice(kv * GROUP, (kv + 1) * GROUP)
                    dve.wait_ge(swa_exp, 2 * n + kv + 1)
                    link(dve.tensor_tensor(rsum[:, four], rsum[:, four], esink[:, four], ALU.add))
                    link(dve.reciprocal(rden[:, four], rsum[:, four]))
                    for h in range(kv * GROUP, (kv + 1) * GROUP):
                        p = prob[n % 2][:, h, lo:2 * WIN]
                        last = dve.tensor_scalar(p, p, rden[:, h:h + 1], None, ALU.mult)
                    last.then_inc(swa_prob, 1)

            def swa_lower(n):
                mix_lower(SWA_PIECE + n, mix_lo[:, 0:GROUP, n * WIN:(n + 1) * WIN],
                          ps[:, 7, :].rearrange("p (h q) -> p h q", h=GROUP), mix_hi[:, 0:GROUP, n * WIN:(n + 1) * WIN])

            def sample_softmax_in():
                dve.wait_ge(swa_scored, 2 * BLOCKS + 1)
                for g in range(2):
                    last = dve.scalar_tensor_tensor(out=prob_s[:, g, :], in0=ps[:, g, 0:WIN + DS], scalar=SWA_SCALE, in1=bias_s[:],
                                                    op0=ALU.mult, op1=ALU.add)
                link(last)
                link(dve.tensor_reduce(smax[:, 0:2], prob_s[:], AX, ALU.max))
                link(dve.tensor_scalar(smax[:, 0:2], smax[:, 0:2], sink_s[:, 0:1], None, ALU.max))
                link(dve.tensor_scalar(nmax[:, 0:2], smax[:, 0:2], -1.0, None, ALU.mult))
                dve.tensor_scalar(dsink[:, 0:2], nmax[:, 0:2], sink_s[:, 0:1], None, ALU.add).then_inc(swa_max, 1)

            def sample_softmax_out():
                dve.wait_ge(swa_exp, 2 * BLOCKS + 1)
                link(dve.tensor_tensor(rsum[:, 0:2], rsum[:, 0:2], esink[:, 0:2], ALU.add))
                link(dve.reciprocal(rden[:, 0:2], rsum[:, 0:2]))
                for g in range(2):
                    last = dve.tensor_scalar(prob_s[:, g, :], prob_s[:, g, :], rden[:, g:g + 1], None, ALU.mult)
                last.then_inc(swa_prob, 1)

            def even():
                for t in range(EVEN_IN):
                    n = S_EVEN + t
                    if t == 0:
                        invert(stat(1))
                        dve.wait_ge(even_landed, EVEN_LOADS)
                    scaled(n, pre[:, t, :], rinv[:])
                    split_next(n)
                    if t == 1:
                        link(dve.memset(q_bd[:], 0.0))
                    if SGT + 1 <= t <= SGT + 5:
                        turned_g(t - SGT - 1)
                    if t == SGT + 6:
                        dve.wait_ge(ln_sd_done, 1)
                        link(dve.reciprocal(ln_r[:, 0:4], ln_sd[:, 0:4]))
                        link(dve.reciprocal(ln_r[0:NS, 4:5], ln_sd[0:NS, 4:5]))
                        normed_g(0)
                        normed_g(1)
                    if t == U_TILE - 1:
                        for kv in range(2):
                            r = kv * HD
                            last = dve.tensor_copy(
                                q_bd[r:r + HD, :, kv * GROUP * DS:(kv + 1) * GROUP * DS].rearrange("p b (h t) -> p b h t", h=GROUP),
                                pre[r:r + HD, Q_TILE:K_TILE, SEQ:T].rearrange("p h (b t) -> p b h t", b=DB))
                        last.then_inc(q_bd_ready, 1)
                    if t == SGT + 7:
                        normed_g(2)
                        normed_g(3)
                    if t == SGT + 8:
                        normed_g(4)
                for g in range(SGT):
                    gated(g)
                    if g == 0:
                        swa_softmax_in(0)
                    else:
                        gated_lower(g - 1)
                gated_lower(SGT - 1)
                swa_softmax_out(0)
                for n in range(BLOCKS):
                    if n + 1 < BLOCKS:
                        swa_softmax_in(n + 1)
                        swa_softmax_out(n + 1)
                    else:
                        sample_softmax_in()
                        sample_softmax_out()
                    swa_lower(n)
                for kv in range(2):
                    r = kv * HD
                    if kv == 0:
                        dve.wait_ge(mix_hi_done, SWA_S_PIECE + 1)
                    last = dve.tensor_tensor(mix_lo[r:r + HD, 0:GROUP, SEQ:T].rearrange("p h (b t) -> p b h t", b=DB),
                                             ps[r:r + HD, 7, 0:DB * NS].rearrange("p (b g h t) -> p b g h t", b=DB, g=2, h=GROUP)[:, :, kv],
                                             mix_hi[r:r + HD, 0:GROUP, SEQ:T].bitcast(F32).rearrange("p h (b t) -> p b h t", b=DB), ALU.subtract)
                last.then_inc(mix_done, 1)
                mixer_out(EVEN_OUT, 1)

            def convolve(t):
                zs = conv_zs[:, t]
                out = prod[:, 0:SEQ]
                out_s = prod[:, SEQ:T].rearrange("p (b s) -> p b s", b=DB)
                link(dve.tensor_scalar(out, conv_z[:, t, 0:SEQ], conv_w[:, 0, t:t + 1], None, ALU.mult))
                link(dve.tensor_scalar(out_s, zs[:, :, 0:DS], conv_w[:, 0, t:t + 1], None, ALU.mult))
                for j in range(1, 3):
                    link(dve.scalar_tensor_tensor(out=out, in0=conv_z[:, t, j:j + SEQ], scalar=conv_w[:, j, t:t + 1], in1=out,
                                                  op0=ALU.mult, op1=ALU.add))
                    link(dve.scalar_tensor_tensor(out=out_s, in0=zs[:, :, j:j + DS], scalar=conv_w[:, j, t:t + 1], in1=out_s,
                                                  op0=ALU.mult, op1=ALU.add))
                dve.tensor_tensor(prod[:], prod[:], silu[:], ALU.mult).then_inc(mix_ready, 1)

            def rope(t2d, count):
                r = slice(NOPE, QK)
                dve.wait_ge(rotated, count)
                dve.tensor_tensor(halves(silu[r, :]), ps[r, 6:8, 0:TH], halves(sin[r, :]), ALU.mult)
                link(dve.tensor_tensor(prod[r, :], t2d, cos[r, :], ALU.mult))
                return dve.tensor_tensor(t2d, prod[r, :], silu[r, :], ALU.add)

            def mark(ins):
                steps[0] += 1
                ins.then_inc(step, 1)
                return steps[0]

            def mla_maxima(h):
                masked, found = {}, {}
                for k in range(BLOCKS + 2):
                    if k < BLOCKS:
                        i = BY_LENGTH[k]
                        diag = ps[:, i, i * P:(i + 1) * P]
                        dve.wait_ge(mla_scored, BLOCKS * h + k + 1)
                        masked[k] = mark(dve.tensor_tensor(diag, diag, causal[:], ALU.add))
                    if 1 <= k <= BLOCKS:
                        i = BY_LENGTH[k - 1]
                        dve.wait_ge(step, masked[k - 1])
                        found[k - 1] = mark(dve.tensor_reduce(mx[:, i:i + 1], ps[:, i, 0:(i + 1) * P], AX, ALU.max))
                    if k >= 2:
                        i = BY_LENGTH[k - 2]
                        dve.wait_ge(step, found[k - 2])
                        dve.tensor_scalar(nmx[:, i:i + 1], mx[:, i:i + 1], -MLA_SCALE, None, ALU.mult).then_inc(mla_max, 1)

            def mla_normalise(h):
                inverse = {}
                for k in range(BLOCKS + 1):
                    if k < BLOCKS:
                        i = BY_LENGTH[k]
                        dve.wait_ge(mla_exp, BLOCKS * h + k + 1)
                        inverse[k] = mark(dve.reciprocal(rs[:, i:i + 1], sm[:, i:i + 1]))
                    if k:
                        i = BY_LENGTH[k - 1]
                        p = p_mla[:, i * (i + 1) // 2:(i + 1) * (i + 2) // 2, :].rearrange("p j k -> p (j k)")
                        dve.wait_ge(step, inverse[k - 1])
                        dve.tensor_scalar(p, p, rs[:, i:i + 1], None, ALU.mult).then_inc(mla_prob, 1)

            def mla_lower(h):
                r = VD * (h % 2)
                mix_lower(MLA_PIECE + h, mix_lo[r:r + VD, CT + h // 2, 0:SEQ], ps[r:r + VD, 7, :], mix_hi[r:r + VD, CT + h // 2, 0:SEQ])

            def sample_max(b, q):
                r = NS * (b % 4)
                dve.wait_ge(page_scored, b * PAGES + 4 * q + 4)
                return dve.tensor_reduce(mx[r:r + NS, q:q + 1], ps[r:r + NS, q, :], AX, ALU.max)

            def sample_maxima(b):
                r = slice(NS * (b % 4), NS * (b % 4) + NS)
                sample_max(b, 3)
                dve.wait_ge(s_new_ready, b + 1)
                link(dve.tensor_tensor(s_new[r, :], ps[r, 7, KV_LORA:KV_LORA + DS], causal_s[r, :], ALU.add))
                link(dve.tensor_reduce(mx[r, 4:5], s_new[r, :], AX, ALU.max))
                link(dve.tensor_reduce(mx[r, 5:6], mx[r, 0:5], AX, ALU.max))
                dve.tensor_scalar(nmx[r, 3:4], mx[r, 5:6], -MLA_SCALE, None, ALU.mult).then_inc(s_max, 1)

            def sample_tokens(b):
                r = slice(NS * (b % 4), NS * (b % 4) + NS)
                dve.wait_ge(values_done, b + 1)
                link(dve.tensor_reduce(rs[r, 0:1], sm[r, 0:5], AX, ALU.add))
                link(dve.reciprocal(rs[r, 1:2], rs[r, 0:1]))
                dve.tensor_scalar(o_tok[r, :], ps[r, 7, 0:KV_LORA], rs[r, 1:2], None, ALU.mult).then_inc(o_tok_done, 1)

            def sample_latents(g):
                dve.wait_ge(o_turned, g + 1)
                for c in range(KT):
                    last = dve.tensor_copy(o_lat[:, c].rearrange("p h (b t) -> p b h t", b=DB)[:, 4 * g:4 * g + 4],
                                           ps[:, 6, c * P:(c + 1) * P].rearrange("p (b h t) -> p b h t", b=4, h=HEADS))
                last.then_inc(o_lat_done, 1)

            def sample():
                for b in range(DB + 1):
                    for p in range(PAGES):
                        g = b * PAGES + p
                        if b < DB and p % 2 == 0:
                            dve.wait_ge(page_turned, g + 1)
                            if g >= KT_SLOTS:
                                dve.wait_ge(page_scored, g - KT_SLOTS + 1)
                            dve.tensor_copy(keys_t[g % KT_SLOTS][:].rearrange("p j k -> p (j k)"), ps[0:QK, page_bank[g], 0:3 * PAGE])\
                               .then_inc(keys_copied[0], 1)
                        if b < DB and p in (7, 11, 15):
                            sample_max(b, p // 4 - 1)
                        if b and p == AT_MAX:
                            sample_maxima(b - 1)
                        if b and p == AT_OUT:
                            sample_tokens(b - 1)
                        if b == 5 and p == 2:
                            sample_latents(0)
                sample_latents(1)

            def odd():
                for t in range(ODD_IN):
                    n = S_ODD + t
                    if t == 0:
                        invert(stat(4))
                        dve.wait_ge(odd_landed, ODD_LOADS)
                        link(dve.memset(conv_z[:, :, 0:2], 0.0))
                    if t < 3 * CT:
                        scaled(n, (gate, up, silu)[t % 3][:], rinv[:])
                        split_next(n)
                        dve.wait_ge(acc_read, n + 1)
                        if t % 3 == 1:
                            link(dve.tensor_tensor(conv_z[:, t // 3, 2:SEQ + 2], gate[:, 0:SEQ], up[:, 0:SEQ], ALU.mult))
                            link(dve.tensor_tensor(conv_zs[:, t // 3, :, 2:DS + 2], gate[:, SEQ:T].rearrange("p (b s) -> p b s", b=DB),
                                                   up[:, SEQ:T].rearrange("p (b s) -> p b s", b=DB), ALU.mult))
                        if t % 3 == 2:
                            convolve(t // 3)
                            mix_lower(CONV_PIECE + t // 3, mix_lo[:, t // 3, :], prod[:], mix_hi[:, t // 3, :])
                    elif n < CKV0:
                        c = n - CQ0
                        if c >= 2:
                            dve.wait_ge(square_done, sumsq_steps(4) + c - 1)
                        buf = prod if c % 2 else silu
                        scaled(n, buf[:], rinv[:])
                        split_next(n)
                        dve.wait_ge(cq_hi_done, c + 1)
                        dve.wait_ge(acc_read, n + 1)
                        dve.scalar_tensor_tensor(out=cq_lo[:, c, :], in0=buf[:], scalar=q_gain[:, c:c + 1], in1=cq_hi[:, c, :].bitcast(F32),
                                                 op0=ALU.mult, op1=ALU.subtract).then_inc(cq_done, 1)
                    else:
                        if n == KPE:
                            invert(stat(4) + 1, gate)
                        scaled(n, kpe[:] if n == KPE else ckv[:, n - CKV0, :], rinv[:])
                        split_next(n)
                for h in range(HEADS):
                    n = ODD_UQ + h
                    dve.wait_ge(panel_done, n + 1)
                    dve.tensor_tensor(halves(qf[0:QK, h, :]), acc_of(n % 2, QK), halves(gate[0:QK, :]), ALU.mult).then_inc(acc_read, 1)
                    split_next(n)
                    if h == 0:
                        dve.wait_ge(spare_landed, 48)
                        rope(kpe[NOPE:QK, :], 1).then_inc(kpe_done, 1)
                    else:
                        rope(qf[NOPE:QK, h - 1, :], h + 1).then_inc(q_done, 1)
                    if h == 1:
                        invert(stat(4) + 2, up)
                    if h == 2:
                        dve.wait_ge(square_done, sumsq_steps(4) + QT + KT)
                        for c in range(KT):
                            dve.scalar_tensor_tensor(out=ckv[:, c, :], in0=ckv[:, c, :], scalar=kv_gain[:, c:c + 1], in1=up[:],
                                                     op0=ALU.mult, op1=ALU.mult).then_inc(ckv_done, 1)
                rope(qf[NOPE:QK, HEADS - 1, :], HEADS + 1).then_inc(q_done, 1)
                mla_maxima(0)
                dve.wait_ge(qa_ready, 1)
                for j in range(3):
                    rows = QK if j < 2 else NOPE
                    src = ps[0:rows, 4, j * HEADS * NS:(j + 1) * HEADS * NS] if j < 2 else ps[0:rows, 5, 0:HEADS * NS]
                    dve.tensor_copy(qa[0:rows, j].rearrange("p b (h t) -> p b h t", h=HEADS), src.rearrange("p (h b t) -> p b h t", h=HEADS, b=DB))
                for c in range(KT):
                    dve.tensor_copy(qa_new[:, c].rearrange("p b (h t) -> p b h t", h=HEADS),
                                    ps[:, 6, c * HEADS * NS:(c + 1) * HEADS * NS].rearrange("p (h b t) -> p b h t", h=HEADS, b=DB))
                dve.tensor_copy(qa[NOPE:QK, 2].rearrange("p b (h t) -> p b h t", h=HEADS),
                                qf[NOPE:QK, :, SEQ:T].rearrange("p h (b t) -> p b h t", b=DB)).then_inc(qa_done, 1)
                mla_normalise(0)
                for h in range(HEADS):
                    if h + 1 < HEADS:
                        mla_maxima(h + 1)
                        mla_normalise(h + 1)
                    mla_lower(h)
                sample()
                mix_lower(MLA_S_PIECE, mix_lo[:, CT:2 * CT, SEQ:T], ps[:, 4, 0:CT * NS].rearrange("p (h t) -> p h t", h=CT), mix_hi[:, CT:2 * CT, SEQ:T])
                mixer_out(ODD_OUT, 4)

            dve.wait_ge(gains_landed, 32)
            split_lo(0, 0, DT * P)
            for t in range(DT):
                if t % X_PIECE == 0:
                    dve.wait_ge(x_landed[t // X_PIECE], 16)
                input_lo(0, t)
                if t > POOL_TILES:
                    dve.wait_ge(late_squared, t - POOL_TILES + 1)
                    total = dve.tensor_tensor(up[:], up[:], late_square[t - POOL_TILES][:], ALU.add)
                    if t < DT - 1:
                        link(total)
                    else:
                        total.then_inc(others_added, 1)
                if t == POOL_TILES:
                    split_lo(1, 1, DT * P)
            ffn(*FFNS[0])
            even()
            ffn(*FFNS[1])
            ffn(*FFNS[2])
            odd()
            ffn(*FFNS[3])
            dve.wait_ge(acc_read, N_PANELS)
            dve.tensor_tensor(up[:], x[:, DT - 1, :], x[:, DT - 1, :], ALU.mult).then_inc(others_added, 1)
            invert(stat(6))
            for t in range(DT):
                dve.scalar_tensor_tensor(out=y[:, t, :], in0=x[:, t, :], scalar=gains[:, N_NORMS - 1, t:t + 1], in1=rinv[:],
                                         op0=ALU.mult, op1=ALU.mult).then_inc(y_done, 1)

        @block.gpsimd
        def _(pool):
            def add_square(k, src, first):
                pool.tensor_tensor(sumsq[:] if first else square[:], src, src, ALU.mult).then_inc(square_done, 1)
                pool.wait_ge(square_done, k + 1)
                if first:
                    pool.nop().then_inc(sumsq_step, 1)
                else:
                    pool.tensor_tensor(sumsq[:], sumsq[:], square[:], ALU.add).then_inc(sumsq_step, 1)

            def x_squares(k0, n1, tiles=DT):
                pool.wait_ge(acc_read, n1 + 1)
                add_square(k0, x[:, 0, :], True)
                with pool.Fori(1, tiles) as m:
                    pool.wait_ge(acc_read, n1 + m + 1)
                    pool.wait_ge(sumsq_step, k0 + m)
                    add_square(k0 + m, tile_of(x, m), False)

            def ffn_end(start):
                return start + CHUNKS * (2 * FT + DT) - DT

            for t, name in ((ones, "ones"), (ident, "ident")):
                pool.dma_start(t[:], d[name]).then_inc(consts_landed, 16)
            for t, name in ((rel, "rel"), (onehot, "onehot")):
                pool.dma_start(t[:], d[name]).then_inc(rel_landed, 16)
            for t in range(POOL_TILES):
                if t % X_PIECE == 0:
                    pool.wait_ge(x_landed[t // X_PIECE], 16)
                if t:
                    pool.wait_ge(sumsq_step, t)
                add_square(t, x[:, t, :], t == 0)
            pool.wait_ge(dist_copied, 1)
            pool.dma_start(d["dist"], by_dist[:].unsqueeze(1).to_broadcast([HEADS, P, 3 * WIN])).then_inc(dist_stored, 16)
            pool.wait_ge(dist_stored, 16)
            dist = d["dist"]
            row = P * 3 * WIN
            pool.dma_start(bias[:], bass.AP(dist.tensor, P - 1, [[3 * WIN - 1, P], [row, HEADS], [1, 2 * WIN]])).then_inc(even_landed, 16)
            for b4 in range(4):
                pool.dma_start(bias_s[b4 * NS:(b4 + 1) * NS, :], bass.AP(dist.tensor, P - 1, [[row, HEADS], [3 * WIN - 1, DS], [1, WIN + DS]]))\
                    .then_inc(even_landed, 16)
            for t, name in ((sgu_w, "sgu_w"), (sgu_ws, "sgu_ws"), (sgu_b, "sgu_b"), (sgu_bs, "sgu_bs"), (ln_g, "ln_g"), (ln_b, "ln_b"),
                            (sink, "sink")):
                src = d[name] if name not in ("ln_g", "ln_b", "sink") else d[name].partition_broadcast(P)
                pool.dma_start(t[:], src).then_inc(even_landed, 16)
            for b4 in range(4):
                pool.dma_start(sink_s[b4 * NS:(b4 + 1) * NS, :], d["sink_s"]).then_inc(even_landed, 16)
            pool.wait_ge(even_landed, EVEN_LOADS)
            pool.affine_select(out=sgu_w[:], in_=sgu_w[:], compare_op=ALU.is_ge, fill=0.0, base=0, pattern=[[0, SGT], [1, P]],
                               channel_multiplier=-1).then_inc(sgu_masked, 1)
            pool.affine_select(out=sgu_ws[:], in_=sgu_ws[:], compare_op=ALU.is_ge, fill=0.0, base=0, pattern=[[0, SGT], [1, NS]],
                               channel_multiplier=-1).then_inc(sgu_masked, 1)
            x_squares(sumsq_steps(0), ffn_end(START["f0"]))
            pool.wait_ge(panel_done, S_EVEN)
            for t, name in ((k_cache, "k_cache"), (v_cache, "v_cache")):
                pool.dma_start(t[:], d[name]).then_inc(cache_landed, 16)
            pool.wait_ge(acc_read, EVEN_OUT)
            for name, t, c0, c1 in (("o_kp", K_TILE, SEQ - WIN, SEQ), ("o_vp", V_TILE, SEQ - WIN, SEQ),
                                     ("o_ks", K_TILE, SEQ, T), ("o_vs", V_TILE, SEQ, T)):
                pool.dma_start(d[name], pre[:, t, c0:c1]).then_inc(stored_even, 16)
            pool.wait_ge(v_ln_done, 5)
            pool.dma_start(d["o_sgu"], v_ln[0:NS, 4, :]).then_inc(stored_even, 16)
            x_squares(sumsq_steps(1), EVEN_OUT)
            pool.wait_ge(mix_done, EVEN_PIECES)
            pool.wait_ge(stored_even, 16 * 5)
            for t, name in ((w_uk, "w_uk"), (w_uv, "w_uv"), (perm, "perm"), (conv_w, "conv_w"), (q_gain, "q_gain"), (kv_gain, "kv_gain"),
                            (causal, "causal"), (causal_s, "causal_s")):
                pool.dma_start(t[:], d[name]).then_inc(odd_landed, 16)
            for t in range(CT):
                pool.dma_start(conv_zs[:, t, :, 0:2], d["conv_state"][:, t]).then_inc(odd_landed, 16)
            pool.dma_start(table[:], d["table"]).then_inc(table_landed, 16)
            x_squares(sumsq_steps(2), ffn_end(START["f1"]))
            x_squares(sumsq_steps(3), ffn_end(START["f2"]))
            pool.wait_ge(panel_done, S_ODD)
            for t, name in ((w_uk_t, "w_uk_t"), (cos, "cos"), (sin, "sin")):
                pool.dma_start(t[:], d[name]).then_inc(spare_landed, 16)
            for c in range(QT):
                k = sumsq_steps(4) + c
                pool.wait_ge(acc_read, CQ0 + c + 1)
                if c:
                    pool.wait_ge(sumsq_step, k)
                add_square(k, (prod if c % 2 else silu)[:], c == 0)
            for c in range(KT):
                k = sumsq_steps(4) + QT + c
                pool.wait_ge(acc_read, CKV0 + c + 1)
                if c == 0:
                    pool.wait_ge(stat_ready, stat(4) + 1)
                else:
                    pool.wait_ge(sumsq_step, k)
                add_square(k, ckv[:, c, :], c == 0)
            pool.dma_start(d["o_convp"], conv_z[:, :, SEQ:SEQ + 2]).then_inc(stored_conv, 16)
            pool.dma_start(d["o_convs"], conv_zs[:, :, :, DS:DS + 2]).then_inc(stored_conv, 16)
            pool.wait_ge(ckv_done, KT)
            pool.dma_start(d["o_ckv"], ckv[:]).then_inc(stored_odd, 16)
            pool.wait_ge(kpe_done, 1)
            pool.dma_start(d["o_kpe"], kpe[NOPE:QK, :]).then_inc(stored_odd, 16)
            for u in range(UNITS):
                if u % UNIT_SLOTS % 3 == 2:
                    load_pages(pool, u)
            x_squares(sumsq_steps(4) + QT + KT, ODD_OUT)
            x_squares(sumsq_steps(5), ffn_end(START["f3"]), DT - 1)


def rope_tables():
    half = ROPE // 2
    pos = np.concatenate([np.arange(SEQ), np.tile(PAGES * PAGE + np.arange(DS), DB)]).astype(np.float32)
    inv = np.exp(np.float32(-np.log(10000.0)) * np.arange(half, dtype=np.float32) / np.float32(half)).astype(np.float32)
    ang = pos[None, :] * inv[:, None]
    cos, sin = (np.tile(f(ang).astype(np.float32), (2, 1)) for f in (np.cos, np.sin))
    swap = np.zeros((ROPE, ROPE), np.float32)
    for i in range(half):
        swap[half + i, i] = -1.0
        swap[i, half + i] = 1.0
    return cos, sin, swap


def constants():
    c = {"ident": np.eye(P, dtype=np.float32), "ones": np.ones((P, P), np.float32), "eps": np.full((P, 1), EPS, np.float32)}
    dist = 2 * WIN - 1 - np.arange(3 * WIN)
    n = np.maximum(dist, 0)
    exact = BUCKETS // 2
    large = exact + (np.log(np.maximum(n, 1).astype(np.float32) / exact) / np.log(WIN / exact) * (BUCKETS - exact)).astype(np.int32)
    bucket = np.where(n < exact, n, np.minimum(large, BUCKETS - 1))
    bucket = np.where((dist >= 0) & (dist <= WIN), bucket, BUCKETS)
    c["onehot"] = (bucket[None, :] == np.arange(BUCKETS + 1)[:, None]).astype(np.float32)
    cos, sin, swap = rope_tables()
    pad = lambda a: np.concatenate([np.zeros((NOPE, a.shape[1]), np.float32), a, np.zeros((P - QK, a.shape[1]), np.float32)])
    c["cos"], c["sin"], c["perm"] = pad(cos), pad(sin), pad(swap)
    q = np.arange(P)
    c["causal"] = np.where(q[None, :] <= q[:, None], 0.0, NEG).astype(np.float32)
    c["causal_s"] = np.where(np.arange(DS)[None, :] <= (q % DS)[:, None], 0.0, NEG).astype(np.float32)
    return c


def panels(w, m=P):
    *lead, k, cols = w.shape
    w = w.reshape(*lead, k // P, P, cols // m, m)
    n = len(lead)
    w = w.transpose(*range(n), n + 2, n + 1, n, n + 3)
    return np.ascontiguousarray(w).reshape(*lead, cols // m, P, k // P * m)


def features(v):
    v = v.reshape(*v.shape[:-1], v.shape[-1] // P, P)
    return np.ascontiguousarray(np.moveaxis(v, -1, 0))


def layout(i):
    a = constants()
    tok = np.concatenate([i["x_prompt"].reshape(SEQ, D), i["x_sample"].reshape(NS, D)], 0)
    a["xT"] = tok.T.reshape(DT, P, T).transpose(1, 0, 2)
    for f in (1, 2):
        g, u = panels(i[f"ffn{f}_w_gate"]), panels(i[f"ffn{f}_w_up"])
        a[f"gu{f}"] = np.stack([g, u], 2)
        dn = i[f"ffn{f}_w_down"]
        a[f"down{f}"] = panels(dn.reshape(dn.shape[0], CHUNKS, FT * P, D))
    a["gains"] = features(np.stack([i["ffn1_norm"][0], i["mix_norm"][0], i["ffn2_norm"][0], i["ffn1_norm"][1], i["mix_norm"][1],
                                    i["ffn2_norm"][1], i["final_norm"]]))
    q_w, kv_w = HEADS * HD, 2 * HD
    pair = np.concatenate([np.r_[t * HD:(t + 1) * HD, (GROUP + t) * HD:(GROUP + t + 1) * HD] for t in range(GROUP)])
    w = i["even_w_in"][0]
    u0 = q_w + 2 * kv_w
    order = np.concatenate([np.arange(u0 + SGW, u0 + 2 * SGW), pair, np.arange(q_w, u0), np.arange(u0, u0 + SGW)])
    a["even_in"] = panels(w[:, order])
    a["even_out"] = panels(i["even_w_out"][0][np.concatenate([pair, np.arange(q_w, q_w + SGW)])])
    a["rel"] = np.concatenate([i["rel_bias"], np.full((1, HEADS), NEG, np.float32)])
    a["sink"] = i["attn_sinks"][0]
    a["sink_s"] = np.repeat(i["attn_sinks"][0], DS)[:, None]
    a["ln_g"], a["ln_b"] = i["sgu_ln_g"][0], i["sgu_ln_b"][0]
    sw = i["sgu_w"][0]
    a["sgu_w"] = sw.transpose(2, 0, 1)
    ws = np.zeros((NS, SGT, NS), np.float32)
    for b in range(DB):
        ws[b * DS:(b + 1) * DS, :, b * DS:(b + 1) * DS] = sw[:, :DS, :DS].transpose(2, 0, 1)
    a["sgu_ws"] = ws
    a["sgu_b"] = i["sgu_b"]
    a["sgu_bs"] = np.tile(i["sgu_b"][:, :, :DS], (1, 1, DB))
    k, v = i["cache_swa_k"][0].reshape(DB, WIN, P), i["cache_swa_v"][0].reshape(DB, WIN, P)
    a["k_nat"], a["v_nat"] = k, v
    a["k_cache"], a["v_cache"] = k.transpose(2, 0, 1), v.transpose(1, 0, 2)
    c_w = CT * P
    w = i["odd_w_in"][0]
    tiles = [np.arange(s * c_w + t * P, s * c_w + (t + 1) * P) for t in range(CT) for s in (1, 2, 0)]
    k0 = 3 * c_w + Q_LORA + KV_LORA
    order = np.concatenate(tiles + [np.arange(3 * c_w, k0)] + [np.arange(k0, k0 + ROPE)] * 4)
    a["odd_in"] = panels(w[:, order])
    a["odd_out"] = panels(i["odd_w_out"][0])
    a["w_uq"] = panels(i["mla_w_uq"][0], QK)
    a["q_gain"], a["kv_gain"] = features(i["mla_q_norm"][0]), features(i["mla_kv_norm"][0])
    uk, uv = i["mla_w_uk"][0], i["mla_w_uv"][0]
    a["w_uk"] = uk.reshape(KT, P, HEADS * NOPE).transpose(1, 0, 2)
    a["w_uv"] = uv.reshape(KT, P, HEADS * VD).transpose(1, 0, 2)
    a["w_uk_t"] = uk.transpose(2, 1, 0)
    a["conv_w"] = features(i["conv_w"][0])
    a["conv_state"] = i["state_conv"][0].reshape(DB, 2, CT, P).transpose(3, 2, 0, 1)
    a["page_pool"] = np.concatenate([i["cache_mla_ckv"][0], i["cache_mla_kpe"][0]], -1)
    a["table"] = i["page_table"].reshape(1, DB * PAGES)
    return {k: np.ascontiguousarray(v) for k, v in a.items()}


OUTPUTS = {"o_y": (P, DT, T), "o_kp": (P, WIN), "o_vp": (P, WIN), "o_ks": (P, NS), "o_vs": (P, NS), "o_kc": (DB, WIN - DS, P),
           "o_vc": (DB, WIN - DS, P), "o_sgu": (NS, SGW), "o_convp": (P, CT, 2), "o_convs": (P, CT, DB, 2), "o_ckv": (P, KT, T),
           "o_kpe": (ROPE, T)}


def results(o):
    y = o["o_y"].transpose(2, 1, 0).reshape(T, D)
    heads = (2, HD)

    def window(cached, new):
        new = new.T.reshape(DB, DS, P)
        return np.concatenate([cached, new], 1).reshape(1, DB, WIN, *heads)
    ckv = o["o_ckv"].transpose(2, 1, 0).reshape(T, KV_LORA)
    kpe = o["o_kpe"].T
    return (y[:SEQ].reshape(1, SEQ, D), y[SEQ:].reshape(DB, DS, D),
            o["o_kp"].T.reshape(1, 1, WIN, *heads), o["o_vp"].T.reshape(1, 1, WIN, *heads),
            window(o["o_kc"], o["o_ks"]), window(o["o_vc"], o["o_vs"]),
            o["o_sgu"].reshape(1, DB, DS, SGW),
            o["o_convp"].transpose(2, 1, 0).reshape(1, 1, 2, CT * P),
            o["o_convs"].transpose(2, 3, 1, 0).reshape(1, DB, 2, CT * P),
            ckv[:SEQ].reshape(1, 1, SEQ, KV_LORA), kpe[:SEQ].reshape(1, 1, SEQ, ROPE),
            ckv[SEQ:].reshape(1, DB, DS, KV_LORA), kpe[SEQ:].reshape(1, DB, DS, ROPE))


def kernel(**inputs):
    import concourse.bacc as bacc
    from concourse.bass_utils import run_bass_kernel_spmd

    arrays = layout({k: np.asarray(v) for k, v in inputs.items()})
    nc = bacc.Bacc("TRN2", target_bir_lowering=False, num_devices=1)
    d = {k: nc.dram_tensor(k, v.shape, mybir.dt.from_np(v.dtype), kind="ExternalInput").ap() for k, v in arrays.items()}
    for k, shape in OUTPUTS.items():
        d[k] = nc.dram_tensor(k, shape, F32, kind="ExternalOutput").ap()
    d["dist"] = nc.dram_tensor("dist", (HEADS, P, 3 * WIN), F32, kind="Internal").ap()
    decoder_step(nc, d)
    return results(run_bass_kernel_spmd(nc, [arrays], core_ids=[0]).results[0])
```
